# Optimizing a Trainium2 kernel written in Bass

```python
import math
import jax, jax.numpy as jnp
from jax import lax
import numpy as np

D_MODEL = 1024
BATCH = 1
SEQ = 256
DEPTH = 1

D_MIX = D_MODEL
ATT_WIDTH = D_MIX // 2
POOL_WIDTH = D_MIX - ATT_WIDTH
HEAD_DIM = 64
N_HEADS = ATT_WIDTH // HEAD_DIM
IDX_HEADS = 4
IDX_DIM = 64
IDX_ROPE_DIM = 32
INDEX_TOPK = 256
POOL_WINDOWS = (2, 4, 8, 16)
N_POOL_GROUPS = len(POOL_WINDOWS)
POOL_CH = POOL_WIDTH // N_POOL_GROUPS
D_FF = 2816
ROPE_THETA = 10000.0
NORM_EPS = 1e-6
Q_BLOCK = 128
IN_SPLITS = (ATT_WIDTH, ATT_WIDTH, ATT_WIDTH, IDX_HEADS * IDX_DIM, IDX_DIM, IDX_HEADS, POOL_WIDTH)
IN_COLS = sum(IN_SPLITS)


def rms_norm(x, g):
    xf = x.astype(jnp.float32)
    y = xf * lax.rsqrt(jnp.mean(xf * xf, axis=-1, keepdims=True) + NORM_EPS)
    return (y * g.astype(jnp.float32)).astype(x.dtype)

def rope(x, pos, rot_dim):
    half = rot_dim // 2
    inv = ROPE_THETA ** (-jnp.arange(half, dtype=jnp.float32) / half)
    ang = pos.astype(jnp.float32)[:, None] * inv[None, :]
    cos = jnp.cos(ang)[:, None, :]
    sin = jnp.sin(ang)[:, None, :]
    xr = x[..., :rot_dim].astype(jnp.float32)
    x1, x2 = xr[..., :half], xr[..., half:]
    rot = jnp.concatenate([x1 * cos - x2 * sin, x2 * cos + x1 * sin], axis=-1).astype(x.dtype)
    return jnp.concatenate([rot, x[..., rot_dim:]], axis=-1)

def swiglu(x, w_gate, w_up, w_down):
    return (jax.nn.silu(x @ w_gate) * (x @ w_up)) @ w_down

def dsa_attention(q, k, v, q_idx, k_idx, w_idx, top_k):
    B, S, H, Dh = q.shape
    nb = S // Q_BLOCK
    key_pos = jnp.arange(S)
    scale = Dh ** -0.5

    def to_blocks(a):
        return a.reshape((B, nb, Q_BLOCK) + a.shape[2:]).swapaxes(0, 1)

    def block(args):
        qb, qib, wb, posb = args
        rel = jax.nn.relu(jnp.einsum('bthd,bsd->bths', qib, k_idx).astype(jnp.float32))
        score = jnp.einsum('bth,bths->bts', wb.astype(jnp.float32), rel)
        causal = key_pos[None, :] <= posb[:, None]
        score = jnp.where(causal[None], score, -jnp.inf)
        _, idx = lax.top_k(score, top_k)
        valid = idx <= posb[None, :, None]
        k_sel = jax.vmap(lambda kk, ii: kk[ii])(k, idx)
        v_sel = jax.vmap(lambda vv, ii: vv[ii])(v, idx)
        logits = jnp.einsum('bthd,btkhd->bhtk', qb, k_sel).astype(jnp.float32) * scale
        logits = jnp.where(valid[:, None], logits, -jnp.inf)
        p = jax.nn.softmax(logits, axis=-1).astype(v.dtype)
        return jnp.einsum('bhtk,btkhd->bthd', p, v_sel)

    pos_blocks = jnp.arange(S).reshape(nb, Q_BLOCK)
    out = lax.map(block, (to_blocks(q), to_blocks(q_idx), to_blocks(w_idx), pos_blocks))
    return out.swapaxes(0, 1).reshape(B, S, H * Dh)

def multiscale_pool(u):
    B, S, _ = u.shape
    uf = u.astype(jnp.float32).reshape(B, S, N_POOL_GROUPS, POOL_CH)
    c = jnp.concatenate([jnp.zeros((B, 1, N_POOL_GROUPS, POOL_CH), jnp.float32),
                         jnp.cumsum(uf, axis=1)], axis=1)
    t = jnp.arange(S)
    outs = []
    for g, w in enumerate(POOL_WINDOWS):
        cg = c[:, :, g]
        c_lo = jnp.concatenate([jnp.zeros((B, w - 1, POOL_CH), jnp.float32), cg[:, :S + 1 - w]], axis=1)
        count = jnp.minimum(t + 1, w).astype(jnp.float32)[None, :, None]
        outs.append((cg[:, 1:] - c_lo) / count - uf[:, :, g])
    return jnp.stack(outs, axis=2).astype(u.dtype)

def first_inputs(seed: int = 0) -> dict:
    key = jax.random.key(seed)
    ks = jax.random.split(key, 20)
    f32 = jnp.float32

    def nrm(k, shape, fan_in):
        return jax.random.normal(k, shape, f32) * fan_in ** -0.5

    def gain(k, shape):
        return 1.0 + 0.02 * jax.random.normal(k, shape, f32)

    L = DEPTH
    return {
        "x": jax.random.normal(ks[0], (BATCH, SEQ, D_MODEL), f32),
        "ffn1_norm": gain(ks[1], (L, D_MODEL)),
        "ffn1_w_gate": nrm(ks[2], (L, D_MODEL, D_FF), D_MODEL),
        "ffn1_w_up": nrm(ks[3], (L, D_MODEL, D_FF), D_MODEL),
        "ffn1_w_down": nrm(ks[4], (L, D_FF, D_MODEL), D_FF),
        "mix_norm": gain(ks[5], (L, D_MODEL)),
        "w_in": nrm(ks[6], (L, D_MODEL, IN_COLS), D_MODEL),
        "q_norm": gain(ks[7], (L, HEAD_DIM)),
        "k_norm": gain(ks[8], (L, HEAD_DIM)),
        "pool_w": nrm(ks[9], (L, N_POOL_GROUPS, POOL_CH, POOL_CH), POOL_CH),
        "pool_scale": 0.5 + 0.05 * jax.random.normal(ks[10], (L, POOL_WIDTH), f32),
        "w_out": nrm(ks[11], (L, D_MIX, D_MODEL), D_MIX),
        "ffn2_norm": gain(ks[12], (L, D_MODEL)),
        "ffn2_w_gate": nrm(ks[13], (L, D_MODEL, D_FF), D_MODEL),
        "ffn2_w_up": nrm(ks[14], (L, D_MODEL, D_FF), D_MODEL),
        "ffn2_w_down": nrm(ks[15], (L, D_FF, D_MODEL), D_FF),
    }

def first_block(x, ffn1_norm, ffn1_w_gate, ffn1_w_up, ffn1_w_down, mix_norm, w_in,
              q_norm, k_norm, pool_w, pool_scale, w_out,
              ffn2_norm, ffn2_w_gate, ffn2_w_up, ffn2_w_down):
    B, S, _ = x.shape
    top_k = min(INDEX_TOPK, S // 4)
    pos = jnp.arange(S)
    split_points = list(np.cumsum(IN_SPLITS)[:-1])
    idx_scale = (IDX_HEADS ** -0.5) * (IDX_DIM ** -0.5)

    for l in range(DEPTH):
        x = x + 0.5 * swiglu(rms_norm(x, ffn1_norm[l]), ffn1_w_gate[l], ffn1_w_up[l], ffn1_w_down[l])

        h = rms_norm(x, mix_norm[l])
        proj = h @ w_in[l]
        q, k, v, qi, ki, wi, u = jnp.split(proj, split_points, axis=-1)
        q = rope(rms_norm(q.reshape(B, S, N_HEADS, HEAD_DIM), q_norm[l]), pos, HEAD_DIM)
        k = rope(rms_norm(k.reshape(B, S, N_HEADS, HEAD_DIM), k_norm[l]), pos, HEAD_DIM)
        v = v.reshape(B, S, N_HEADS, HEAD_DIM)
        qi = rope(qi.reshape(B, S, IDX_HEADS, IDX_DIM), pos, IDX_ROPE_DIM)
        ki = rope(ki.reshape(B, S, 1, IDX_DIM), pos, IDX_ROPE_DIM)[:, :, 0]
        wi = wi * idx_scale

        attn = dsa_attention(q, k, v, qi, ki, wi, top_k)

        pooled = jnp.einsum('bsgc,gcd->bsgd', multiscale_pool(u), pool_w[l])
        pooled = pooled.reshape(B, S, POOL_WIDTH) * pool_scale[l]

        x = x + jnp.concatenate([attn, pooled], axis=-1) @ w_out[l]

        x = x + 0.5 * swiglu(rms_norm(x, ffn2_norm[l]), ffn2_w_gate[l], ffn2_w_up[l], ffn2_w_down[l])
    return x


CHUNK = 128
A_WIDTH = D_MODEL
A_HEADS = 8
A_HEAD_DIM = A_WIDTH // A_HEADS
B_WIDTH = D_MODEL
B_GROUPS = 16
B_GROUP_DIM = B_WIDTH // B_GROUPS
CONV_WIDTH = 3
D_FF_2 = ((8 * D_MODEL // 3 + 127) // 128) * 128
N_IN = 2 * A_WIDTH + 3 * B_WIDTH + 2 * D_MODEL
EPS = 1e-6


def rmsnorm(x, g):
    x32 = x.astype(jnp.float32)
    y = x32 * lax.rsqrt(jnp.mean(x32 * x32, axis=-1, keepdims=True) + EPS)
    return y.astype(x.dtype) * g

def swiglu_2(h, w_in, w_out):
    gate, up = jnp.split(h @ w_in, 2, axis=-1)
    return (jax.nn.silu(gate) * up) @ w_out

def spatial_gating(u, v, norm_g, w_s, b_s):
    bsz, s, _ = v.shape
    v = rmsnorm(v, norm_g)
    v = v.reshape(bsz, s // CHUNK, CHUNK, A_HEADS, A_HEAD_DIM)
    v = jnp.einsum('hqp,bcphd->bcqhd', w_s, v) + b_s.T[None, None, :, :, None]
    return u * v.reshape(bsz, s, A_WIDTH)

def short_conv(t, w):
    s = t.shape[1]
    pad = CONV_WIDTH // 2
    tp = jnp.pad(t, ((0, 0), (pad, CONV_WIDTH - 1 - pad), (0, 0)))
    out = w[0] * tp[:, 0:s]
    for k in range(1, CONV_WIDTH):
        out = out + w[k] * tp[:, k:k + s]
    return out

def hybrid_mixer(h, w_in, sgu_norm, sgu_w, sgu_b, conv_w, w_proj_a, w_proj_b, w_out):
    z = h @ w_in
    za, zb, zg = jnp.split(z, [2 * A_WIDTH, 2 * A_WIDTH + 3 * B_WIDTH], axis=-1)
    u, v = jnp.split(jax.nn.gelu(za), 2, axis=-1)
    y_a = spatial_gating(u, v, sgu_norm, sgu_w, sgu_b) @ w_proj_a
    gate_b, gate_c, xb = jnp.split(zb, 3, axis=-1)
    y_b = (gate_b * short_conv(gate_c * xb, conv_w)) @ w_proj_b
    g_a, g_b = jnp.split(zg, 2, axis=-1)
    merged = jax.nn.sigmoid(g_a) * y_a + jax.nn.sigmoid(g_b) * y_b
    return merged @ w_out

def second_inputs(seed: int = 0) -> dict:
    key = jax.random.key(seed)
    ks = jax.random.split(key, 20)
    f32 = jnp.float32

    def nrm(k, shape, scale):
        return jax.random.normal(k, shape, f32) * scale

    def gain(k, shape):
        return 1.0 + 0.05 * jax.random.normal(k, shape, f32)

    return {
        "x": nrm(ks[0], (BATCH, SEQ, D_MODEL), 1.0),
        "ffn1_norm": gain(ks[1], (DEPTH, D_MODEL)),
        "ffn1_w_in": nrm(ks[2], (DEPTH, D_MODEL, 2 * D_FF_2), D_MODEL ** -0.5),
        "ffn1_w_out": nrm(ks[3], (DEPTH, D_FF_2, D_MODEL), D_FF_2 ** -0.5),
        "mix_norm": gain(ks[4], (DEPTH, D_MODEL)),
        "w_in": nrm(ks[5], (DEPTH, D_MODEL, N_IN), D_MODEL ** -0.5),
        "sgu_norm": gain(ks[6], (DEPTH, A_WIDTH)),
        "sgu_w": nrm(ks[7], (DEPTH, A_HEADS, CHUNK, CHUNK), CHUNK ** -0.5),
        "sgu_b": gain(ks[8], (DEPTH, A_HEADS, CHUNK)),
        "conv_w": nrm(ks[9], (DEPTH, CONV_WIDTH, B_WIDTH), CONV_WIDTH ** -0.5),
        "w_proj_a": nrm(ks[10], (DEPTH, A_WIDTH, D_MODEL), A_WIDTH ** -0.5),
        "w_proj_b": nrm(ks[11], (DEPTH, B_WIDTH, D_MODEL), B_WIDTH ** -0.5),
        "w_out": nrm(ks[12], (DEPTH, D_MODEL, D_MODEL), D_MODEL ** -0.5),
        "ffn2_norm": gain(ks[13], (DEPTH, D_MODEL)),
        "ffn2_w_in": nrm(ks[14], (DEPTH, D_MODEL, 2 * D_FF_2), D_MODEL ** -0.5),
        "ffn2_w_out": nrm(ks[15], (DEPTH, D_FF_2, D_MODEL), D_FF_2 ** -0.5),
        "final_norm": gain(ks[16], (D_MODEL,)),
    }

def second_block(x, ffn1_norm, ffn1_w_in, ffn1_w_out, mix_norm, w_in, sgu_norm, sgu_w,
              sgu_b, conv_w, w_proj_a, w_proj_b, w_out, ffn2_norm, ffn2_w_in,
              ffn2_w_out, final_norm):
    for l in range(DEPTH):
        x = x + 0.5 * swiglu_2(rmsnorm(x, ffn1_norm[l]), ffn1_w_in[l], ffn1_w_out[l])
        x = x + hybrid_mixer(rmsnorm(x, mix_norm[l]), w_in[l], sgu_norm[l], sgu_w[l],
                             sgu_b[l], conv_w[l], w_proj_a[l], w_proj_b[l], w_out[l])
        x = x + 0.5 * swiglu_2(rmsnorm(x, ffn2_norm[l]), ffn2_w_in[l], ffn2_w_out[l])
    return rmsnorm(x, final_norm)


def setup_inputs(seed=0):
    out = dict(first_inputs(seed))
    for name, value in second_inputs(seed + 1).items():
        if name != "x":
            out[name + "_2"] = value
    return out


def reference(
    x, ffn1_norm, ffn1_w_gate, ffn1_w_up, ffn1_w_down, mix_norm, w_in, q_norm, k_norm, pool_w,
    pool_scale, w_out, ffn2_norm, ffn2_w_gate, ffn2_w_up, ffn2_w_down, ffn1_norm_2, ffn1_w_in_2,
    ffn1_w_out_2, mix_norm_2, w_in_2, sgu_norm_2, sgu_w_2, sgu_b_2, conv_w_2, w_proj_a_2,
    w_proj_b_2, w_out_2, ffn2_norm_2, ffn2_w_in_2, ffn2_w_out_2, final_norm_2,
):
    x = first_block(
        x, ffn1_norm, ffn1_w_gate, ffn1_w_up, ffn1_w_down, mix_norm, w_in, q_norm, k_norm,
        pool_w, pool_scale, w_out, ffn2_norm, ffn2_w_gate, ffn2_w_up, ffn2_w_down,
    )
    return second_block(
        x, ffn1_norm_2, ffn1_w_in_2, ffn1_w_out_2, mix_norm_2, w_in_2, sgu_norm_2, sgu_w_2,
        sgu_b_2, conv_w_2, w_proj_a_2, w_proj_b_2, w_out_2, ffn2_norm_2, ffn2_w_in_2,
        ffn2_w_out_2, final_norm_2,
    )


_drawn_inputs = setup_inputs


def setup_inputs(seed=0):
    import zlib

    import numpy as np

    out = dict(_drawn_inputs(seed))
    spreads = {}
    factors = {'ffn1_norm': 2.995,
     'q_norm': 8.0,
     'k_norm': 8.0,
     'ffn2_norm': 6.077,
     'sgu_norm_2': 36.528,
     'sgu_b_2': 33.128,
     'ffn2_norm_2': 29.32,
     'pool_scale': 3.932,
     'ffn1_norm_2': 8.0,
     'mix_norm_2': 4.77}
    for name, (base, spread) in spreads.items():
        noise = np.random.default_rng([zlib.crc32(name.encode()), seed]).standard_normal(out[name].shape)
        drawn = base * np.exp(spread * noise) if base else spread * noise
        out[name] = __import__('jax').numpy.asarray(drawn.astype(out[name].dtype))
    for name, factor in factors.items():
        out[name] = (out[name] * factor).astype(out[name].dtype)
    return out
```

```python
from contextlib import ExitStack

import numpy as np

import concourse.bass as bass
from concourse import mybir

F32 = mybir.dt.float32
F32R = mybir.dt.float32r
BF16 = mybir.dt.bfloat16
ALU = mybir.AluOpType
ACT = mybir.ActivationFunctionType
AX = mybir.AxisListType

P = 128
D = 1024
S = 256
KC = D // P
TT = S // P
FF = 2816
FC = FF // P
HEADS, HD = 8, 64
ATT = HEADS * HD
PAIRS = ATT // P
IH, ID, IROT = 4, 64, 32
TOPK = 64
POOLS = (2, 4, 8, 16)
THETA = 10000.0
EPS = 1e-6
SGU_HEADS = 8
CONV = 3

BW = 1024
RING = 4
IDX_W = IH * ID + ID + IH
IDX_K = BW // IDX_W
IDX_B = -(-KC // IDX_K)
TOK_K = BW // 512
TOK_B = KC // TOK_K

FFN_B = 3 * FC
MIX1_B = 4 * TOK_B + IDX_B + KC
CONV_B, GATE_B = 3 * KC, 4 * KC
MIX2_B = 2 * TOK_B + CONV_B + KC + GATE_B + KC
START = np.cumsum([0, FFN_B, MIX1_B, FFN_B, FFN_B, MIX2_B, FFN_B]).tolist()
BLOCKS = START[-1]

COLS = {"ffn1": 0, "mix": 8, "ffn2": 16, "ffn1_2": 24, "mix_2": 32, "ffn2_2": 40, "final": 48, "sgu": 56,
        "conv": 64, "pool": 88}
NCOLS = 92
PHASE_GAIN = ["ffn1", "mix", "ffn2", "ffn1_2", "mix_2", "ffn2_2", "final"]
C_COS, C_SIN, C_ICOS, C_ISIN, C_ID, C_ONE, C_BAND = 0, 128, 256, 288, 320, 448, 576
NCONST = 576 + 2 * 4 * 256

UNSEL, NEG, MASKED = -3.0e38, -2.0e38, -1.0e30


def build(nc, stream, x_in, cols_in, rows_in, const_in, sgu_w_in, pool_w_in, out):
    ctx = ExitStack()
    with ctx:
        def sb(name, shape, dt=F32):
            return ctx.enter_context(nc.sbuf_tensor(name, shape, dt))

        def sem(name):
            return ctx.enter_context(nc.semaphore(name))

        w_raw = sb("w_raw", [P, RING, BW])
        w_hi = sb("w_hi", [P, RING, BW], F32R)
        w_lo = sb("w_lo", [P, RING, BW], F32R)
        x = sb("x", [P, KC, S])
        x_hi = sb("x_hi", [P, KC, S], F32R)
        x_lo = sb("x_lo", [P, KC, S], F32R)
        x_sq = sb("x_sq", [P, KC, S])
        ms = sb("ms", [P, S])
        root = sb("root", [P, S])
        newton = sb("newton", [P, S])
        rstd = sb("rstd", [P, S])
        rstd_sq = sb("rstd_sq", [P, S])
        r_col = sb("r_col", [P, TT])
        r_col16 = sb("r_col16", [P, TT])
        cols = sb("cols", [P, NCOLS])
        rows = sb("rows", [P, 2 * HD + SGU_HEADS * P])
        const = sb("const", [P, NCONST])
        sgu_w = sb("sgu_w", [P, SGU_HEADS, P])
        pool_w = sb("pool_w", [P, 4, P])
        zeros = sb("zeros", [P, 512], BF16)
        tmp = sb("tmp", [P, 4, S])
        gate_s, up_s, silu, hid = (tmp[:, n, :] for n in range(4))
        hid_hi = sb("hid_hi", [P, 2, S], F32R)
        hid_lo = sb("hid_lo", [P, 2, S], F32R)
        mix_hi = sb("mix_hi", [P, KC, S], F32R)
        mix_lo = sb("mix_lo", [P, KC, S], F32R)
        q_tok = sb("q_tok", [P, 2 * TT, ATT])
        qk_a = sb("qk_a", [P, 2 * TT, ATT])
        qk_b = x_sq[:].rearrange("p (a b) s -> p a (b s)", b=2)
        v_tok = sb("v_tok", [P, TT, D])
        u_tok = v_tok[:, :, ATT:2 * ATT]
        qk_ss = sb("qk_ss", [P, 2 * TT * HEADS])
        qk_ms = sb("qk_ms", [P, 2 * TT * HEADS])
        qk_root = sb("qk_root", [P, 2 * TT * HEADS])
        qk_nt = sb("qk_nt", [P, 2 * TT * HEADS])
        qk_r = sb("qk_r", [P, 2 * TT * HEADS])
        rope_c = sb("rope_c", [P, 2, TT, HD])
        rope_s = sb("rope_s", [P, 2, TT, HD])
        idx_tok = sb("idx_tok", [P, TT, (IH + 2) * ID])
        idx_w = sb("idx_w", [P, TT, IH])
        idx_t = tmp[:].rearrange("p a s -> p (a s)")[:, 0:4 * TT * (IH + 2) * IROT // 2].rearrange(
            "p (a t h d) -> p a t h d", a=4, t=TT, h=IH + 2)
        qiT = sb("qiT", [P, 2, S])
        kiT = sb("kiT", [P, S])
        rel = x_sq[:].rearrange("p (t h) s -> p t h s", t=TT)
        score = sb("score", [P, TT, S])
        work = sb("work", [P, TT, S])
        top8 = sb("top8", [P, TT, 8])
        bias = sb("bias", [P, TT, S])
        qT = q_tok[:, 0:2, :].rearrange("p a (b s) -> p (a b) s", b=2)
        kT = q_tok[:, 2:4, :].rearrange("p a (b s) -> p (a b) s", b=2)
        logit = qk_a[:, 0:2, :].rearrange("p a (t s) -> p a t s", t=TT)
        prob = qk_a[:, 2:4, :].rearrange("p a (t s) -> p a t s", t=TT)
        top1 = sb("top1", [P, HEADS, TT])
        neg1 = sb("neg1", [P, HEADS, TT])
        psums = sb("psums", [P, HEADS, TT])
        rsum = sb("rsum", [P, HEADS, TT])
        probT = sb("probT", [P, 2, 3 * P])
        pool_in = tmp
        v_ss = sb("v_ss", [P, 5, TT])
        gc_s, gb_s, conv_a, conv_y = (tmp[:, n, :] for n in range(4))
        conv_in = sb("conv_in", [P, S + 2])
        yb_hi = sb("yb_hi", [P, KC, S], F32R)
        yb_lo = sb("yb_lo", [P, KC, S], F32R)
        ya_hi = sb("ya_hi", [P, KC, S], F32R)
        ya_lo = sb("ya_lo", [P, KC, S], F32R)
        sg = x_sq
        u_s = qk_a[:, 0:2, :].rearrange("p a (b s) -> p (a b) s", b=2)
        gates, sig, branch = (q_tok[:, n, :] for n in range(3))
        ya = q_tok[:, 3, :].rearrange("p (a s) -> p a s", a=2)
        merged = tmp[:, 0, :]

        bank = [ctx.enter_context(nc.psum_tensor(f"bank{i}", [P, 512], F32)) for i in range(8)]

        ident = const[:, C_ID:C_ID + P]
        ones = const[:, C_ONE:C_ONE + P]

        def acc(m):
            return bank[m // 2][:, (m % 2) * S:(m % 2 + 1) * S]

        arrived = [sem(f"arrived{i}") for i in range(RING)]
        w_hi_done = sem("w_hi_done")
        w_split = sem("w_split")
        w_used = sem("w_used")
        x_loaded = sem("x_loaded")
        cols_loaded = sem("cols_loaded")
        const_loaded = sem("const_loaded")
        rows_loaded = sem("rows_loaded")
        sgu_loaded = sem("sgu_loaded")
        pool_loaded = sem("pool_loaded")
        zeros_set = sem("zeros_set")
        tables_made = sem("tables_made")
        acc_done = sem("acc_done")
        x_new = sem("x_new")
        x_hi_done = sem("x_hi_done")
        x_split = sem("x_split")
        x_sq_done = sem("x_sq_done")
        sumsq_done = sem("sumsq_done")
        ms_done = sem("ms_done")
        root_done = sem("root_done")
        rstd_done = sem("rstd_done")
        rT_done = sem("rT_done")
        r_col_done = sem("r_col_done")
        gate_scaled = sem("gate_scaled")
        up_scaled = sem("up_scaled")
        silu_done = sem("silu_done")
        hid_done = sem("hid_done")
        hid_hi_done = sem("hid_hi_done")
        hid_split = sem("hid_split")
        q_copied = sem("q_copied")
        qk_sq = sem("qk_sq")
        qk_ms_done = sem("qk_ms_done")
        qk_root_done = sem("qk_root_done")
        qk_normed = sem("qk_normed")
        qk_cos = sem("qk_cos")
        pool_chain = sem("pool_chain")
        qk_roped = sem("qk_roped")
        idx_copied = sem("idx_copied")
        idx_roped = sem("idx_roped")
        idx_T = sem("idx_T")
        idx_T_copied = sem("idx_T_copied")
        v_copied = sem("v_copied")
        u_copied = sem("u_copied")
        idx_dots = sem("idx_dots")
        rel_done = sem("rel_done")
        score_done = sem("score_done")
        score_masked = sem("score_masked")
        sel_done = sem("sel_done")
        bias_done = sem("bias_done")
        pool_mean = sem("pool_mean")
        pool_mean_copied = sem("pool_mean_copied")
        pool_out = sem("pool_out")
        mix_hi_done = sem("mix_hi_done")
        mix_split = sem("mix_split")
        qk_T = sem("qk_T")
        qk_T_copied = sem("qk_T_copied")
        logits_done = sem("logits_done")
        logits_read = sem("logits_read")
        neg_done = sem("neg_done")
        exp_done = sem("exp_done")
        prob_done = sem("prob_done")
        probT_done = sem("probT_done")
        probT_copied = sem("probT_copied")
        pv_done = sem("pv_done")
        v_gelu = sem("v_gelu")
        v_sq = sem("v_sq")
        v_ms_done = sem("v_ms_done")
        v_root_done = sem("v_root_done")
        v_normed = sem("v_normed")
        spatial_done = sem("spatial_done")
        sg_done = sem("sg_done")
        conv_read = sem("conv_read")
        gc_scaled = sem("gc_scaled")
        conv_filled = sem("conv_filled")
        conv_mid = sem("conv_mid")
        conv_done = sem("conv_done")
        yb_hi_done = sem("yb_hi_done")
        yb_split = sem("yb_split")
        u_scaled = sem("u_scaled")
        u_gelu = sem("u_gelu")
        ya_done = sem("ya_done")
        ya_hi_done = sem("ya_hi_done")
        ya_split = sem("ya_split")
        gates_scaled = sem("gates_scaled")
        sig_done = sem("sig_done")
        branch_done = sem("branch_done")
        merged_done = sem("merged_done")
        dve_step = sem("dve_step")
        out_ready = sem("out_ready")
        stored = sem("stored")

        block = ctx.enter_context(nc.Block())

        @block.sync
        def _(sp):
            for n in range(RING):
                sp.dma_start(w_raw[:, n, :], stream[n]).then_inc(arrived[n], 16)
            with sp.Fori(1, BLOCKS // RING) as i:
                for j in range(RING):
                    sp.wait_ge(w_split, RING * i + (j - RING + 1))
                    sp.dma_start(w_raw[:, j, :],
                                 stream[bass.ds(RING * i + j, 1), :, :].rearrange("a p c -> p (a c)")
                                 ).then_inc(arrived[j], 16)
            for n in range(BLOCKS // RING * RING, BLOCKS):
                sp.wait_ge(w_split, n - RING + 1)
                sp.dma_start(w_raw[:, n % RING, :], stream[n]).then_inc(arrived[n % RING], 16)
            for c in range(4):
                sp.wait_ge(out_ready, 2 * c + 2)
                sp.dma_start(out[:, 2 * c:2 * c + 2, :], x_sq[:, 2 * c:2 * c + 2, :]).then_inc(stored, 16)
            sp.wait_ge(stored, 64)

        @block.gpsimd
        def _(pool):
            nc.gpsimd.memset(zeros[:], 0.0).then_inc(zeros_set, 1)
            nc.gpsimd.memset(conv_in[:], 0.0).then_inc(zeros_set, 1)
            pool.wait_ge(const_loaded, 16)
            pool.wait_ge(rows_loaded, 16)
            cos = const[:, C_COS:C_COS + P].rearrange("p (t d) -> p t d", t=TT)
            sin = const[:, C_SIN:C_SIN + P].rearrange("p (t d) -> p t d", t=TT)
            h = HD // 2
            for a in range(2):
                for t in range(TT):
                    gain = rows[:, a * HD:(a + 1) * HD]
                    nc.gpsimd.tensor_tensor(rope_c[:, a, t, :], gain, cos[:, t, :], ALU.mult)
                    nc.gpsimd.tensor_tensor(rope_s[:, a, t, 0:h], gain[:, h:HD], sin[:, t, 0:h], ALU.mult)
                    last = nc.gpsimd.tensor_tensor(rope_s[:, a, t, h:HD], gain[:, 0:h], sin[:, t, h:HD], ALU.mult)
                    last.then_inc(tables_made, 1)
            for t in range(TT):
                n = (t + 1) * P
                pool.wait_ge(score_done, t + 1)
                nc.gpsimd.affine_select(out=work[:, t, 0:n], in_=score[:, t, 0:n], compare_op=ALU.is_ge, fill=NEG,
                                        base=t * P, pattern=[[-1, n]], channel_multiplier=1).then_inc(score_masked, 1)
            pool.wait_ge(tables_made, 4)
            for a in range(2):
                pool.wait_ge(qk_normed, a + 1)
                for t in range(TT):
                    src = q_tok[:, 2 * a + t, :].rearrange("p (h d) -> p h d", d=HD)
                    dst = qk_b[:, 2 * a + t, :].rearrange("p (h d) -> p h d", d=HD)
                    for lo, hi in ((0, h), (h, 0)):
                        nc.gpsimd.tensor_tensor(dst[:, :, lo:lo + h], src[:, :, hi:hi + h],
                                                rope_s[:, a, t, lo:lo + h].unsqueeze(1).to_broadcast([P, HEADS, h]),
                                                ALU.mult).then_inc(pool_chain, 1)
                pool.wait_ge(pool_chain, 4 * (a + 1))
                pool.wait_ge(qk_cos, a + 1)
                nc.gpsimd.tensor_tensor(qk_b[:, 2 * a:2 * a + 2, :], qk_b[:, 2 * a:2 * a + 2, :],
                                        qk_a[:, 2 * a:2 * a + 2, :], ALU.add).then_inc(qk_roped, 1)
            for t in range(TT):
                n = (t + 1) * P
                pool.wait_ge(sel_done, t + 1)
                nc.gpsimd.affine_select(out=bias[:, t, 0:n], in_=score[:, t, 0:n], compare_op=ALU.is_ge, fill=MASKED,
                                        base=t * P, pattern=[[-1, n]], channel_multiplier=1).then_inc(bias_done, 1)

        @block.scalar
        def _(act):
            def split(n, i=0, per=0):
                if n >= BLOCKS:
                    return
                slot = n % RING
                act.wait_ge(arrived[slot], 16 * (n // RING + 1) + 16 * (per // RING) * i)
                if n >= RING:
                    act.wait_ge(w_used, n - RING + 1 + per * i)
                nc.scalar.activation(w_hi[:, slot, :], w_raw[:, slot, :], ACT.Copy).then_inc(w_hi_done, 1)

            def phase_input(p):
                g = COLS[PHASE_GAIN[p]]
                for k in range(KC):
                    if p:
                        act.wait_ge(x_new, 4 * (p - 1) + k // 2 + 1)
                    if p < 6:
                        nc.scalar.activation(x_hi[:, k, :], x[:, k, :], ACT.Identity,
                                             scale=cols[:, g + k:g + k + 1]).then_inc(x_hi_done, 1)
                    nc.scalar.activation(x_sq[:, k, :], x[:, k, :], ACT.Square).then_inc(x_sq_done, 1)

            def rms_root(p):
                act.wait_ge(ms_done, p + 1)
                nc.scalar.activation(root[:], ms[:], ACT.Sqrt).then_inc(root_done, 1)

            def ffn(e, n0, p):
                split(n0 + 2)
                split(n0 + 3)
                rms_root(p)
                split(n0 + 4)

                def gate(f):
                    act.wait_ge(gate_scaled, FC * e + 1 + f)
                    nc.scalar.activation(silu, gate_s, ACT.Silu).then_inc(silu_done, 1)

                def hidden(f, slot):
                    act.wait_ge(hid_done, FC * e + 1 + f)
                    nc.scalar.activation(hid_hi[:, slot, :], hid, ACT.Copy).then_inc(hid_hi_done, 1)

                gate(0)
                hidden(0, 0)
                with act.Fori(0, (FC - 2) // 4) as i:
                    for j in range(4):
                        b = n0 + 2 + 3 * j
                        split(b + 3, i, 12)
                        split(b + 4, i, 12)
                        gate(4 * i + (1 + j))
                        split(b + 5, i, 12)
                        hidden(4 * i + (1 + j), (1 + j) % 2)
                split(n0 + 65)
                gate(FC - 1)
                hidden(FC - 1, (FC - 1) % 2)
                split(n0 + 66)
                split(n0 + 67)

            def attention_mixer(n0, p):
                for b in range(2, 6):
                    split(n0 + b)
                rms_root(p)
                for b in range(6, 10):
                    split(n0 + b)
                act.wait_ge(r_col_done, 1)

                def tokens_out(dst, src, used, done):
                    act.wait_ge(w_used, n0 + used)
                    for t in range(TT):
                        nc.scalar.activation(dst[t], src[t], ACT.Identity, scale=r_col[:, t:t + 1]).then_inc(done, 1)

                tokens_out([q_tok[:, 0, :], q_tok[:, 1, :]], [bank[4][:], bank[5][:]], 4, q_copied)
                split(n0 + 10)
                split(n0 + 11)
                tokens_out([q_tok[:, 2, :], q_tok[:, 3, :]], [bank[6][:], bank[7][:]], 8, q_copied)
                split(n0 + 12)
                split(n0 + 13)
                split(n0 + 14)
                act.wait_ge(w_used, n0 + 11)
                q_w = IH * ID
                for t in range(TT):
                    src, r = bank[t], r_col[:, t:t + 1]
                    nc.scalar.activation(idx_tok[:, t, 0:q_w + ID], src[:, 0:q_w + ID], ACT.Identity, scale=r)
                    nc.scalar.activation(idx_tok[:, t, q_w + ID:q_w + 2 * ID], src[:, q_w:q_w + ID], ACT.Identity, scale=r)
                    nc.scalar.activation(idx_w[:, t, :], src[:, q_w + ID:IDX_W], ACT.Identity,
                                         scale=r_col16[:, t:t + 1]).then_inc(idx_copied, 1)
                for a in range(2):
                    act.wait_ge(q_copied, 2 * a + 2)
                    nc.scalar.activation(qk_a[:, 2 * a:2 * a + 2, :], q_tok[:, 2 * a:2 * a + 2, :],
                                         ACT.Square).then_inc(qk_sq, 1)
                split(n0 + 15)
                split(n0 + 16)
                act.wait_ge(idx_T, 1)
                nc.scalar.activation(qiT[:].rearrange("p c s -> p (c s)"), bank[6][:], ACT.Copy).then_inc(idx_T_copied, 1)
                nc.scalar.activation(kiT[:], bank[7][:, 0:S], ACT.Copy).then_inc(idx_T_copied, 1)
                split(n0 + 17)
                split(n0 + 18)
                tokens_out([v_tok[:, 0, 0:ATT], v_tok[:, 1, 0:ATT]], [bank[2][:], bank[3][:]], 15, v_copied)
                act.wait_ge(idx_dots, 1)
                for t in range(TT):
                    n = (t + 1) * P
                    for odd in range(2):
                        nc.scalar.activation(rel[:, t, odd::2, 0:n],
                                             bank[6 * t + odd][:, 0:2 * n].rearrange("p (h s) -> p h s", h=2),
                                             ACT.Relu).then_inc(rel_done, 1)
                act.wait_ge(qk_ms_done, 1)
                nc.scalar.activation(qk_root[:], qk_ms[:], ACT.Sqrt).then_inc(qk_root_done, 1)
                for b in range(19, 23):
                    split(n0 + b)
                tokens_out([u_tok[:, 0, :], u_tok[:, 1, :]], [bank[4][:], bank[5][:]], 19, u_copied)
                for g in range(4):
                    act.wait_ge(pool_mean, g // 2 + 1)
                    nc.scalar.activation(pool_in[:, g, :], bank[2 + g // 2][:, (g % 2) * S:(g % 2 + 1) * S],
                                         ACT.Copy).then_inc(pool_mean_copied, 1)
                for g in range(4):
                    act.wait_ge(pool_out, g // 2 + 1)
                    nc.scalar.activation(mix_hi[:, PAIRS + g, :], bank[2 + g // 2][:, (g % 2) * S:(g % 2 + 1) * S],
                                         ACT.Identity, scale=cols[:, COLS["pool"] + g:COLS["pool"] + g + 1]
                                         ).then_inc(mix_hi_done, 1)
                for b in range(4):
                    act.wait_ge(qk_T, b + 1)
                    nc.scalar.activation((qT, kT)[b // 2][:, 2 * (b % 2):2 * (b % 2) + 2, :],
                                         bank[(6, 7, 4, 5)[b]][:].rearrange("p (c s) -> p c s", c=2),
                                         ACT.Copy).then_inc(qk_T_copied, 1)
                for b in range(23, 27):
                    split(n0 + b)
                for s in range(HEADS + 2):
                    if s < HEADS:
                        act.wait_ge(neg_done, s + 1)
                        if s >= 2:
                            act.wait_ge(probT_done, s - 1)
                        for t in range(TT):
                            n = (t + 1) * P
                            nc.scalar.activation(prob[:, s % 2, t, 0:n], logit[:, s % 2, t, 0:n], ACT.Exp,
                                                 bias=neg1[:, s, t:t + 1],
                                                 accum_out=psums[:, s, t:t + 1]).then_inc(exp_done, 1)
                    if 1 <= s <= HEADS:
                        act.wait_ge(probT_done, s)
                        if s >= 3:
                            act.wait_ge(pv_done, s - 2)
                        nc.scalar.activation(probT[:, (s - 1) % 2, :], bank[6][:, 0:3 * P],
                                             ACT.Copy).then_inc(probT_copied, 1)
                    if s >= 2:
                        hd = s - 2
                        lo = hd % 2 * HD
                        act.wait_ge(pv_done, hd + 1)
                        nc.scalar.activation(mix_hi[lo:lo + HD, hd // 2, :], bank[7][lo:lo + HD, 0:S],
                                             ACT.Copy).then_inc(mix_hi_done, 1)
                split(n0 + 27)
                split(n0 + 28)

            def gated_mixer(n0, p):
                for b in range(2, 6):
                    split(n0 + b)
                rms_root(p)
                for b in range(6, 11):
                    split(n0 + b)
                act.wait_ge(r_col_done, 2)
                for g in range(2):
                    act.wait_ge(w_used, n0 + 4 * g + 4)
                    for t in range(TT):
                        nc.scalar.activation(v_tok[:, t, g * 512:(g + 1) * 512], bank[4 + 2 * g + t][:],
                                             ACT.Gelu_apprx_tanh, scale=r_col[:, t:t + 1]).then_inc(v_gelu, 1)
                act.wait_ge(v_gelu, 4)
                for t in range(TT):
                    nc.scalar.activation(qk_a[:, 2 * t:2 * t + 2, :].rearrange("p a c -> p (a c)"), v_tok[:, t, :],
                                         ACT.Square, accum_out=v_ss[:, 0, t:t + 1]).then_inc(v_sq, 1)
                with act.Fori(0, 2) as i:
                    for j in range(4):
                        b = n0 + 8 + 3 * j
                        split(b + 3, i, 12)
                        split(b + 4, i, 12)
                        split(b + 5, i, 12)
                        act.wait_ge(conv_done, 4 * i + (j + 1))
                        nc.scalar.activation(yb_hi[:, bass.ds(4 * i + j, 1), :], conv_y.unsqueeze(1),
                                             ACT.Copy).then_inc(yb_hi_done, 1)
                split(n0 + 35)
                act.wait_ge(v_ms_done, 1)
                nc.scalar.activation(v_ss[:, 2, :], v_ss[:, 1, :], ACT.Sqrt).then_inc(v_root_done, 1)
                for b in range(36, 40):
                    split(n0 + b)

                def u_gelus(m0):
                    for m in range(m0, m0 + 4):
                        act.wait_ge(u_scaled, m + 1)
                        nc.scalar.activation(u_s[:, m % 4, :], u_s[:, m % 4, :],
                                             ACT.Gelu_apprx_tanh).then_inc(u_gelu, 1)

                def ya_his(m0):
                    for m in range(m0, m0 + 4):
                        act.wait_ge(ya_done, m + 1)
                        nc.scalar.activation(ya_hi[:, m, :], ya[:, m % 2, :], ACT.Copy).then_inc(ya_hi_done, 1)

                u_gelus(0)
                for b in range(40, 43):
                    split(n0 + b)
                ya_his(0)
                u_gelus(4)
                ya_his(4)
                with act.Fori(0, 4) as i:
                    for j in range(2):
                        b = n0 + 40 + 4 * j
                        for c in range(3, 6):
                            split(b + c, i, 8)
                        act.wait_ge(gates_scaled, 2 * i + (j + 1))
                        nc.scalar.activation(sig, gates, ACT.Sigmoid).then_inc(sig_done, 1)
                        split(b + 6, i, 8)
                        act.wait_ge(merged_done, 2 * i + (j + 1))
                        nc.scalar.activation(mix_hi[:, bass.ds(2 * i + j, 1), :], merged.unsqueeze(1),
                                             ACT.Copy).then_inc(mix_hi_done, 1)
                for b in range(75, 82):
                    split(n0 + b)

            act.dma_start(x[:], x_in).then_inc(x_loaded, 16)
            act.dma_start(cols[:], cols_in).then_inc(cols_loaded, 16)
            act.dma_start(const[:], const_in).then_inc(const_loaded, 16)
            act.dma_start(rows[:], rows_in).then_inc(rows_loaded, 16)
            act.dma_start(sgu_w[:], sgu_w_in).then_inc(sgu_loaded, 16)
            act.dma_start(pool_w[:], pool_w_in).then_inc(pool_loaded, 16)
            split(0)
            split(1)
            act.wait_ge(x_loaded, 16)
            act.wait_ge(cols_loaded, 16)
            phase_input(0)
            ffn(0, START[0], 0)
            phase_input(1)
            attention_mixer(START[1], 1)
            phase_input(2)
            ffn(1, START[2], 2)
            phase_input(3)
            ffn(2, START[3], 3)
            phase_input(4)
            gated_mixer(START[4], 4)
            phase_input(5)
            ffn(3, START[5], 5)
            phase_input(6)
            rms_root(6)

        @block.vector
        def _(dve):
            steps = [0]

            def step(ins):
                steps[0] += 1
                ins.then_inc(dve_step, 1)
                dve.wait_ge(dve_step, steps[0])

            def split(n, i=0, per=0):
                if n >= BLOCKS:
                    return
                slot = n % RING
                dve.wait_ge(w_hi_done, n + 1 + per * i)
                nc.vector.tensor_tensor(w_lo[:, slot, :], w_raw[:, slot, :], w_hi[:, slot, :].bitcast(F32),
                                        ALU.subtract).then_inc(w_split, 1)

            def input_lo(p, k):
                g = COLS[PHASE_GAIN[p]]
                dve.wait_ge(x_hi_done, 8 * p + k + 1)
                nc.vector.scalar_tensor_tensor(x_lo[:, k, :], x[:, k, :], cols[:, g + k:g + k + 1],
                                               x_hi[:, k, :].bitcast(F32), ALU.mult, ALU.subtract).then_inc(x_split, 1)

            def residual(p, factor):
                for c in range(4):
                    dve.wait_ge(acc_done, 4 * p + c + 1)
                    two = x[:, 2 * c:2 * c + 2, :].rearrange("p a s -> p (a s)")
                    nc.vector.scalar_tensor_tensor(two, bank[c][:], factor, two, ALU.mult, ALU.add).then_inc(x_new, 1)
                    if c and p < 5:
                        input_lo(p + 1, 2 * c - 2)
                        input_lo(p + 1, 2 * c - 1)
                if p < 5:
                    input_lo(p + 1, KC - 2)
                    input_lo(p + 1, KC - 1)

            def inv_root(ms_ap, root_ap, tmp, r):
                step(nc.vector.reciprocal(r, root_ap))
                step(nc.vector.tensor_tensor(tmp, r, r, ALU.mult))
                step(nc.vector.tensor_tensor(tmp, tmp, ms_ap, ALU.mult))
                step(nc.vector.tensor_scalar(tmp, tmp, -0.5, 1.5, ALU.mult, ALU.add))
                return nc.vector.tensor_tensor(r, r, tmp, ALU.mult)

            def rms(p):
                dve.wait_ge(sumsq_done, p + 1)
                nc.vector.tensor_scalar(ms[:], bank[STAT[p]][:, 0:S], 1.0 / D, EPS, ALU.mult, ALU.add).then_inc(ms_done, 1)
                dve.wait_ge(root_done, p + 1)
                inv_root(ms[:], root[:], newton[:], rstd[:]).then_inc(rstd_done, 1)
                dve.wait_ge(rstd_done, p + 1)

            def token_scales(n):
                dve.wait_ge(rT_done, n)
                for t in range(TT):
                    last = nc.vector.tensor_copy(r_col[:, t:t + 1], bank[2][:, t * P:t * P + 1])
                    step(last)
                nc.vector.tensor_scalar(r_col16[:], r_col[:], IH ** -0.5 * ID ** -0.5, None,
                                        ALU.mult).then_inc(r_col_done, 1)

            def ffn(e, n0, p):
                split(n0 + 2)
                split(n0 + 3)
                rms(p)
                split(n0 + 4)

                def scale(f, slot, used):
                    dve.wait_ge(w_used, used)
                    nc.vector.tensor_tensor(gate_s, bank[4 + slot][:, 0:S], rstd[:], ALU.mult).then_inc(gate_scaled, 1)
                    nc.vector.tensor_tensor(up_s, bank[4 + slot][:, S:2 * S], rstd[:], ALU.mult).then_inc(up_scaled, 1)

                def hidden(f, slot):
                    dve.wait_ge(up_scaled, FC * e + 1 + f)
                    dve.wait_ge(silu_done, FC * e + 1 + f)
                    nc.vector.tensor_tensor(hid, silu, up_s, ALU.mult).then_inc(hid_done, 1)
                    dve.wait_ge(hid_hi_done, FC * e + 1 + f)
                    nc.vector.tensor_tensor(hid_lo[:, slot, :], hid, hid_hi[:, slot, :].bitcast(F32),
                                            ALU.subtract).then_inc(hid_split, 1)

                scale(0, 0, n0 + 2)
                hidden(0, 0)
                with dve.Fori(0, (FC - 2) // 4) as i:
                    for j in range(4):
                        b = n0 + 2 + 3 * j
                        f = 4 * i + (1 + j)
                        split(b + 3, i, 12)
                        split(b + 4, i, 12)
                        scale(f, (1 + j) % 2, 12 * i + (b + 2))
                        split(b + 5, i, 12)
                        hidden(f, (1 + j) % 2)
                split(n0 + 65)
                scale(FC - 1, (FC - 1) % 2, n0 + 64)
                hidden(FC - 1, (FC - 1) % 2)
                split(n0 + 66)
                split(n0 + 67)
                residual(p, 0.5)

            def attention_mixer(n0, p):
                for b in range(2, 6):
                    split(n0 + b)
                rms(p)
                for b in range(6, 10):
                    split(n0 + b)
                token_scales(1)
                for b in range(10, 15):
                    split(n0 + b)
                dve.wait_ge(idx_copied, 2)
                heads = idx_tok[:].rearrange("p t (h d) -> p t h d", d=ID)
                h = IROT // 2
                x1, x2 = heads[:, :, :, 0:h], heads[:, :, :, h:IROT]
                shape = [P, TT, IH + 2, h]
                cos = const[:, C_ICOS:C_ICOS + TT * h].rearrange("p (t d) -> p t d", t=TT).unsqueeze(2).to_broadcast(shape)
                sin = const[:, C_ISIN:C_ISIN + TT * h].rearrange("p (t d) -> p t d", t=TT).unsqueeze(2).to_broadcast(shape)
                t1, t2, t3, t4 = (idx_t[:, n] for n in range(4))
                nc.vector.tensor_tensor(t1, x1, cos, ALU.mult)
                nc.vector.tensor_tensor(t2, x2, sin, ALU.mult)
                nc.vector.tensor_tensor(t3, x2, cos, ALU.mult)
                step(nc.vector.tensor_tensor(t4, x1, sin, ALU.mult))
                nc.vector.tensor_tensor(x1, t1, t2, ALU.subtract).then_inc(idx_roped, 1)
                nc.vector.tensor_tensor(x2, t3, t4, ALU.add).then_inc(idx_roped, 1)
                split(n0 + 15)
                split(n0 + 16)
                for a in range(2):
                    dve.wait_ge(qk_sq, a + 1)
                    step(nc.vector.tensor_reduce(qk_ss[:, 16 * a:16 * a + 16],
                                                 qk_a[:, 2 * a:2 * a + 2, :].rearrange("p t (h d) -> p (t h) d", d=HD),
                                                 AX.X, ALU.add))
                nc.vector.tensor_scalar(qk_ms[:], qk_ss[:], 1.0 / HD, EPS, ALU.mult, ALU.add).then_inc(qk_ms_done, 1)
                split(n0 + 17)
                split(n0 + 18)
                for t in range(TT):
                    n = (t + 1) * P
                    dve.wait_ge(rel_done, 2 * t + 2)
                    dst = score[:, t, 0:n]
                    step(nc.vector.tensor_scalar(dst, rel[:, t, 0, 0:n], idx_w[:, t, 0:1], None, ALU.mult))
                    for hd in range(1, IH):
                        last = nc.vector.scalar_tensor_tensor(dst, rel[:, t, hd, 0:n], idx_w[:, t, hd:hd + 1], dst,
                                                              ALU.mult, ALU.add)
                        if hd < IH - 1:
                            step(last)
                    last.then_inc(score_done, 1)
                dve.wait_ge(qk_root_done, 1)
                step(inv_root(qk_ms[:], qk_root[:], qk_nt[:], qk_r[:]))
                for a in range(2):
                    dve.wait_ge(qk_sq, a + 1)
                    heads = q_tok[:, 2 * a:2 * a + 2, :].rearrange("p t (h d) -> p (t h) d", d=HD)
                    nc.vector.tensor_tensor(heads, heads, qk_r[:, 16 * a:16 * a + 16].unsqueeze(2).to_broadcast([P, 16, HD]),
                                            ALU.mult).then_inc(qk_normed, 1)
                    split(n0 + 19 + 2 * a)
                    split(n0 + 20 + 2 * a)
                dve.wait_ge(tables_made, 4)
                for a in range(2):
                    dve.wait_ge(qk_normed, a + 1)
                    for t in range(TT):
                        last = nc.vector.tensor_tensor(
                            qk_a[:, 2 * a + t, :].rearrange("p (h d) -> p h d", d=HD),
                            q_tok[:, 2 * a + t, :].rearrange("p (h d) -> p h d", d=HD),
                            rope_c[:, a, t, :].unsqueeze(1).to_broadcast([P, HEADS, HD]), ALU.mult)
                    last.then_inc(qk_cos, 1)
                dve.wait_ge(score_masked, 2)
                for r in range(TOPK // 8):
                    for t in range(TT):
                        last = nc.vector.max(top8[:, t, :], work[:, t, 0:(t + 1) * P])
                    step(last)
                    for t in range(TT):
                        last = nc.vector.match_replace(work[:, t, 0:(t + 1) * P], top8[:, t, :],
                                                       work[:, t, 0:(t + 1) * P], UNSEL)
                    step(last)
                for t in range(TT):
                    nc.vector.tensor_scalar(score[:, t, 0:(t + 1) * P], work[:, t, 0:(t + 1) * P], UNSEL, MASKED,
                                            ALU.not_equal, ALU.mult).then_inc(sel_done, 1)
                for g in range(4):
                    dve.wait_ge(mix_hi_done, 2 * (g // 2) + 2)
                    nc.vector.scalar_tensor_tensor(mix_lo[:, PAIRS + g, :],
                                                   bank[2 + g // 2][:, (g % 2) * S:(g % 2 + 1) * S],
                                                   cols[:, COLS["pool"] + g:COLS["pool"] + g + 1],
                                                   mix_hi[:, PAIRS + g, :].bitcast(F32), ALU.mult,
                                                   ALU.subtract).then_inc(mix_split, 1)
                for b in range(23, 27):
                    split(n0 + b)
                dve.wait_ge(bias_done, 2)
                for s in range(HEADS + 2):
                    if s < HEADS:
                        dve.wait_ge(logits_done, s + 1)
                        for t in range(TT):
                            n = (t + 1) * P
                            nc.vector.tensor_tensor_reduce(logit[:, s % 2, t, 0:n], bank[4 + s % 2][:, t * P:t * P + n],
                                                           bias[:, t, 0:n], HD ** -0.5, MASKED, ALU.add, ALU.max,
                                                           top1[:, s, t:t + 1]).then_inc(logits_read, 1)
                        dve.wait_ge(logits_read, 2 * s + 2)
                        nc.vector.tensor_scalar(neg1[:, s, :], top1[:, s, :], -1.0, None, ALU.mult).then_inc(neg_done, 1)
                    if 1 <= s <= HEADS:
                        hd = s - 1
                        dve.wait_ge(exp_done, 2 * hd + 2)
                        step(nc.vector.reciprocal(rsum[:, hd, :], psums[:, hd, :]))
                        for t in range(TT):
                            n = (t + 1) * P
                            nc.vector.tensor_scalar(prob[:, hd % 2, t, 0:n], prob[:, hd % 2, t, 0:n],
                                                    rsum[:, hd, t:t + 1], None, ALU.mult).then_inc(prob_done, 1)
                    if s >= 2:
                        hd = s - 2
                        lo = hd % 2 * HD
                        dve.wait_ge(mix_hi_done, 4 + hd + 1)
                        nc.vector.tensor_tensor(mix_lo[lo:lo + HD, hd // 2, :], bank[7][lo:lo + HD, 0:S],
                                                mix_hi[lo:lo + HD, hd // 2, :].bitcast(F32),
                                                ALU.subtract).then_inc(mix_split, 1)
                split(n0 + 27)
                split(n0 + 28)
                residual(p, 1.0)

            def gated_mixer(n0, p):
                for b in range(2, 6):
                    split(n0 + b)
                rms(p)
                for b in range(6, 10):
                    split(n0 + b)
                token_scales(2)
                split(n0 + 10)
                step(nc.vector.tensor_tensor(rstd_sq[:], rstd[:], rstd[:], ALU.mult))
                with dve.Fori(0, 2) as i:
                    for j in range(4):
                        b = n0 + 8 + 3 * j
                        m = 4 * i + j
                        split(b + 3, i, 12)
                        split(b + 4, i, 12)
                        split(b + 5, i, 12)
                        dve.wait_ge(w_used, 12 * i + (b + 3))
                        pair, single = bank[4 + 2 * (j % 2)], bank[5 + 2 * (j % 2)]
                        nc.vector.tensor_tensor(gc_s, pair[:, 0:S], rstd_sq[:], ALU.mult).then_inc(gc_scaled, 1)
                        nc.vector.tensor_tensor(gb_s, single[:, 0:S], rstd[:], ALU.mult)
                        dve.wait_ge(gc_scaled, m + 1)
                        nc.vector.tensor_tensor(conv_in[:, 1:S + 1], pair[:, S:2 * S], gc_s, ALU.mult).then_inc(conv_read, 1)

                        def tap(k):
                            return cols[:, bass.ds(m + (COLS["conv"] + k * KC), 1)]

                        dve.wait_ge(conv_read, m + 1)
                        nc.vector.tensor_scalar(conv_a, conv_in[:, 0:S], tap(0), None, ALU.mult).then_inc(conv_mid, 1)
                        for k in (1, 2):
                            dve.wait_ge(conv_mid, 3 * m + k)
                            nc.vector.scalar_tensor_tensor(conv_a, conv_in[:, k:S + k], tap(k), conv_a, ALU.mult,
                                                           ALU.add).then_inc(conv_mid, 1)
                        dve.wait_ge(conv_mid, 3 * m + 3)
                        nc.vector.tensor_tensor(conv_y, conv_a, gb_s, ALU.mult).then_inc(conv_done, 1)
                        dve.wait_ge(yb_hi_done, m + 1)
                        nc.vector.tensor_tensor(yb_lo[:, bass.ds(m, 1), :], conv_y.unsqueeze(1),
                                                yb_hi[:, bass.ds(m, 1), :].bitcast(F32), ALU.subtract).then_inc(yb_split, 1)
                split(n0 + 35)
                dve.wait_ge(v_sq, 2)
                nc.vector.tensor_scalar(v_ss[:, 1, :], v_ss[:, 0, :], 1.0 / D, EPS, ALU.mult, ALU.add).then_inc(v_ms_done, 1)
                dve.wait_ge(v_root_done, 1)
                step(inv_root(v_ss[:, 1, :], v_ss[:, 2, :], v_ss[:, 3, :], v_ss[:, 4, :]))
                for t in range(TT):
                    nc.vector.tensor_scalar(v_tok[:, t, :], v_tok[:, t, :], v_ss[:, 4, t:t + 1], None,
                                            ALU.mult).then_inc(v_normed, 1)
                for b in range(36, 40):
                    split(n0 + b)

                def u_scales(m0):
                    for m in range(m0, m0 + 4):
                        dve.wait_ge(w_used, n0 + 32 + m + 1)
                        if m >= 4:
                            dve.wait_ge(ya_done, m - 3)
                        nc.vector.tensor_tensor(u_s[:, m % 4, :], bank[4 + m % 4][:, 0:S], rstd[:],
                                                ALU.mult).then_inc(u_scaled, 1)

                def u_gates(m0):
                    for m in range(m0, m0 + 4):
                        dve.wait_ge(u_gelu, m + 1)
                        dve.wait_ge(sg_done, m + 1)
                        if m >= 2:
                            dve.wait_ge(ya_split, m - 1)
                        nc.vector.tensor_tensor(ya[:, m % 2, :], u_s[:, m % 4, :], sg[:, m, :], ALU.mult).then_inc(ya_done, 1)
                        dve.wait_ge(ya_hi_done, m + 1)
                        nc.vector.tensor_tensor(ya_lo[:, m, :], ya[:, m % 2, :], ya_hi[:, m, :].bitcast(F32),
                                                ALU.subtract).then_inc(ya_split, 1)

                u_scales(0)
                dve.wait_ge(spatial_done, 1)
                dve.wait_ge(rows_loaded, 16)
                for m in range(KC):
                    nc.vector.scalar_tensor_tensor(
                        sg[:, m, :].rearrange("p (c q) -> p c q", c=TT),
                        acc(m).rearrange("p (c q) -> p c q", c=TT), cols[:, COLS["sgu"] + m:COLS["sgu"] + m + 1],
                        rows[:, 2 * HD + m * P:2 * HD + (m + 1) * P].unsqueeze(1).to_broadcast([P, TT, P]),
                        ALU.mult, ALU.add).then_inc(sg_done, 1)
                for b in range(40, 43):
                    split(n0 + b)
                u_gates(0)
                u_scales(4)
                u_gates(4)
                with dve.Fori(0, 4) as i:
                    for j in range(2):
                        b = n0 + 40 + 4 * j
                        m = 2 * i + j
                        for c in range(3, 6):
                            split(b + c, i, 8)
                        dve.wait_ge(w_used, 8 * i + (b + 2))
                        nc.vector.tensor_tensor(gates.rearrange("p (g s) -> p g s", g=2),
                                                bank[4 + 2 * j][:].rearrange("p (g s) -> p g s", g=2),
                                                rstd[:].unsqueeze(1).to_broadcast([P, 2, S]), ALU.mult).then_inc(gates_scaled, 1)
                        split(b + 6, i, 8)
                        dve.wait_ge(w_used, 8 * i + (b + 4))
                        dve.wait_ge(sig_done, m + 1)
                        nc.vector.tensor_tensor(branch, bank[5 + 2 * j][:], sig, ALU.mult).then_inc(branch_done, 1)
                        dve.wait_ge(branch_done, m + 1)
                        nc.vector.tensor_tensor(merged, branch[:, 0:S], branch[:, S:2 * S], ALU.add).then_inc(merged_done, 1)
                        dve.wait_ge(mix_hi_done, m + (4 + HEADS + 1))
                        nc.vector.tensor_tensor(mix_lo[:, bass.ds(m, 1), :], merged.unsqueeze(1),
                                                mix_hi[:, bass.ds(m, 1), :].bitcast(F32), ALU.subtract).then_inc(mix_split, 1)
                for b in range(75, 82):
                    split(n0 + b)
                residual(p, 1.0)

            split(0)
            split(1)
            dve.wait_ge(x_loaded, 16)
            dve.wait_ge(cols_loaded, 16)
            for k in range(KC):
                input_lo(0, k)
            ffn(0, START[0], 0)
            attention_mixer(START[1], 1)
            ffn(1, START[2], 2)
            ffn(2, START[3], 3)
            gated_mixer(START[4], 4)
            ffn(3, START[5], 5)
            rms(6)
            for k in range(KC):
                g = COLS["final"] + k
                nc.vector.scalar_tensor_tensor(x_sq[:, k, :], x[:, k, :], cols[:, g:g + 1], rstd[:], ALU.mult,
                                               ALU.mult).then_inc(out_ready, 1)

        @block.tensor
        def _(pe):
            def three(dst, a_hi, a_lo, b_hi, b_lo, first, last):
                nc.tensor.matmul(dst, a_hi, b_hi, start=first, stop=False, skip_group_check=True)
                nc.tensor.matmul(dst, a_hi, b_lo, start=False, stop=False, skip_group_check=True)
                return nc.tensor.matmul(dst, a_lo, b_hi, start=False, stop=last, skip_group_check=True)

            def feature_block(n, dst, b_hi, b_lo, i=0, per=0, p=None, ready=None):
                slot = n % RING
                pe.wait_ge(w_split, n + 1 + per * i)
                for k in range(KC):
                    if p is not None:
                        pe.wait_ge(x_split, 8 * p + k + 1)
                    if ready is not None:
                        pe.wait_ge(ready, k + 1)
                    w = slice(k * P, (k + 1) * P)
                    last = three(dst, w_hi[:, slot, w], w_lo[:, slot, w], b_hi[:, k, :], b_lo[:, k, :], k == 0, k == KC - 1)
                last.then_inc(w_used, 1)

            def token_block(n, b, per_block, width, dst, p=None):
                slot = n % RING
                pe.wait_ge(w_split, n + 1)
                for kk in range(min(per_block, KC - b * per_block)):
                    k = b * per_block + kk
                    if p is not None:
                        pe.wait_ge(x_split, 8 * p + k + 1)
                    for t in range(TT):
                        tok, w = slice(t * P, (t + 1) * P), slice(kk * width, (kk + 1) * width)
                        last = three(dst[t][:, 0:width], x_hi[:, k, tok], x_lo[:, k, tok], w_hi[:, slot, w],
                                     w_lo[:, slot, w], k == 0, k == KC - 1)
                last.then_inc(w_used, 1)

            def chunk_block(n, b_hi, b_lo, i=0, per=0):
                slot = n % RING
                pe.wait_ge(w_split, n + 1 + per * i)
                for m in range(KC):
                    w = slice(m * P, (m + 1) * P)
                    last = three(acc(m), w_hi[:, slot, w], w_lo[:, slot, w], b_hi, b_lo, False, False)
                last.then_inc(w_used, 1)

            def last_chunks(n, ops):
                pe.wait_ge(w_split, n + 2)
                for m in range(KC):
                    w = slice(m * P, (m + 1) * P)
                    for c, (b_hi, b_lo) in enumerate(ops):
                        slot = (n + c) % RING
                        last = three(acc(m), w_hi[:, slot, w], w_lo[:, slot, w], b_hi, b_lo, False, c == 1)
                    if m % 2:
                        last.then_inc(acc_done, 1)
                for c in range(2):
                    nc.tensor.matmul(bank[6][0:P, 0:2], zeros[:, 0:P], zeros[:, 0:2], start=True, stop=True,
                                     skip_group_check=True).then_inc(w_used, 1)

            def sum_squares(p):
                if p == 0:
                    pe.wait_ge(const_loaded, 16)
                pe.wait_ge(x_sq_done, 8 * p + 8)
                for k in range(KC):
                    last = nc.tensor.matmul(bank[STAT[p]][:, 0:S], ones, x_sq[:, k, :], start=(k == 0), stop=(k == KC - 1),
                                            skip_group_check=True)
                last.then_inc(sumsq_done, 1)

            def token_scales(p):
                pe.wait_ge(rstd_done, p + 1)
                for t in range(TT):
                    last = nc.tensor.transpose(bank[2][:, t * P:(t + 1) * P], rstd[:, t * P:(t + 1) * P], ident)
                last.then_inc(rT_done, 1)

            def clear_acc():
                for a in range(4):
                    nc.tensor.matmul(bank[a][:], zeros[:, 0:P], zeros[:], start=True, stop=False, skip_group_check=True)

            def ffn(e, n0, p):
                feature_block(n0, bank[4][:, 0:S], x_hi, x_lo, p=p)
                sum_squares(p)
                clear_acc()
                feature_block(n0 + 1, bank[4][:, S:2 * S], x_hi, x_lo)
                with pe.Fori(0, (FC - 2) // 4) as i:
                    for j in range(4):
                        b = n0 + 2 + 3 * j
                        g = bank[4 + (1 + j) % 2]
                        feature_block(b, g[:, 0:S], x_hi, x_lo, i, 12)
                        feature_block(b + 1, g[:, S:2 * S], x_hi, x_lo, i, 12)
                        pe.wait_ge(hid_split, 4 * i + (FC * e + 1 + j))
                        chunk_block(b + 2, hid_hi[:, j % 2, :], hid_lo[:, j % 2, :], i, 12)
                g = bank[4 + (FC - 1) % 2]
                feature_block(n0 + 62, g[:, 0:S], x_hi, x_lo)
                feature_block(n0 + 63, g[:, S:2 * S], x_hi, x_lo)
                pe.wait_ge(hid_split, FC * (e + 1))
                last_chunks(n0 + 64, [(hid_hi[:, f % 2, :], hid_lo[:, f % 2, :]) for f in (FC - 2, FC - 1)])

            def attention_mixer(n0, p):
                for b in range(4):
                    token_block(n0 + b, b, TOK_K, 512, (bank[4], bank[5]), p)
                sum_squares(p)
                for b in range(4):
                    if b == 2:
                        token_scales(p)
                    token_block(n0 + 4 + b, b, TOK_K, 512, (bank[6], bank[7]))
                for b in range(IDX_B):
                    token_block(n0 + 8 + b, b, IDX_K, IDX_W, (bank[0], bank[1]))
                pe.wait_ge(r_col_done, 1)
                for b in range(2):
                    token_block(n0 + 11 + b, b, TOK_K, 512, (bank[2], bank[3]))
                pe.wait_ge(idx_roped, 2)
                pe.wait_ge(q_copied, 4)
                for c in range(3):
                    for t in range(TT):
                        dst = bank[6 + c // 2][:, (c % 2) * S + t * P:(c % 2) * S + (t + 1) * P]
                        last = nc.tensor.transpose(dst, idx_tok[:, t, c * P:(c + 1) * P], ident)
                last.then_inc(idx_T, 1)
                for b in range(2, 4):
                    token_block(n0 + 11 + b, b, TOK_K, 512, (bank[2], bank[3]))
                pe.wait_ge(idx_T_copied, 2)
                for t in range(TT):
                    for hd in range(IH):
                        rows_ = slice(hd % 2 * ID, hd % 2 * ID + ID)
                        n = (t + 1) * P
                        dst = bank[6 * t + hd % 2][:, hd // 2 * n:(hd // 2 + 1) * n]
                        last = nc.tensor.matmul(dst, qiT[rows_, hd // 2, t * P:(t + 1) * P], kiT[rows_, 0:n], start=True,
                                                stop=True, skip_group_check=True)
                last.then_inc(idx_dots, 1)
                for b in range(4):
                    token_block(n0 + 15 + b, b, TOK_K, 512, (bank[4], bank[5]))
                band = const[:, C_BAND:].rearrange("p (t g s) -> p t g s", t=TT, g=4)
                pe.wait_ge(u_copied, 2)
                pe.wait_ge(v_copied, 2)
                for g in range(4):
                    for t in range(TT):
                        last = nc.tensor.matmul(bank[2 + g // 2][:, (g % 2) * S:(g % 2 + 1) * S],
                                                u_tok[:, t, g * P:(g + 1) * P], band[:, t, g, :], start=(t == 0),
                                                stop=(t == TT - 1), skip_group_check=True)
                    if g % 2:
                        last.then_inc(pool_mean, 1)
                pe.wait_ge(pool_loaded, 16)
                for g in range(4):
                    pe.wait_ge(pool_mean_copied, 2 * (g // 2) + 2)
                    last = nc.tensor.matmul(bank[2 + g // 2][:, (g % 2) * S:(g % 2 + 1) * S], pool_w[:, g, :],
                                            pool_in[:, g, :], start=True, stop=True, skip_group_check=True)
                    if g % 2:
                        last.then_inc(pool_out, 1)
                pe.wait_ge(mix_split, 4)
                pe.wait_ge(rel_done, 4)
                clear_acc()
                for g in range(4):
                    chunk_block(n0 + 19 + g, mix_hi[:, PAIRS + g, :], mix_lo[:, PAIRS + g, :])
                for a in range(2):
                    pe.wait_ge(qk_roped, a + 1)
                    for c in range(PAIRS):
                        for t in range(TT):
                            dst = bank[(6, 7, 4, 5)[2 * a + c // 2]][:, (c % 2) * S + t * P:(c % 2) * S + (t + 1) * P]
                            last = nc.tensor.transpose(dst, qk_b[:, 2 * a + t, c * P:(c + 1) * P], ident)
                        if c % 2:
                            last.then_inc(qk_T, 1)
                pe.wait_ge(qk_T_copied, 4)
                for s in range(HEADS + 2):
                    if s < HEADS:
                        rows_ = slice(s % 2 * HD, s % 2 * HD + HD)
                        if s >= 2:
                            pe.wait_ge(logits_read, 2 * (s - 1))
                        for t in range(TT):
                            n = (t + 1) * P
                            last = nc.tensor.matmul(bank[4 + s % 2][:, t * P:t * P + n], qT[rows_, s // 2, t * P:(t + 1) * P],
                                                    kT[rows_, s // 2, 0:n], start=True, stop=True, skip_group_check=True)
                        last.then_inc(logits_done, 1)
                    if 1 <= s <= HEADS:
                        hd = s - 1
                        pe.wait_ge(prob_done, 2 * s)
                        if hd:
                            pe.wait_ge(probT_copied, hd)
                        for n, (t, kt) in enumerate(((0, 0), (1, 0), (1, 1))):
                            last = nc.tensor.transpose(bank[6][:, n * P:(n + 1) * P],
                                                       prob[:, hd % 2, t, kt * P:(kt + 1) * P], ident)
                        last.then_inc(probT_done, 1)
                    if s >= 2:
                        hd = s - 2
                        pe.wait_ge(probT_copied, hd + 1)
                        if hd:
                            pe.wait_ge(mix_split, 4 + hd)
                        pair = slice(hd // 2 * P, (hd // 2 + 1) * P)
                        nc.tensor.matmul(bank[7][:, 0:S], v_tok[:, 0, pair], probT[:, hd % 2, 0:S], start=True, stop=False,
                                         skip_group_check=True)
                        nc.tensor.matmul(bank[7][:, P:S], v_tok[:, 1, pair], probT[:, hd % 2, S:S + P], start=False,
                                         stop=True, skip_group_check=True).then_inc(pv_done, 1)
                    if s in (5, 7):
                        c = (s - 5) // 2
                        pe.wait_ge(mix_split, 4 + 2 * c + 2)
                        chunk_block(n0 + 23 + c, mix_hi[:, c, :], mix_lo[:, c, :])
                pe.wait_ge(mix_split, 4 + HEADS)
                last_chunks(n0 + 25, [(mix_hi[:, c, :], mix_lo[:, c, :]) for c in (2, 3)])

            def gated_mixer(n0, p):
                for b in range(4):
                    token_block(n0 + b, b, TOK_K, 512, (bank[4], bank[5]), p)
                sum_squares(p)
                for b in range(4):
                    if b == 2:
                        token_scales(p)
                    token_block(n0 + 4 + b, b, TOK_K, 512, (bank[6], bank[7]))
                pe.wait_ge(v_gelu, 4)
                with pe.Fori(0, 2) as i:
                    for j in range(4):
                        b = n0 + 8 + 3 * j
                        pair, single = bank[4 + 2 * (j % 2)], bank[5 + 2 * (j % 2)]
                        if j >= 2:
                            pe.wait_ge(conv_read, 4 * i + (j - 1))
                        feature_block(b, pair[:, 0:S], x_hi, x_lo, i, 12)
                        feature_block(b + 1, pair[:, S:2 * S], x_hi, x_lo, i, 12)
                        feature_block(b + 2, single[:, 0:S], x_hi, x_lo, i, 12)
                    pe.wait_ge(conv_read, 4 * i + 4)
                for m in range(4):
                    feature_block(n0 + 32 + m, bank[4 + m][:, 0:S], x_hi, x_lo)
                pe.wait_ge(v_normed, 2)
                pe.wait_ge(sgu_loaded, 16)
                for m in range(KC):
                    for t in range(TT):
                        last = nc.tensor.matmul(acc(m)[:, t * P:(t + 1) * P], v_tok[:, t, m * P:(m + 1) * P], sgu_w[:, m, :],
                                                start=True, stop=True, skip_group_check=True)
                last.then_inc(spatial_done, 1)
                for m in range(4, KC):
                    pe.wait_ge(u_scaled, m - 3)
                    feature_block(n0 + 32 + m, bank[m][:, 0:S], x_hi, x_lo)
                pe.wait_ge(u_scaled, KC)
                with pe.Fori(0, 4) as i:
                    for j in range(2):
                        b = n0 + 40 + 4 * j
                        g, y = bank[4 + 2 * j], bank[5 + 2 * j]
                        feature_block(b, g[:, 0:S], x_hi, x_lo, i, 8)
                        feature_block(b + 1, g[:, S:2 * S], x_hi, x_lo, i, 8)
                        pe.wait_ge(ya_split, KC)
                        feature_block(b + 2, y[:, 0:S], ya_hi, ya_lo, i, 8)
                        pe.wait_ge(yb_split, KC)
                        feature_block(b + 3, y[:, S:2 * S], yb_hi, yb_lo, i, 8)
                        if j:
                            pe.wait_ge(branch_done, 2 * i + 1)
                base = 4 + HEADS
                pe.wait_ge(sg_done, KC)
                clear_acc()
                for c in range(KC - 2):
                    pe.wait_ge(mix_split, base + c + 1)
                    chunk_block(n0 + 72 + c, mix_hi[:, c, :], mix_lo[:, c, :])
                pe.wait_ge(mix_split, base + KC)
                last_chunks(n0 + 72 + KC - 2, [(mix_hi[:, c, :], mix_lo[:, c, :]) for c in (KC - 2, KC - 1)])

            pe.wait_ge(zeros_set, 2)
            ffn(0, START[0], 0)
            attention_mixer(START[1], 1)
            ffn(1, START[2], 2)
            ffn(2, START[3], 3)
            gated_mixer(START[4], 4)
            ffn(3, START[5], 5)
            sum_squares(6)


STAT = [6, 3, 6, 6, 3, 6, 6]


def _cols(a):
    return np.asarray(a, np.float32).reshape(-1, P).T


def _features(w):
    return w.reshape(KC, P, -1, P).transpose(2, 1, 0, 3).reshape(-1, P, BW)


def _tokens(w, per_block):
    width = w.shape[1]
    n = -(-KC // per_block)
    out = np.zeros((n, P, BW), np.float32)
    for k in range(KC):
        b, j = divmod(k, per_block)
        out[b, :, j * width:(j + 1) * width] = w[k * P:(k + 1) * P]
    return out


def _chunks(w):
    return w.reshape(-1, P, BW)


def _ffn(gate, up, down):
    g, u, d = _features(gate), _features(up), _chunks(down)
    out = [g[0], u[0]]
    for f in range(1, FC):
        out += [g[f], u[f]]
        if f < FC - 1:
            out.append(d[f - 1])
    return np.stack(out + [d[FC - 2], d[FC - 1]])


def _constants():
    c = np.zeros((P, NCONST), np.float32)
    pos = np.arange(S, dtype=np.float32)

    def tables(half):
        inv = np.float32(THETA) ** (-np.arange(half, dtype=np.float32) / np.float32(half))
        ang = pos[:, None] * inv[None, :]
        return np.cos(ang), np.sin(ang)

    cos, sin = tables(HD // 2)
    c[:, C_COS:C_COS + P] = np.concatenate([cos, cos], 1).reshape(TT, P, HD).transpose(1, 0, 2).reshape(P, -1)
    c[:, C_SIN:C_SIN + P] = np.concatenate([-sin, sin], 1).reshape(TT, P, HD).transpose(1, 0, 2).reshape(P, -1)
    cos, sin = tables(IROT // 2)
    c[:, C_ICOS:C_ICOS + 32] = cos.reshape(TT, P, -1).transpose(1, 0, 2).reshape(P, -1)
    c[:, C_ISIN:C_ISIN + 32] = sin.reshape(TT, P, -1).transpose(1, 0, 2).reshape(P, -1)
    c[:, C_ID:C_ID + P] = np.eye(P)
    c[:, C_ONE:C_ONE + P] = 1.0
    band = np.zeros((S, 4, S), np.float32)
    for g, w in enumerate(POOLS):
        for t in range(S):
            lo = max(0, t - w + 1)
            band[lo:t + 1, g, t] = np.float32(1.0) / np.float32(t + 1 - lo)
            band[t, g, t] -= 1.0
    c[:, C_BAND:] = band.reshape(TT, P, 4 * S).transpose(1, 0, 2).reshape(P, -1)
    return c


def kernel(**inputs):
    import concourse.bacc as bacc
    from concourse.bass_utils import run_bass_kernel_spmd

    a = {k: np.asarray(v) for k, v in inputs.items()}
    w1 = {k: v[0] for k, v in a.items() if k not in ("x", "final_norm_2")}
    wi, wz = w1["w_in"], w1["w_in_2"]
    n_idx = 3 * ATT + IDX_W
    wo = _chunks(w1["w_out"])
    z = _features(wz)
    pa, pb = _features(w1["w_proj_a_2"]), _features(w1["w_proj_b_2"])
    up1, up2 = w1["ffn1_w_in_2"], w1["ffn2_w_in_2"]
    stream = np.concatenate([
        _ffn(w1["ffn1_w_gate"], w1["ffn1_w_up"], w1["ffn1_w_down"]),
        _tokens(wi[:, 0:ATT], TOK_K), _tokens(wi[:, ATT:2 * ATT], TOK_K), _tokens(wi[:, 3 * ATT:n_idx], IDX_K),
        _tokens(wi[:, 2 * ATT:3 * ATT], TOK_K), _tokens(wi[:, n_idx:], TOK_K), wo[4:], wo[:4],
        _ffn(w1["ffn2_w_gate"], w1["ffn2_w_up"], w1["ffn2_w_down"]),
        _ffn(up1[:, :FF], up1[:, FF:], w1["ffn1_w_out_2"]),
        _tokens(wz[:, D:D + 512], TOK_K), _tokens(wz[:, D + 512:2 * D], TOK_K),
        np.stack([z[c + m] for m in range(KC) for c in (24, 32, 16)]), z[0:8],
        np.stack([b[m] for m in range(KC) for b in (z[40:48], z[48:56], pa, pb)]),
        _chunks(w1["w_out_2"]),
        _ffn(up2[:, :FF], up2[:, FF:], w1["ffn2_w_out_2"]),
    ])
    assert stream.shape == (BLOCKS, P, BW)
    arrays = {
        "stream": stream,
        "x_in": a["x"][0].T.reshape(KC, P, S).transpose(1, 0, 2),
        "cols_in": np.concatenate([_cols(v) for v in (
            w1["ffn1_norm"], w1["mix_norm"], w1["ffn2_norm"], w1["ffn1_norm_2"], w1["mix_norm_2"], w1["ffn2_norm_2"],
            a["final_norm_2"], w1["sgu_norm_2"], w1["conv_w_2"].reshape(-1), w1["pool_scale"])], 1),
        "rows_in": np.broadcast_to(np.concatenate([w1["q_norm"], w1["k_norm"], w1["sgu_b_2"].reshape(-1)]),
                                   (P, 2 * HD + SGU_HEADS * P)),
        "const_in": _constants(),
        "sgu_w_in": w1["sgu_w_2"].transpose(2, 0, 1),
        "pool_w_in": w1["pool_w"].transpose(1, 0, 2),
    }
    arrays = {k: np.ascontiguousarray(v) for k, v in arrays.items()}
    nc = bacc.Bacc("TRN2", target_bir_lowering=False, num_devices=1)
    args = [nc.dram_tensor(k, v.shape, F32, kind="ExternalInput").ap() for k, v in arrays.items()]
    args.append(nc.dram_tensor("out", (P, KC, S), F32, kind="ExternalOutput").ap())
    build(nc, *args)
    r = run_bass_kernel_spmd(nc, [arrays], core_ids=[0])
    y = r.results[0]["out"]
    return y.transpose(1, 0, 2).reshape(D, S).T.reshape(1, S, D)
```

```python
from contextlib import ExitStack

import numpy as np

import concourse.bass as bass
from concourse import mybir

F32 = mybir.dt.float32
F32R = mybir.dt.float32r
BF16 = mybir.dt.bfloat16
ALU = mybir.AluOpType
ACT = mybir.ActivationFunctionType
AX = mybir.AxisListType

P = 128
D = 1024
S = 256
KC = D // P
TT = S // P
FF = 2816
FC = FF // P
HEADS, HD = 8, 64
ATT = HEADS * HD
PAIRS = ATT // P
IH, ID, IROT = 4, 64, 32
TOPK = 64
POOLS = (2, 4, 8, 16)
THETA = 10000.0
EPS = 1e-6
SGU_HEADS = 8
CONV = 3

BW = 1024
RING = 4
IDX_W = IH * ID + ID + IH
IDX_K = BW // IDX_W
IDX_B = -(-KC // IDX_K)
TOK_K = BW // 512
TOK_B = KC // TOK_K

FFN_B = 3 * FC
LOOPED = (FC - 4) // 4 * 4
MIX1_B = 4 * TOK_B + IDX_B + KC
CONV_B, GATE_B = 3 * KC, 4 * KC
MIX2_B = 2 * TOK_B + CONV_B + KC + GATE_B + KC
START = np.cumsum([0, FFN_B, MIX1_B, FFN_B, FFN_B, MIX2_B, FFN_B]).tolist()
BLOCKS = START[-1]

COLS = {"ffn1": 0, "mix": 8, "ffn2": 16, "ffn1_2": 24, "mix_2": 32, "ffn2_2": 40, "final": 48, "sgu": 56,
        "conv": 64, "pool": 88}
NCOLS = 92
PHASE_GAIN = ["ffn1", "mix", "ffn2", "ffn1_2", "mix_2", "ffn2_2", "final"]
C_COS, C_SIN, C_ICOS, C_ISIN, C_ID, C_BAND = 0, 128, 256, 288, 320, 448
NCONST = 448 + 2 * 4 * 256

UNSEL, NEG, MASKED = -3.0e38, -2.0e38, -1.0e30


def build(nc, stream, x_in, cols_in, rows_in, const_in, sgu_w_in, pool_w_in, out):
    ctx = ExitStack()
    with ctx:
        def sb(name, shape, dt=F32):
            return ctx.enter_context(nc.sbuf_tensor(name, shape, dt))

        def sem(name):
            return ctx.enter_context(nc.semaphore(name))

        w_raw = sb("w_raw", [P, RING, BW])
        w_hi = sb("w_hi", [P, RING, BW], F32R)
        w_lo = sb("w_lo", [P, RING, BW], F32R)
        x = sb("x", [P, KC, S])
        x_hi = sb("x_hi", [P, KC, S], F32R)
        x_lo = sb("x_lo", [P, KC, S], F32R)
        x_sq = sb("x_sq", [P, KC, S])
        ms = sb("ms", [P, S])
        root = sb("root", [P, S])
        newton = sb("newton", [P, S])
        rstd = sb("rstd", [P, S])
        rstd_sq = sb("rstd_sq", [P, S])
        r_col = sb("r_col", [P, TT])
        r_col16 = sb("r_col16", [P, TT])
        cols = sb("cols", [P, NCOLS])
        rows = sb("rows", [P, 2 * HD + SGU_HEADS * P])
        const = sb("const", [P, NCONST])
        sgu_w = sb("sgu_w", [P, SGU_HEADS, P])
        pool_w = sb("pool_w", [P, 4, P])
        ones = sb("ones", [P, P])
        zeros = sb("zeros", [P, 512], BF16)
        tmp = sb("tmp", [P, 4, S])
        gate_s, up_s, silu, hid = (tmp[:, n, :] for n in range(4))
        hid_hi = sb("hid_hi", [P, 4, S], F32R)
        hid_lo = sb("hid_lo", [P, 4, S], F32R)
        mix_hi = sb("mix_hi", [P, KC, S], F32R)
        mix_lo = sb("mix_lo", [P, KC, S], F32R)
        q_tok = sb("q_tok", [P, 2 * TT, ATT])
        qk_a = sb("qk_a", [P, 2 * TT, ATT])
        qk_b = x_sq[:].rearrange("p (a b) s -> p a (b s)", b=2)
        v_tok = sb("v_tok", [P, TT, D])
        u_tok = v_tok[:, :, ATT:2 * ATT]
        qk_ss = sb("qk_ss", [P, 2 * TT * HEADS])
        qk_ms = sb("qk_ms", [P, 2 * TT * HEADS])
        qk_root = sb("qk_root", [P, 2 * TT * HEADS])
        qk_nt = sb("qk_nt", [P, 2 * TT * HEADS])
        qk_r = sb("qk_r", [P, 2 * TT * HEADS])
        rope_c = sb("rope_c", [P, 2, TT, HD])
        rope_s = sb("rope_s", [P, 2, TT, HD])
        idx_tok = sb("idx_tok", [P, TT, (IH + 2) * ID])
        idx_w = sb("idx_w", [P, TT, IH])
        idx_t = tmp[:].rearrange("p a s -> p (a s)")[:, 0:4 * TT * (IH + 2) * IROT // 2].rearrange(
            "p (a t h d) -> p a t h d", a=4, t=TT, h=IH + 2)
        qiT = sb("qiT", [P, 2, S])
        kiT = sb("kiT", [P, S])
        rel = x_sq[:].rearrange("p (t h) s -> p t h s", t=TT)
        score = sb("score", [P, TT, S])
        work = sb("work", [P, TT, S])
        top8 = sb("top8", [P, TT, 8])
        bias = sb("bias", [P, TT, S])
        qT = q_tok[:, 0:2, :].rearrange("p a (b s) -> p (a b) s", b=2)
        kT = q_tok[:, 2:4, :].rearrange("p a (b s) -> p (a b) s", b=2)
        logit = qk_a[:, 0:2, :].rearrange("p a (t s) -> p a t s", t=TT)
        prob = qk_a[:, 2:4, :].rearrange("p a (t s) -> p a t s", t=TT)
        top1 = sb("top1", [P, HEADS, TT])
        neg1 = sb("neg1", [P, HEADS, TT])
        psums = sb("psums", [P, HEADS, TT])
        rsum = sb("rsum", [P, HEADS, TT])
        probT = idx_tok
        pool_in = tmp
        v_ss = sb("v_ss", [P, 5, TT])
        gc_s, gb_s, conv_a, conv_y = (tmp[:, n, :] for n in range(4))
        conv_in = sb("conv_in", [P, S + 2])
        yb_hi = sb("yb_hi", [P, KC, S], F32R)
        yb_lo = sb("yb_lo", [P, KC, S], F32R)
        ya_hi = sb("ya_hi", [P, KC, S], F32R)
        ya_lo = sb("ya_lo", [P, KC, S], F32R)
        sg = x_sq
        u_s = qk_a[:].rearrange("p a (b s) -> p (a b) s", b=2)
        gates, sig, branch = (q_tok[:, n, :] for n in range(3))
        ya = q_tok[:, 3, :].rearrange("p (a s) -> p a s", a=2)
        merged = tmp[:, 0, :]

        bank = [ctx.enter_context(nc.psum_tensor(f"bank{i}", [P, 512], F32)) for i in range(8)]

        ident = const[:, C_ID:C_ID + P]

        def acc(m):
            return bank[m // 2][:, (m % 2) * S:(m % 2 + 1) * S]

        arrived = [sem(f"arrived{i}") for i in range(RING)]
        w_hi_done = sem("w_hi_done")
        w_split = sem("w_split")
        w_used = sem("w_used")
        x_loaded = [sem(f"x_loaded{c}") for c in range(4)]
        cols_loaded = sem("cols_loaded")
        const_loaded = sem("const_loaded")
        rows_loaded = sem("rows_loaded")
        sgu_loaded = sem("sgu_loaded")
        pool_loaded = sem("pool_loaded")
        filled = sem("filled")
        tables_made = sem("tables_made")
        acc_done = sem("acc_done")
        x_new = sem("x_new")
        x_hi_done = sem("x_hi_done")
        x_split = sem("x_split")
        x_sq_done = sem("x_sq_done")
        x_sq_added = sem("x_sq_added")
        sumsq_done = sem("sumsq_done")
        ms_done = sem("ms_done")
        root_done = sem("root_done")
        rstd_done = sem("rstd_done")
        rT_done = sem("rT_done")
        r_col_done = sem("r_col_done")
        gate_scaled = sem("gate_scaled")
        up_scaled = sem("up_scaled")
        silu_done = sem("silu_done")
        hid_done = sem("hid_done")
        hid_hi_done = sem("hid_hi_done")
        hid_split = sem("hid_split")
        q_copied = sem("q_copied")
        qk_sq = sem("qk_sq")
        qk_ms_done = sem("qk_ms_done")
        qk_root_done = sem("qk_root_done")
        qk_normed = sem("qk_normed")
        qk_cos = sem("qk_cos")
        qk_sin = sem("qk_sin")
        qk_roped = sem("qk_roped")
        idx_copied = sem("idx_copied")
        idx_roped = sem("idx_roped")
        idx_T = sem("idx_T")
        idx_T_copied = sem("idx_T_copied")
        v_copied = sem("v_copied")
        u_copied = sem("u_copied")
        idx_dots = sem("idx_dots")
        rel_done = sem("rel_done")
        score_done = sem("score_done")
        score_masked = sem("score_masked")
        sel_done = sem("sel_done")
        bias_done = sem("bias_done")
        pool_mean = sem("pool_mean")
        pool_mean_copied = sem("pool_mean_copied")
        pool_out = sem("pool_out")
        mix_hi_done = sem("mix_hi_done")
        mix_split = sem("mix_split")
        qk_T = sem("qk_T")
        qk_T_copied = sem("qk_T_copied")
        logits_done = sem("logits_done")
        logits_read = sem("logits_read")
        neg_done = sem("neg_done")
        exp_done = sem("exp_done")
        prob_done = sem("prob_done")
        probT_done = sem("probT_done")
        probT_copied = sem("probT_copied")
        pv_done = sem("pv_done")
        v_gelu = sem("v_gelu")
        v_sq = sem("v_sq")
        v_ms_done = sem("v_ms_done")
        v_root_done = sem("v_root_done")
        v_normed = sem("v_normed")
        spatial_done = sem("spatial_done")
        sg_done = sem("sg_done")
        conv_read = sem("conv_read")
        gc_scaled = sem("gc_scaled")
        conv_filled = sem("conv_filled")
        conv_mid = sem("conv_mid")
        conv_done = sem("conv_done")
        yb_hi_done = sem("yb_hi_done")
        yb_split = sem("yb_split")
        u_scaled = sem("u_scaled")
        u_gelu = sem("u_gelu")
        ya_done = sem("ya_done")
        ya_hi_done = sem("ya_hi_done")
        ya_split = sem("ya_split")
        gates_scaled = sem("gates_scaled")
        sig_done = sem("sig_done")
        branch_done = sem("branch_done")
        merged_done = sem("merged_done")
        dve_step = sem("dve_step")
        out_ready = sem("out_ready")
        stored = sem("stored")

        block = ctx.enter_context(nc.Block())

        @block.sync
        def _(sp):
            for n in range(RING):
                sp.dma_start(w_raw[:, n, :], stream[n]).then_inc(arrived[n], 16)
            with sp.Fori(1, BLOCKS // RING) as i:
                for j in range(RING):
                    sp.wait_ge(w_split, RING * i + (j - RING + 1))
                    sp.dma_start(w_raw[:, j, :],
                                 stream[bass.ds(RING * i + j, 1), :, :].rearrange("a p c -> p (a c)")
                                 ).then_inc(arrived[j], 16)
            for n in range(BLOCKS // RING * RING, BLOCKS):
                sp.wait_ge(w_split, n - RING + 1)
                sp.dma_start(w_raw[:, n % RING, :], stream[n]).then_inc(arrived[n % RING], 16)
            for c in range(4):
                sp.wait_ge(out_ready, 2 * c + 2)
                sp.dma_start(out[:, 2 * c:2 * c + 2, :], x_sq[:, 2 * c:2 * c + 2, :]).then_inc(stored, 16)
            sp.wait_ge(stored, 64)

        @block.gpsimd
        def _(pool):
            nc.gpsimd.memset(zeros[:], 0.0).then_inc(filled, 1)
            nc.gpsimd.memset(ones[:], 1.0).then_inc(filled, 1)
            nc.gpsimd.memset(conv_in[:], 0.0).then_inc(filled, 1)

            def add_squares(p):
                def pair(c):
                    return x_sq[:, 2 * c:2 * c + 2, :].rearrange("p a s -> p (a s)")

                for c in range(1, 4):
                    pool.wait_ge(x_sq_done, 4 * p + c + 1)
                    if c > 1:
                        pool.wait_ge(x_sq_added, 3 * p + c - 1)
                    nc.gpsimd.tensor_tensor(pair(0), pair(0), pair(c), ALU.add).then_inc(x_sq_added, 1)

            add_squares(0)
            pool.dma_start(const[:], const_in).then_inc(const_loaded, 16)
            pool.dma_start(rows[:], rows_in).then_inc(rows_loaded, 16)
            pool.dma_start(pool_w[:], pool_w_in).then_inc(pool_loaded, 16)
            pool.dma_start(sgu_w[:], sgu_w_in).then_inc(sgu_loaded, 16)
            pool.wait_ge(const_loaded, 16)
            pool.wait_ge(rows_loaded, 16)
            cos = const[:, C_COS:C_COS + P].rearrange("p (t d) -> p t d", t=TT)
            sin = const[:, C_SIN:C_SIN + P].rearrange("p (t d) -> p t d", t=TT)
            h = HD // 2
            for a in range(2):
                for t in range(TT):
                    gain = rows[:, a * HD:(a + 1) * HD]
                    nc.gpsimd.tensor_tensor(rope_c[:, a, t, :], gain, cos[:, t, :], ALU.mult)
                    nc.gpsimd.tensor_tensor(rope_s[:, a, t, 0:h], gain[:, h:HD], sin[:, t, 0:h], ALU.mult)
                    last = nc.gpsimd.tensor_tensor(rope_s[:, a, t, h:HD], gain[:, 0:h], sin[:, t, h:HD], ALU.mult)
                    last.then_inc(tables_made, 1)
            add_squares(1)
            pool.wait_ge(tables_made, 4)

            def partner_terms(a):
                pool.wait_ge(qk_normed, a + 1)
                for t in range(TT):
                    src = q_tok[:, 2 * a + t, :].rearrange("p (h d) -> p h d", d=HD)
                    dst = qk_b[:, 2 * a + t, :].rearrange("p (h d) -> p h d", d=HD)
                    for lo, hi in ((0, h), (h, 0)):
                        nc.gpsimd.tensor_tensor(dst[:, :, lo:lo + h], src[:, :, hi:hi + h],
                                                rope_s[:, a, t, lo:lo + h].unsqueeze(1).to_broadcast([P, HEADS, h]),
                                                ALU.mult).then_inc(qk_sin, 1)

            pool.wait_ge(score_done, 2)
            partner_terms(0)
            for t in range(TT):
                n = (t + 1) * P
                nc.gpsimd.affine_select(out=work[:, t, 0:n], in_=score[:, t, 0:n], compare_op=ALU.is_ge, fill=NEG,
                                        base=t * P, pattern=[[-1, n]], channel_multiplier=1).then_inc(score_masked, 1)
            partner_terms(1)
            for t in range(TT):
                n = (t + 1) * P
                pool.wait_ge(sel_done, t + 1)
                nc.gpsimd.affine_select(out=bias[:, t, 0:n], in_=score[:, t, 0:n], compare_op=ALU.is_ge, fill=MASKED,
                                        base=t * P, pattern=[[-1, n]], channel_multiplier=1).then_inc(bias_done, 1)
            for p in range(2, 6):
                add_squares(p)

        @block.scalar
        def _(act):
            def split(n, i=0, per=0):
                if n >= BLOCKS:
                    return
                slot = n % RING
                act.wait_ge(arrived[slot], 16 * (n // RING + 1) + 16 * (per // RING) * i)
                if n >= RING:
                    act.wait_ge(w_used, n - RING + 1 + per * i)
                nc.scalar.activation(w_hi[:, slot, :], w_raw[:, slot, :], ACT.Copy).then_inc(w_hi_done, 1)

            def phase_input(p):
                g = COLS[PHASE_GAIN[p]]

                def square(c):
                    nc.scalar.activation(x_sq[:, 2 * c:2 * c + 2, :], x[:, 2 * c:2 * c + 2, :],
                                         ACT.Square).then_inc(x_sq_done, 1)

                for c in range(4):
                    if p:
                        act.wait_ge(x_new, 4 * (p - 1) + c + 1)
                    else:
                        act.wait_ge(x_loaded[c], 16)
                    if p == 6:
                        square(c)
                        continue
                    for k in (2 * c, 2 * c + 1):
                        nc.scalar.activation(x_hi[:, k, :], x[:, k, :], ACT.Identity,
                                             scale=cols[:, g + k:g + k + 1]).then_inc(x_hi_done, 1)
                    if 1 <= c < 3:
                        square(c - 1)
                if p < 6:
                    split(START[p] + 2)
                    square(2)
                    square(3)

            def rms_root(p):
                act.wait_ge(ms_done, p + 1)
                nc.scalar.activation(root[:], ms[:], ACT.Sqrt).then_inc(root_done, 1)

            def ffn(e, n0, p):
                for b in range(3, 6):
                    split(n0 + b)
                rms_root(p)

                def gate(f):
                    act.wait_ge(gate_scaled, FC * e + 1 + f)
                    nc.scalar.activation(silu, gate_s, ACT.Silu).then_inc(silu_done, 1)

                def hidden(f, slot):
                    act.wait_ge(hid_done, FC * e + 1 + f)
                    nc.scalar.activation(hid_hi[:, slot, :], hid, ACT.Copy).then_inc(hid_hi_done, 1)

                for f in range(3):
                    split(n0 + 6 + 2 * f)
                    gate(f)
                    split(n0 + 7 + 2 * f)
                    hidden(f, f)

                def chunk(f, j, i=0):
                    b = n0 + 10 + 3 * (f - 4)
                    split(b + 2, i, 12)
                    gate(4 * i + (f - 1))
                    hidden(4 * i + (f - 1), (j - 1) % 4)
                    split(b + 3, i, 12)
                    split(b + 4, i, 12)

                with act.Fori(0, LOOPED // 4) as i:
                    for j in range(4):
                        chunk(4 + j, j, i)
                for f in range(4 + LOOPED, FC):
                    chunk(f, f % 4)
                split(n0 + FFN_B)
                gate(FC - 1)
                hidden(FC - 1, (FC - 1) % 4)
                split(n0 + FFN_B + 1)

            def attention_mixer(n0, p):
                for b in range(3, 6):
                    split(n0 + b)
                rms_root(p)
                for b in range(6, 10):
                    split(n0 + b)
                act.wait_ge(r_col_done, 1)

                def tokens_out(dst, src, used, done):
                    act.wait_ge(w_used, n0 + used)
                    for t in range(TT):
                        nc.scalar.activation(dst[t], src[t], ACT.Identity, scale=r_col[:, t:t + 1]).then_inc(done, 1)

                tokens_out([q_tok[:, 0, :], q_tok[:, 1, :]], [bank[4][:], bank[5][:]], 4, q_copied)
                split(n0 + 10)
                split(n0 + 11)
                tokens_out([q_tok[:, 2, :], q_tok[:, 3, :]], [bank[6][:], bank[7][:]], 8, q_copied)
                split(n0 + 12)
                split(n0 + 13)
                split(n0 + 14)
                act.wait_ge(w_used, n0 + 11)
                q_w = IH * ID
                for t in range(TT):
                    src, r = bank[t], r_col[:, t:t + 1]
                    nc.scalar.activation(idx_tok[:, t, 0:q_w + ID], src[:, 0:q_w + ID], ACT.Identity, scale=r)
                    nc.scalar.activation(idx_tok[:, t, q_w + ID:q_w + 2 * ID], src[:, q_w:q_w + ID], ACT.Identity, scale=r)
                    nc.scalar.activation(idx_w[:, t, :], src[:, q_w + ID:IDX_W], ACT.Identity,
                                         scale=r_col16[:, t:t + 1]).then_inc(idx_copied, 1)
                for a in range(2):
                    act.wait_ge(q_copied, 2 * a + 2)
                    nc.scalar.activation(qk_a[:, 2 * a:2 * a + 2, :], q_tok[:, 2 * a:2 * a + 2, :],
                                         ACT.Square).then_inc(qk_sq, 1)
                split(n0 + 15)
                split(n0 + 16)
                act.wait_ge(idx_T, 1)
                nc.scalar.activation(qiT[:].rearrange("p c s -> p (c s)"), bank[6][:], ACT.Copy).then_inc(idx_T_copied, 1)
                nc.scalar.activation(kiT[:], bank[7][:, 0:S], ACT.Copy).then_inc(idx_T_copied, 1)
                split(n0 + 17)
                act.wait_ge(qk_ms_done, 1)
                nc.scalar.activation(qk_root[:], qk_ms[:], ACT.Sqrt).then_inc(qk_root_done, 1)
                split(n0 + 18)
                tokens_out([u_tok[:, 0, :], u_tok[:, 1, :]], [bank[2][:], bank[3][:]], 15, u_copied)
                act.wait_ge(idx_dots, 1)
                for t in range(TT):
                    n = (t + 1) * P
                    for odd in range(2):
                        nc.scalar.activation(rel[:, t, odd::2, 0:n],
                                             bank[6 * t + odd][:, 0:2 * n].rearrange("p (h s) -> p h s", h=2),
                                             ACT.Relu).then_inc(rel_done, 1)
                split(n0 + 19)
                for g in range(4):
                    act.wait_ge(pool_mean, g // 2 + 1)
                    nc.scalar.activation(pool_in[:, g, :], bank[2 + g // 2][:, (g % 2) * S:(g % 2 + 1) * S],
                                         ACT.Copy).then_inc(pool_mean_copied, 1)
                split(n0 + 20)
                for g in range(4):
                    act.wait_ge(pool_out, g // 2 + 1)
                    nc.scalar.activation(mix_hi[:, PAIRS + g, :], bank[2 + g // 2][:, (g % 2) * S:(g % 2 + 1) * S],
                                         ACT.Identity, scale=cols[:, COLS["pool"] + g:COLS["pool"] + g + 1]
                                         ).then_inc(mix_hi_done, 1)
                split(n0 + 21)
                split(n0 + 22)
                tokens_out([v_tok[:, 0, 0:ATT], v_tok[:, 1, 0:ATT]], [bank[4][:], bank[5][:]], 19, v_copied)
                split(n0 + 23)
                split(n0 + 24)
                for b in range(4):
                    act.wait_ge(qk_T, b + 1)
                    nc.scalar.activation((qT, kT)[b // 2][:, 2 * (b % 2):2 * (b % 2) + 2, :],
                                         bank[(6, 7, 4, 5)[b]][:].rearrange("p (c s) -> p c s", c=2),
                                         ACT.Copy).then_inc(qk_T_copied, 1)

                def exp(s):
                    act.wait_ge(neg_done, s + 1)
                    if s >= 2:
                        act.wait_ge(probT_done, s - 1)
                    for t in range(TT):
                        n = (t + 1) * P
                        nc.scalar.activation(prob[:, s % 2, t, 0:n], logit[:, s % 2, t, 0:n], ACT.Exp,
                                             bias=neg1[:, s, t:t + 1],
                                             accum_out=psums[:, s, t:t + 1]).then_inc(exp_done, 1)

                for s in range(HEADS + 2):
                    if s >= 2:
                        hd = s - 2
                        lo = hd % 2 * HD
                        act.wait_ge(pv_done, hd + 1)
                        nc.scalar.activation(mix_hi[lo:lo + HD, hd // 2, :], bank[7][lo:lo + HD, 0:S],
                                             ACT.Copy).then_inc(mix_hi_done, 1)
                    if 1 <= s <= HEADS:
                        act.wait_ge(probT_done, s)
                        if s >= 3:
                            act.wait_ge(pv_done, s - 2)
                        nc.scalar.activation(probT[:, (s - 1) % 2, :], bank[6][:, 0:3 * P],
                                             ACT.Copy).then_inc(probT_copied, 1)
                    if s < HEADS:
                        exp(s)
                    if s in (2, 5):
                        split(n0 + 25 + (s - 2) // 3)
                split(n0 + 27)
                split(n0 + 28)

            def gated_mixer(n0, p):
                for b in range(3, 6):
                    split(n0 + b)
                rms_root(p)
                for b in range(6, 11):
                    split(n0 + b)
                act.wait_ge(r_col_done, 2)
                for g in range(2):
                    act.wait_ge(w_used, n0 + 4 * g + 4)
                    for t in range(TT):
                        nc.scalar.activation(v_tok[:, t, g * 512:(g + 1) * 512], bank[4 + 2 * g + t][:],
                                             ACT.Gelu_apprx_tanh, scale=r_col[:, t:t + 1]).then_inc(v_gelu, 1)
                act.wait_ge(v_gelu, 4)
                for t in range(TT):
                    nc.scalar.activation(qk_a[:, 2 * t:2 * t + 2, :].rearrange("p a c -> p (a c)"), v_tok[:, t, :],
                                         ACT.Square, accum_out=v_ss[:, 0, t:t + 1]).then_inc(v_sq, 1)
                with act.Fori(0, 2) as i:
                    for j in range(4):
                        b = n0 + 8 + 3 * j
                        split(b + 3, i, 12)
                        split(b + 4, i, 12)
                        split(b + 5, i, 12)
                        act.wait_ge(conv_done, 4 * i + (j + 1))
                        nc.scalar.activation(yb_hi[:, bass.ds(4 * i + j, 1), :], conv_y.unsqueeze(1),
                                             ACT.Copy).then_inc(yb_hi_done, 1)
                split(n0 + 35)
                act.wait_ge(v_ms_done, 1)
                nc.scalar.activation(v_ss[:, 2, :], v_ss[:, 1, :], ACT.Sqrt).then_inc(v_root_done, 1)
                for b in range(36, 40):
                    split(n0 + b)

                def u_gelus(m0):
                    for m in range(m0, m0 + 4):
                        act.wait_ge(u_scaled, m + 1)
                        nc.scalar.activation(u_s[:, m, :], u_s[:, m, :],
                                             ACT.Gelu_apprx_tanh).then_inc(u_gelu, 1)

                def ya_his(m0):
                    for m in range(m0, m0 + 4):
                        act.wait_ge(ya_done, m + 1)
                        nc.scalar.activation(ya_hi[:, m, :], ya[:, m % 2, :], ACT.Copy).then_inc(ya_hi_done, 1)

                u_gelus(0)
                split(n0 + 40)
                ya_his(0)
                split(n0 + 41)
                u_gelus(4)
                split(n0 + 42)
                ya_his(4)
                with act.Fori(0, 4) as i:
                    for j in range(2):
                        b = n0 + 40 + 4 * j
                        for c in range(3, 6):
                            split(b + c, i, 8)
                        act.wait_ge(gates_scaled, 2 * i + (j + 1))
                        nc.scalar.activation(sig, gates, ACT.Sigmoid).then_inc(sig_done, 1)
                        split(b + 6, i, 8)
                        act.wait_ge(merged_done, 2 * i + (j + 1))
                        nc.scalar.activation(mix_hi[:, bass.ds(2 * i + j, 1), :], merged.unsqueeze(1),
                                             ACT.Copy).then_inc(mix_hi_done, 1)
                for b in range(75, 82):
                    split(n0 + b)

            act.dma_start(cols[:], cols_in).then_inc(cols_loaded, 16)
            for c in range(4):
                act.dma_start(x[:, 2 * c:2 * c + 2, :], x_in[:, 2 * c:2 * c + 2, :]).then_inc(x_loaded[c], 16)
            split(0)
            split(1)
            act.wait_ge(cols_loaded, 16)
            phase_input(0)
            ffn(0, START[0], 0)
            phase_input(1)
            attention_mixer(START[1], 1)
            phase_input(2)
            ffn(1, START[2], 2)
            phase_input(3)
            ffn(2, START[3], 3)
            phase_input(4)
            gated_mixer(START[4], 4)
            phase_input(5)
            ffn(3, START[5], 5)
            phase_input(6)
            rms_root(6)

        @block.vector
        def _(dve):
            steps = [0]

            def step(ins):
                steps[0] += 1
                ins.then_inc(dve_step, 1)
                dve.wait_ge(dve_step, steps[0])

            def split(n, i=0, per=0):
                if n >= BLOCKS:
                    return
                slot = n % RING
                dve.wait_ge(w_hi_done, n + 1 + per * i)
                nc.vector.tensor_tensor(w_lo[:, slot, :], w_raw[:, slot, :], w_hi[:, slot, :].bitcast(F32),
                                        ALU.subtract).then_inc(w_split, 1)

            def input_lo(p, k):
                g = COLS[PHASE_GAIN[p]]
                dve.wait_ge(x_hi_done, 8 * p + k + 1)
                nc.vector.scalar_tensor_tensor(x_lo[:, k, :], x[:, k, :], cols[:, g + k:g + k + 1],
                                               x_hi[:, k, :].bitcast(F32), ALU.mult, ALU.subtract).then_inc(x_split, 1)

            def residual(p, factor):
                for c in range(4):
                    if c < 3:
                        dve.wait_ge(acc_done, 3 * p + c + 1)
                    else:
                        dve.wait_ge(w_used, START[p + 1])
                    two = x[:, 2 * c:2 * c + 2, :].rearrange("p a s -> p (a s)")
                    nc.vector.scalar_tensor_tensor(two, bank[c][:], factor, two, ALU.mult, ALU.add).then_inc(x_new, 1)
                    if c and p < 5:
                        input_lo(p + 1, 2 * c - 2)
                        input_lo(p + 1, 2 * c - 1)
                if p < 5:
                    input_lo(p + 1, KC - 2)
                    input_lo(p + 1, KC - 1)

            def inv_root(ms_ap, root_ap, nt, r):
                step(nc.vector.reciprocal(r, root_ap))
                step(nc.vector.scalar_tensor_tensor(nt, ms_ap, -0.5, r, ALU.mult, ALU.mult))
                step(nc.vector.tensor_tensor(nt, nt, r, ALU.mult))
                return nc.vector.scalar_tensor_tensor(r, nt, 1.5, r, ALU.add, ALU.mult)

            def rms(p):
                dve.wait_ge(sumsq_done, p + 1)
                nc.vector.tensor_scalar(ms[:], bank[STAT[p]][:, 0:S], 1.0 / D, EPS, ALU.mult, ALU.add).then_inc(ms_done, 1)
                dve.wait_ge(root_done, p + 1)
                inv_root(ms[:], root[:], newton[:], rstd[:]).then_inc(rstd_done, 1)
                dve.wait_ge(rstd_done, p + 1)

            def token_scales(n):
                dve.wait_ge(rT_done, n)
                for t in range(TT):
                    last = nc.vector.tensor_copy(r_col[:, t:t + 1], bank[2][:, t * P:t * P + 1])
                    step(last)
                nc.vector.tensor_scalar(r_col16[:], r_col[:], IH ** -0.5 * ID ** -0.5, None,
                                        ALU.mult).then_inc(r_col_done, 1)

            def ffn(e, n0, p):
                for b in range(2, 6):
                    split(n0 + b)
                rms(p)

                def scale(f, slot, used):
                    dve.wait_ge(w_used, used)
                    nc.vector.tensor_tensor(gate_s, bank[4 + slot][:, 0:S], rstd[:], ALU.mult).then_inc(gate_scaled, 1)
                    nc.vector.tensor_tensor(up_s, bank[4 + slot][:, S:2 * S], rstd[:], ALU.mult).then_inc(up_scaled, 1)

                def product(f):
                    dve.wait_ge(up_scaled, FC * e + 1 + f)
                    dve.wait_ge(silu_done, FC * e + 1 + f)
                    nc.vector.tensor_tensor(hid, silu, up_s, ALU.mult).then_inc(hid_done, 1)

                def hidden_lo(f, slot):
                    dve.wait_ge(hid_hi_done, FC * e + 1 + f)
                    nc.vector.tensor_tensor(hid_lo[:, slot, :], hid, hid_hi[:, slot, :].bitcast(F32),
                                            ALU.subtract).then_inc(hid_split, 1)

                for f in range(3):
                    scale(f, f, n0 + 2 * f + 2)
                    split(n0 + 6 + 2 * f)
                    product(f)
                    split(n0 + 7 + 2 * f)
                    hidden_lo(f, f)

                def chunk(f, j, i=0):
                    b = n0 + 10 + 3 * (f - 4)
                    split(b + 2, i, 12)
                    scale(4 * i + (f - 1), (j - 1) % 4, 12 * i + (b - 1))
                    product(4 * i + (f - 1))
                    hidden_lo(4 * i + (f - 1), (j - 1) % 4)
                    split(b + 3, i, 12)
                    split(b + 4, i, 12)

                with dve.Fori(0, LOOPED // 4) as i:
                    for j in range(4):
                        chunk(4 + j, j, i)
                for f in range(4 + LOOPED, FC):
                    chunk(f, f % 4)
                scale(FC - 1, (FC - 1) % 4, n0 + FFN_B - 3)
                split(n0 + FFN_B)
                product(FC - 1)
                hidden_lo(FC - 1, (FC - 1) % 4)
                split(n0 + FFN_B + 1)
                residual(p, 0.5)

            def attention_mixer(n0, p):
                for b in range(2, 6):
                    split(n0 + b)
                rms(p)
                for b in range(6, 10):
                    split(n0 + b)
                token_scales(1)
                for b in range(10, 15):
                    split(n0 + b)
                dve.wait_ge(idx_copied, 2)
                heads = idx_tok[:].rearrange("p t (h d) -> p t h d", d=ID)
                h = IROT // 2
                x1, x2 = heads[:, :, :, 0:h], heads[:, :, :, h:IROT]
                shape = [P, TT, IH + 2, h]
                cos = const[:, C_ICOS:C_ICOS + TT * h].rearrange("p (t d) -> p t d", t=TT).unsqueeze(2).to_broadcast(shape)
                sin = const[:, C_ISIN:C_ISIN + TT * h].rearrange("p (t d) -> p t d", t=TT).unsqueeze(2).to_broadcast(shape)
                t1, t2, t3, t4 = (idx_t[:, n] for n in range(4))
                nc.vector.tensor_tensor(t1, x1, cos, ALU.mult)
                nc.vector.tensor_tensor(t2, x2, sin, ALU.mult)
                nc.vector.tensor_tensor(t3, x2, cos, ALU.mult)
                step(nc.vector.tensor_tensor(t4, x1, sin, ALU.mult))
                nc.vector.tensor_tensor(x1, t1, t2, ALU.subtract).then_inc(idx_roped, 1)
                nc.vector.tensor_tensor(x2, t3, t4, ALU.add).then_inc(idx_roped, 1)
                split(n0 + 15)
                split(n0 + 16)
                for a in range(2):
                    dve.wait_ge(qk_sq, a + 1)
                    step(nc.vector.tensor_reduce(qk_ss[:, 16 * a:16 * a + 16],
                                                 qk_a[:, 2 * a:2 * a + 2, :].rearrange("p t (h d) -> p (t h) d", d=HD),
                                                 AX.X, ALU.add))
                nc.vector.tensor_scalar(qk_ms[:], qk_ss[:], 1.0 / HD, EPS, ALU.mult, ALU.add).then_inc(qk_ms_done, 1)
                split(n0 + 17)
                dve.wait_ge(qk_root_done, 1)
                step(inv_root(qk_ms[:], qk_root[:], qk_nt[:], qk_r[:]))
                for a in range(2):
                    heads = q_tok[:, 2 * a:2 * a + 2, :].rearrange("p t (h d) -> p (t h) d", d=HD)
                    nc.vector.tensor_tensor(heads, heads, qk_r[:, 16 * a:16 * a + 16].unsqueeze(2).to_broadcast([P, 16, HD]),
                                            ALU.mult).then_inc(qk_normed, 1)
                split(n0 + 18)
                for t in range(TT):
                    n = (t + 1) * P
                    dve.wait_ge(rel_done, 2 * t + 2)
                    dst = score[:, t, 0:n]
                    step(nc.vector.tensor_scalar(dst, rel[:, t, 0, 0:n], idx_w[:, t, 0:1], None, ALU.mult))
                    for hd in range(1, IH):
                        last = nc.vector.scalar_tensor_tensor(dst, rel[:, t, hd, 0:n], idx_w[:, t, hd:hd + 1], dst,
                                                              ALU.mult, ALU.add)
                        if hd < IH - 1:
                            step(last)
                    last.then_inc(score_done, 1)
                split(n0 + 19)
                dve.wait_ge(tables_made, 4)
                for a in range(2):
                    dve.wait_ge(qk_normed, a + 1)
                    for t in range(TT):
                        nc.vector.tensor_tensor(
                            qk_a[:, 2 * a + t, :].rearrange("p (h d) -> p h d", d=HD),
                            q_tok[:, 2 * a + t, :].rearrange("p (h d) -> p h d", d=HD),
                            rope_c[:, a, t, :].unsqueeze(1).to_broadcast([P, HEADS, HD]), ALU.mult).then_inc(qk_cos, 1)
                split(n0 + 20)
                for g in range(4):
                    dve.wait_ge(mix_hi_done, 2 * (g // 2) + 2)
                    nc.vector.scalar_tensor_tensor(mix_lo[:, PAIRS + g, :],
                                                   bank[2 + g // 2][:, (g % 2) * S:(g % 2 + 1) * S],
                                                   cols[:, COLS["pool"] + g:COLS["pool"] + g + 1],
                                                   mix_hi[:, PAIRS + g, :].bitcast(F32), ALU.mult,
                                                   ALU.subtract).then_inc(mix_split, 1)
                split(n0 + 21)

                def roped(a):
                    dve.wait_ge(qk_sin, 4 * (a + 1))
                    dve.wait_ge(qk_cos, 2 * (a + 1))
                    nc.vector.tensor_tensor(qk_b[:, 2 * a:2 * a + 2, :], qk_b[:, 2 * a:2 * a + 2, :],
                                            qk_a[:, 2 * a:2 * a + 2, :], ALU.add).then_inc(qk_roped, 1)

                roped(0)
                dve.wait_ge(score_masked, 2)
                for r in range(TOPK // 8):
                    for t in range(TT):
                        last = nc.vector.max(top8[:, t, :], work[:, t, 0:(t + 1) * P])
                    step(last)
                    for t in range(TT):
                        last = nc.vector.match_replace(work[:, t, 0:(t + 1) * P], top8[:, t, :],
                                                       work[:, t, 0:(t + 1) * P], UNSEL)
                    step(last)
                    if r == 3:
                        split(n0 + 22)
                        roped(1)
                for t in range(TT):
                    nc.vector.tensor_scalar(score[:, t, 0:(t + 1) * P], work[:, t, 0:(t + 1) * P], UNSEL, MASKED,
                                            ALU.not_equal, ALU.mult).then_inc(sel_done, 1)
                split(n0 + 23)
                split(n0 + 24)
                dve.wait_ge(bias_done, 2)
                for s in range(HEADS + 2):
                    if 1 <= s <= HEADS:
                        hd = s - 1
                        dve.wait_ge(exp_done, 2 * hd + 2)
                        step(nc.vector.reciprocal(rsum[:, hd, :], psums[:, hd, :]))
                        for t in range(TT):
                            n = (t + 1) * P
                            nc.vector.tensor_scalar(prob[:, hd % 2, t, 0:n], prob[:, hd % 2, t, 0:n],
                                                    rsum[:, hd, t:t + 1], None, ALU.mult).then_inc(prob_done, 1)
                    if s < HEADS:
                        dve.wait_ge(logits_done, s + 1)
                        for t in range(TT):
                            n = (t + 1) * P
                            nc.vector.tensor_tensor_reduce(logit[:, s % 2, t, 0:n], bank[4 + s % 2][:, t * P:t * P + n],
                                                           bias[:, t, 0:n], HD ** -0.5, MASKED, ALU.add, ALU.max,
                                                           top1[:, s, t:t + 1]).then_inc(logits_read, 1)
                        dve.wait_ge(logits_read, 2 * s + 2)
                        nc.vector.tensor_scalar(neg1[:, s, :], top1[:, s, :], -1.0, None, ALU.mult).then_inc(neg_done, 1)
                    if s >= 2:
                        hd = s - 2
                        lo = hd % 2 * HD
                        dve.wait_ge(mix_hi_done, 4 + hd + 1)
                        nc.vector.tensor_tensor(mix_lo[lo:lo + HD, hd // 2, :], bank[7][lo:lo + HD, 0:S],
                                                mix_hi[lo:lo + HD, hd // 2, :].bitcast(F32),
                                                ALU.subtract).then_inc(mix_split, 1)
                    if s in (2, 5):
                        split(n0 + 25 + (s - 2) // 3)
                split(n0 + 27)
                split(n0 + 28)
                residual(p, 1.0)

            def gated_mixer(n0, p):
                for b in range(2, 6):
                    split(n0 + b)
                rms(p)
                for b in range(6, 10):
                    split(n0 + b)
                token_scales(2)
                split(n0 + 10)
                step(nc.vector.tensor_tensor(rstd_sq[:], rstd[:], rstd[:], ALU.mult))
                with dve.Fori(0, 2) as i:
                    for j in range(4):
                        b = n0 + 8 + 3 * j
                        m = 4 * i + j
                        split(b + 3, i, 12)
                        split(b + 4, i, 12)
                        dve.wait_ge(w_used, 12 * i + (b + 3))
                        pair, single = bank[4 + 2 * (j % 2)], bank[5 + 2 * (j % 2)]
                        nc.vector.tensor_tensor(gc_s, pair[:, 0:S], rstd_sq[:], ALU.mult).then_inc(gc_scaled, 1)
                        nc.vector.tensor_tensor(gb_s, single[:, 0:S], rstd[:], ALU.mult)
                        dve.wait_ge(gc_scaled, m + 1)
                        nc.vector.tensor_tensor(conv_in[:, 1:S + 1], pair[:, S:2 * S], gc_s, ALU.mult).then_inc(conv_read, 1)

                        def tap(k):
                            return cols[:, bass.ds(m + (COLS["conv"] + k * KC), 1)]

                        dve.wait_ge(conv_read, m + 1)
                        nc.vector.tensor_scalar(conv_a, conv_in[:, 0:S], tap(0), None, ALU.mult).then_inc(conv_mid, 1)
                        for k in (1, 2):
                            dve.wait_ge(conv_mid, 3 * m + k)
                            nc.vector.scalar_tensor_tensor(conv_a, conv_in[:, k:S + k], tap(k), conv_a, ALU.mult,
                                                           ALU.add).then_inc(conv_mid, 1)
                        dve.wait_ge(conv_mid, 3 * m + 3)
                        nc.vector.tensor_tensor(conv_y, conv_a, gb_s, ALU.mult).then_inc(conv_done, 1)
                        split(b + 5, i, 12)
                        dve.wait_ge(yb_hi_done, m + 1)
                        nc.vector.tensor_tensor(yb_lo[:, bass.ds(m, 1), :], conv_y.unsqueeze(1),
                                                yb_hi[:, bass.ds(m, 1), :].bitcast(F32), ALU.subtract).then_inc(yb_split, 1)
                split(n0 + 35)
                dve.wait_ge(v_sq, 2)
                nc.vector.tensor_scalar(v_ss[:, 1, :], v_ss[:, 0, :], 1.0 / D, EPS, ALU.mult, ALU.add).then_inc(v_ms_done, 1)
                dve.wait_ge(v_root_done, 1)
                step(inv_root(v_ss[:, 1, :], v_ss[:, 2, :], v_ss[:, 3, :], v_ss[:, 4, :]))
                for t in range(TT):
                    nc.vector.tensor_scalar(v_tok[:, t, :], v_tok[:, t, :], v_ss[:, 4, t:t + 1], None,
                                            ALU.mult).then_inc(v_normed, 1)
                for b in range(36, 40):
                    split(n0 + b)

                def u_scales(m0):
                    for m in range(m0, m0 + 4):
                        dve.wait_ge(w_used, n0 + 32 + m + 1)
                        nc.vector.tensor_tensor(u_s[:, m, :], bank[4 + m % 4][:, 0:S], rstd[:],
                                                ALU.mult).then_inc(u_scaled, 1)

                def u_gates(m0):
                    def lo(m):
                        dve.wait_ge(ya_hi_done, m + 1)
                        nc.vector.tensor_tensor(ya_lo[:, m, :], ya[:, m % 2, :], ya_hi[:, m, :].bitcast(F32),
                                                ALU.subtract).then_inc(ya_split, 1)

                    for m in range(m0, m0 + 4):
                        dve.wait_ge(u_gelu, m + 1)
                        dve.wait_ge(sg_done, m + 1)
                        if m >= 2:
                            dve.wait_ge(ya_split, m - 1)
                        nc.vector.tensor_tensor(ya[:, m % 2, :], u_s[:, m, :], sg[:, m, :], ALU.mult).then_inc(ya_done, 1)
                        if m > m0:
                            lo(m - 1)
                    lo(m0 + 3)

                u_scales(0)
                dve.wait_ge(spatial_done, 1)
                dve.wait_ge(rows_loaded, 16)
                for m in range(KC):
                    nc.vector.scalar_tensor_tensor(
                        sg[:, m, :].rearrange("p (c q) -> p c q", c=TT),
                        acc(m).rearrange("p (c q) -> p c q", c=TT), cols[:, COLS["sgu"] + m:COLS["sgu"] + m + 1],
                        rows[:, 2 * HD + m * P:2 * HD + (m + 1) * P].unsqueeze(1).to_broadcast([P, TT, P]),
                        ALU.mult, ALU.add).then_inc(sg_done, 1)
                split(n0 + 40)
                u_gates(0)
                split(n0 + 41)
                u_scales(4)
                split(n0 + 42)
                u_gates(4)
                with dve.Fori(0, 4) as i:
                    for j in range(2):
                        b = n0 + 40 + 4 * j
                        m = 2 * i + j
                        for c in range(3, 6):
                            split(b + c, i, 8)
                        dve.wait_ge(w_used, 8 * i + (b + 2))
                        nc.vector.tensor_tensor(gates.rearrange("p (g s) -> p g s", g=2),
                                                bank[4 + 2 * j][:].rearrange("p (g s) -> p g s", g=2),
                                                rstd[:].unsqueeze(1).to_broadcast([P, 2, S]), ALU.mult).then_inc(gates_scaled, 1)
                        split(b + 6, i, 8)
                        dve.wait_ge(w_used, 8 * i + (b + 4))
                        dve.wait_ge(sig_done, m + 1)
                        nc.vector.tensor_tensor(branch, bank[5 + 2 * j][:], sig, ALU.mult).then_inc(branch_done, 1)
                        dve.wait_ge(branch_done, m + 1)
                        nc.vector.tensor_tensor(merged, branch[:, 0:S], branch[:, S:2 * S], ALU.add).then_inc(merged_done, 1)
                        dve.wait_ge(mix_hi_done, m + (4 + HEADS + 1))
                        nc.vector.tensor_tensor(mix_lo[:, bass.ds(m, 1), :], merged.unsqueeze(1),
                                                mix_hi[:, bass.ds(m, 1), :].bitcast(F32), ALU.subtract).then_inc(mix_split, 1)
                for b in range(75, 82):
                    split(n0 + b)
                residual(p, 1.0)

            split(0)
            split(1)
            for k in range(KC):
                input_lo(0, k)
            ffn(0, START[0], 0)
            attention_mixer(START[1], 1)
            ffn(1, START[2], 2)
            ffn(2, START[3], 3)
            gated_mixer(START[4], 4)
            ffn(3, START[5], 5)
            rms(6)
            for k in range(KC):
                g = COLS["final"] + k
                nc.vector.scalar_tensor_tensor(x_sq[:, k, :], x[:, k, :], cols[:, g:g + 1], rstd[:], ALU.mult,
                                               ALU.mult).then_inc(out_ready, 1)

        @block.tensor
        def _(pe):
            def three(dst, a_hi, a_lo, b_hi, b_lo, first, last):
                nc.tensor.matmul(dst, a_hi, b_hi, start=first, stop=False, skip_group_check=True)
                nc.tensor.matmul(dst, a_hi, b_lo, start=False, stop=False, skip_group_check=True)
                return nc.tensor.matmul(dst, a_lo, b_hi, start=False, stop=last, skip_group_check=True)

            def feature_block(n, dst, b_hi, b_lo, i=0, per=0, p=None, ready=None):
                slot = n % RING
                pe.wait_ge(w_split, n + 1 + per * i)
                for k in range(KC):
                    if p is not None:
                        pe.wait_ge(x_split, 8 * p + k + 1)
                    if ready is not None:
                        pe.wait_ge(ready, k + 1)
                    w = slice(k * P, (k + 1) * P)
                    last = three(dst, w_hi[:, slot, w], w_lo[:, slot, w], b_hi[:, k, :], b_lo[:, k, :], k == 0, k == KC - 1)
                last.then_inc(w_used, 1)

            def token_block(n, b, per_block, width, dst, p=None):
                slot = n % RING
                pe.wait_ge(w_split, n + 1)
                for kk in range(min(per_block, KC - b * per_block)):
                    k = b * per_block + kk
                    if p is not None:
                        pe.wait_ge(x_split, 8 * p + k + 1)
                    for t in range(TT):
                        tok, w = slice(t * P, (t + 1) * P), slice(kk * width, (kk + 1) * width)
                        last = three(dst[t][:, 0:width], x_hi[:, k, tok], x_lo[:, k, tok], w_hi[:, slot, w],
                                     w_lo[:, slot, w], k == 0, k == KC - 1)
                last.then_inc(w_used, 1)

            def chunk_block(n, b_hi, b_lo, i=0, per=0, first=False):
                slot = n % RING
                pe.wait_ge(w_split, n + 1 + per * i)
                for m in range(KC):
                    w = slice(m * P, (m + 1) * P)
                    last = three(acc(m), w_hi[:, slot, w], w_lo[:, slot, w], b_hi, b_lo, first and m % 2 == 0, False)
                last.then_inc(w_used, 1)

            def last_chunk(n, b_hi, b_lo):
                slot = n % RING
                pe.wait_ge(w_split, n + 1)
                for m in range(KC):
                    w = slice(m * P, (m + 1) * P)
                    last = three(acc(m), w_hi[:, slot, w], w_lo[:, slot, w], b_hi, b_lo, False, True)
                    if m % 2 and m < KC - 1:
                        last.then_inc(acc_done, 1)
                last.then_inc(w_used, 1)

            def sum_squares(p):
                pe.wait_ge(x_sq_added, 3 * p + 3)
                for k in range(2):
                    last = nc.tensor.matmul(bank[STAT[p]][:, 0:S], ones[:], x_sq[:, k, :], start=(k == 0), stop=(k == 1),
                                            skip_group_check=True)
                last.then_inc(sumsq_done, 1)

            def token_scales(p):
                pe.wait_ge(rstd_done, p + 1)
                for t in range(TT):
                    last = nc.tensor.transpose(bank[2][:, t * P:(t + 1) * P], rstd[:, t * P:(t + 1) * P], ident)
                last.then_inc(rT_done, 1)

            def ffn(e, n0, p):
                pe.wait_ge(w_split, n0 + 2)
                for k in range(KC):
                    pe.wait_ge(x_split, 8 * p + k + 1)
                    w = slice(k * P, (k + 1) * P)
                    for c in range(2):
                        slot = (n0 + c) % RING
                        last = three(bank[4][:, c * S:(c + 1) * S], w_hi[:, slot, w], w_lo[:, slot, w], x_hi[:, k, :],
                                     x_lo[:, k, :], k == 0 and c == 0, k == KC - 1)
                        if k == KC - 1:
                            last.then_inc(w_used, 1)
                feature_block(n0 + 2, bank[5][:, 0:S], x_hi, x_lo)
                sum_squares(p)
                feature_block(n0 + 3, bank[5][:, S:2 * S], x_hi, x_lo)
                for b in range(4, 8):
                    feature_block(n0 + b, bank[4 + b // 2][:, b % 2 * S:(b % 2 + 1) * S], x_hi, x_lo)
                for f in range(2):
                    pe.wait_ge(hid_split, FC * e + f + 1)
                    chunk_block(n0 + 8 + f, hid_hi[:, f, :], hid_lo[:, f, :], first=(f == 0))

                def chunk(f, j, i=0):
                    b = n0 + 10 + 3 * (f - 4)
                    g = bank[4 + j]
                    feature_block(b, g[:, 0:S], x_hi, x_lo, i, 12)
                    feature_block(b + 1, g[:, S:2 * S], x_hi, x_lo, i, 12)
                    pe.wait_ge(hid_split, 4 * i + (FC * e + f - 1))
                    chunk_block(b + 2, hid_hi[:, (j - 2) % 4, :], hid_lo[:, (j - 2) % 4, :], i, 12)

                with pe.Fori(0, LOOPED // 4) as i:
                    for j in range(4):
                        chunk(4 + j, j, i)
                for f in range(4 + LOOPED, FC):
                    chunk(f, f % 4)
                pe.wait_ge(hid_split, FC * (e + 1) - 1)
                f = (FC - 2) % 4
                chunk_block(n0 + 64, hid_hi[:, f, :], hid_lo[:, f, :])
                pe.wait_ge(hid_split, FC * (e + 1))
                last_chunk(n0 + 65, hid_hi[:, f + 1, :], hid_lo[:, f + 1, :])

            def attention_mixer(n0, p):
                for b in range(4):
                    token_block(n0 + b, b, TOK_K, 512, (bank[4], bank[5]), p)
                sum_squares(p)
                for b in range(4):
                    if b == 2:
                        token_scales(p)
                    token_block(n0 + 4 + b, b, TOK_K, 512, (bank[6], bank[7]))
                for b in range(IDX_B):
                    token_block(n0 + 8 + b, b, IDX_K, IDX_W, (bank[0], bank[1]))
                pe.wait_ge(r_col_done, 1)
                for b in range(2):
                    token_block(n0 + 11 + b, b, TOK_K, 512, (bank[2], bank[3]))
                pe.wait_ge(idx_roped, 2)
                pe.wait_ge(q_copied, 4)
                for c in range(3):
                    for t in range(TT):
                        dst = bank[6 + c // 2][:, (c % 2) * S + t * P:(c % 2) * S + (t + 1) * P]
                        last = nc.tensor.transpose(dst, idx_tok[:, t, c * P:(c + 1) * P], ident)
                last.then_inc(idx_T, 1)
                for b in range(2, 4):
                    token_block(n0 + 11 + b, b, TOK_K, 512, (bank[2], bank[3]))
                pe.wait_ge(idx_T_copied, 2)
                for t in range(TT):
                    for hd in range(IH):
                        rows_ = slice(hd % 2 * ID, hd % 2 * ID + ID)
                        n = (t + 1) * P
                        dst = bank[6 * t + hd % 2][:, hd // 2 * n:(hd // 2 + 1) * n]
                        last = nc.tensor.matmul(dst, qiT[rows_, hd // 2, t * P:(t + 1) * P], kiT[rows_, 0:n], start=True,
                                                stop=True, skip_group_check=True)
                last.then_inc(idx_dots, 1)
                token_block(n0 + 15, 0, TOK_K, 512, (bank[4], bank[5]))
                band = const[:, C_BAND:].rearrange("p (t g s) -> p t g s", t=TT, g=4)
                pe.wait_ge(u_copied, 2)
                for g in range(4):
                    for t in range(TT):
                        last = nc.tensor.matmul(bank[2 + g // 2][:, (g % 2) * S + t * P:(g % 2 + 1) * S],
                                                u_tok[:, t, g * P:(g + 1) * P], band[:, t, g, t * P:S], start=(t == 0),
                                                stop=(t == TT - 1), skip_group_check=True)
                    if g % 2:
                        last.then_inc(pool_mean, 1)
                token_block(n0 + 16, 1, TOK_K, 512, (bank[4], bank[5]))
                pe.wait_ge(pool_loaded, 16)
                for g in range(4):
                    pe.wait_ge(pool_mean_copied, 2 * (g // 2) + 2)
                    last = nc.tensor.matmul(bank[2 + g // 2][:, (g % 2) * S:(g % 2 + 1) * S], pool_w[:, g, :],
                                            pool_in[:, g, :], start=True, stop=True, skip_group_check=True)
                    if g % 2:
                        last.then_inc(pool_out, 1)
                for b in range(2, 4):
                    token_block(n0 + 15 + b, b, TOK_K, 512, (bank[4], bank[5]))
                pe.wait_ge(mix_split, 4)
                pe.wait_ge(rel_done, 4)

                def pooled(g):
                    chunk_block(n0 + 19 + g, mix_hi[:, PAIRS + g, :], mix_lo[:, PAIRS + g, :], first=(g == 0))

                pooled(0)
                for a in range(2):
                    pe.wait_ge(qk_roped, a + 1)
                    if a:
                        pe.wait_ge(v_copied, 2)
                    for c in range(PAIRS):
                        for t in range(TT):
                            dst = bank[(6, 7, 4, 5)[2 * a + c // 2]][:, (c % 2) * S + t * P:(c % 2) * S + (t + 1) * P]
                            last = nc.tensor.transpose(dst, qk_b[:, 2 * a + t, c * P:(c + 1) * P], ident)
                        if c % 2:
                            last.then_inc(qk_T, 1)
                    pooled(1 + a)
                pe.wait_ge(qk_T_copied, 4)

                def logits(s):
                    rows_ = slice(s % 2 * HD, s % 2 * HD + HD)
                    if s >= 2:
                        pe.wait_ge(logits_read, 2 * (s - 1))
                    for t in range(TT):
                        n = (t + 1) * P
                        last = nc.tensor.matmul(bank[4 + s % 2][:, t * P:t * P + n], qT[rows_, s // 2, t * P:(t + 1) * P],
                                                kT[rows_, s // 2, 0:n], start=True, stop=True, skip_group_check=True)
                    last.then_inc(logits_done, 1)

                logits(0)
                for s in range(HEADS + 2):
                    if s + 1 < HEADS:
                        logits(s + 1)
                    if s == 0:
                        pooled(3)
                    if s >= 2:
                        hd = s - 2
                        pe.wait_ge(probT_copied, hd + 1)
                        if hd:
                            pe.wait_ge(mix_split, 4 + hd)
                        pair = slice(hd // 2 * P, (hd // 2 + 1) * P)
                        nc.tensor.matmul(bank[7][:, 0:S], v_tok[:, 0, pair], probT[:, hd % 2, 0:S], start=True, stop=False,
                                         skip_group_check=True)
                        nc.tensor.matmul(bank[7][:, P:S], v_tok[:, 1, pair], probT[:, hd % 2, S:S + P], start=False,
                                         stop=True, skip_group_check=True).then_inc(pv_done, 1)
                    if 1 <= s <= HEADS:
                        hd = s - 1
                        pe.wait_ge(prob_done, 2 * s)
                        if hd:
                            pe.wait_ge(probT_copied, hd)
                        for n, (t, kt) in enumerate(((0, 0), (1, 0), (1, 1))):
                            last = nc.tensor.transpose(bank[6][:, n * P:(n + 1) * P],
                                                       prob[:, hd % 2, t, kt * P:(kt + 1) * P], ident)
                        last.then_inc(probT_done, 1)
                    if s in (5, 7, 9):
                        c = (s - 5) // 2
                        pe.wait_ge(mix_split, 4 + 2 * c + 2)
                        chunk_block(n0 + 23 + c, mix_hi[:, c, :], mix_lo[:, c, :])
                pe.wait_ge(mix_split, 4 + HEADS)
                last_chunk(n0 + 26, mix_hi[:, 3, :], mix_lo[:, 3, :])

            def gated_mixer(n0, p):
                for b in range(4):
                    token_block(n0 + b, b, TOK_K, 512, (bank[4], bank[5]), p)
                sum_squares(p)
                for b in range(4):
                    if b == 2:
                        token_scales(p)
                    token_block(n0 + 4 + b, b, TOK_K, 512, (bank[6], bank[7]))
                pe.wait_ge(v_gelu, 2)
                with pe.Fori(0, 2) as i:
                    for j in range(4):
                        b = n0 + 8 + 3 * j
                        pair, single = bank[4 + 2 * (j % 2)], bank[5 + 2 * (j % 2)]
                        if j == 1:
                            pe.wait_ge(v_gelu, 4)
                        feature_block(b, pair[:, 0:S], x_hi, x_lo, i, 12)
                        feature_block(b + 1, pair[:, S:2 * S], x_hi, x_lo, i, 12)
                        feature_block(b + 2, single[:, 0:S], x_hi, x_lo, i, 12)
                for m in range(4):
                    if m == 2:
                        pe.wait_ge(conv_read, KC)
                    feature_block(n0 + 32 + m, bank[4 + m][:, 0:S], x_hi, x_lo)
                pe.wait_ge(v_normed, 2)
                pe.wait_ge(sgu_loaded, 16)
                for m in range(KC):
                    for t in range(TT):
                        last = nc.tensor.matmul(acc(m)[:, t * P:(t + 1) * P], v_tok[:, t, m * P:(m + 1) * P], sgu_w[:, m, :],
                                                start=True, stop=True, skip_group_check=True)
                last.then_inc(spatial_done, 1)
                for m in range(4, KC):
                    pe.wait_ge(u_scaled, m - 3)
                    feature_block(n0 + 32 + m, bank[m][:, 0:S], x_hi, x_lo)
                pe.wait_ge(u_scaled, KC)
                with pe.Fori(0, 4) as i:
                    for j in range(2):
                        b = n0 + 40 + 4 * j
                        g, y = bank[4 + 2 * j], bank[5 + 2 * j]
                        feature_block(b, g[:, 0:S], x_hi, x_lo, i, 8)
                        feature_block(b + 1, g[:, S:2 * S], x_hi, x_lo, i, 8)
                        pe.wait_ge(ya_split, KC)
                        feature_block(b + 2, y[:, 0:S], ya_hi, ya_lo, i, 8)
                        pe.wait_ge(yb_split, KC)
                        feature_block(b + 3, y[:, S:2 * S], yb_hi, yb_lo, i, 8)
                base = 4 + HEADS
                pe.wait_ge(sg_done, KC)
                for c in range(KC - 1):
                    pe.wait_ge(mix_split, base + c + 1)
                    chunk_block(n0 + 72 + c, mix_hi[:, c, :], mix_lo[:, c, :], first=(c == 0))
                pe.wait_ge(mix_split, base + KC)
                last_chunk(n0 + 79, mix_hi[:, KC - 1, :], mix_lo[:, KC - 1, :])

            pe.wait_ge(filled, 1)
            for _ in range(WARM):
                nc.tensor.matmul(bank[7][:], zeros[:, 0:P], zeros[:], start=True, stop=True, skip_group_check=True)
            pe.wait_ge(filled, 3)
            ffn(0, START[0], 0)
            attention_mixer(START[1], 1)
            ffn(1, START[2], 2)
            ffn(2, START[3], 3)
            gated_mixer(START[4], 4)
            ffn(3, START[5], 5)
            for k in range(KC):
                pe.wait_ge(x_sq_done, 24 + k // 2 + 1)
                last = nc.tensor.matmul(bank[4][:, 0:S], ones[:], x_sq[:, k, :], start=(k == 0), stop=(k == KC - 1),
                                        skip_group_check=True)
            last.then_inc(sumsq_done, 1)


STAT = [0, 3, 0, 0, 3, 0, 4]
WARM = 20


def _cols(a):
    return np.asarray(a, np.float32).reshape(-1, P).T


def _features(w):
    return w.reshape(KC, P, -1, P).transpose(2, 1, 0, 3).reshape(-1, P, BW)


def _tokens(w, per_block):
    width = w.shape[1]
    n = -(-KC // per_block)
    out = np.zeros((n, P, BW), np.float32)
    for k in range(KC):
        b, j = divmod(k, per_block)
        out[b, :, j * width:(j + 1) * width] = w[k * P:(k + 1) * P]
    return out


def _chunks(w):
    return w.reshape(-1, P, BW)


def _ffn(gate, up, down):
    g, u, d = _features(gate), _features(up), _chunks(down)
    out = [w[f] for f in range(4) for w in (g, u)] + [d[0], d[1]]
    for f in range(4, FC):
        out += [g[f], u[f], d[f - 2]]
    return np.stack(out + [d[FC - 2], d[FC - 1]])


def _constants():
    c = np.zeros((P, NCONST), np.float32)
    pos = np.arange(S, dtype=np.float32)

    def tables(half):
        inv = np.float32(THETA) ** (-np.arange(half, dtype=np.float32) / np.float32(half))
        ang = pos[:, None] * inv[None, :]
        return np.cos(ang), np.sin(ang)

    cos, sin = tables(HD // 2)
    c[:, C_COS:C_COS + P] = np.concatenate([cos, cos], 1).reshape(TT, P, HD).transpose(1, 0, 2).reshape(P, -1)
    c[:, C_SIN:C_SIN + P] = np.concatenate([-sin, sin], 1).reshape(TT, P, HD).transpose(1, 0, 2).reshape(P, -1)
    cos, sin = tables(IROT // 2)
    c[:, C_ICOS:C_ICOS + 32] = cos.reshape(TT, P, -1).transpose(1, 0, 2).reshape(P, -1)
    c[:, C_ISIN:C_ISIN + 32] = sin.reshape(TT, P, -1).transpose(1, 0, 2).reshape(P, -1)
    c[:, C_ID:C_ID + P] = np.eye(P)
    band = np.zeros((S, 4, S), np.float32)
    for g, w in enumerate(POOLS):
        for t in range(S):
            lo = max(0, t - w + 1)
            band[lo:t + 1, g, t] = np.float32(1.0) / np.float32(t + 1 - lo)
            band[t, g, t] -= 1.0
    c[:, C_BAND:] = band.reshape(TT, P, 4 * S).transpose(1, 0, 2).reshape(P, -1)
    return c


def kernel(**inputs):
    import concourse.bacc as bacc
    from concourse.bass_utils import run_bass_kernel_spmd

    a = {k: np.asarray(v) for k, v in inputs.items()}
    w1 = {k: v[0] for k, v in a.items() if k not in ("x", "final_norm_2")}
    wi, wz = w1["w_in"], w1["w_in_2"]
    n_idx = 3 * ATT + IDX_W
    wo = _chunks(w1["w_out"])
    z = _features(wz)
    pa, pb = _features(w1["w_proj_a_2"]), _features(w1["w_proj_b_2"])
    up1, up2 = w1["ffn1_w_in_2"], w1["ffn2_w_in_2"]
    stream = np.concatenate([
        _ffn(w1["ffn1_w_gate"], w1["ffn1_w_up"], w1["ffn1_w_down"]),
        _tokens(wi[:, 0:ATT], TOK_K), _tokens(wi[:, ATT:2 * ATT], TOK_K), _tokens(wi[:, 3 * ATT:n_idx], IDX_K),
        _tokens(wi[:, n_idx:], TOK_K), _tokens(wi[:, 2 * ATT:3 * ATT], TOK_K), wo[4:], wo[:4],
        _ffn(w1["ffn2_w_gate"], w1["ffn2_w_up"], w1["ffn2_w_down"]),
        _ffn(up1[:, :FF], up1[:, FF:], w1["ffn1_w_out_2"]),
        _tokens(wz[:, D:D + 512], TOK_K), _tokens(wz[:, D + 512:2 * D], TOK_K),
        np.stack([z[c + m] for m in range(KC) for c in (24, 32, 16)]), z[0:8],
        np.stack([b[m] for m in range(KC) for b in (z[40:48], z[48:56], pa, pb)]),
        _chunks(w1["w_out_2"]),
        _ffn(up2[:, :FF], up2[:, FF:], w1["ffn2_w_out_2"]),
    ])
    assert stream.shape == (BLOCKS, P, BW)
    arrays = {
        "stream": stream,
        "x_in": a["x"][0].T.reshape(KC, P, S).transpose(1, 0, 2),
        "cols_in": np.concatenate([_cols(v) for v in (
            w1["ffn1_norm"], w1["mix_norm"], w1["ffn2_norm"], w1["ffn1_norm_2"], w1["mix_norm_2"], w1["ffn2_norm_2"],
            a["final_norm_2"], w1["sgu_norm_2"], w1["conv_w_2"].reshape(-1), w1["pool_scale"])], 1),
        "rows_in": np.broadcast_to(np.concatenate([w1["q_norm"], w1["k_norm"], w1["sgu_b_2"].reshape(-1)]),
                                   (P, 2 * HD + SGU_HEADS * P)),
        "const_in": _constants(),
        "sgu_w_in": w1["sgu_w_2"].transpose(2, 0, 1),
        "pool_w_in": w1["pool_w"].transpose(1, 0, 2),
    }
    arrays = {k: np.ascontiguousarray(v) for k, v in arrays.items()}
    nc = bacc.Bacc("TRN2", target_bir_lowering=False, num_devices=1)
    args = [nc.dram_tensor(k, v.shape, F32, kind="ExternalInput").ap() for k, v in arrays.items()]
    args.append(nc.dram_tensor("out", (P, KC, S), F32, kind="ExternalOutput").ap())
    build(nc, *args)
    r = run_bass_kernel_spmd(nc, [arrays], core_ids=[0])
    y = r.results[0]["out"]
    return y.transpose(1, 0, 2).reshape(D, S).T.reshape(1, S, D)
```

```python
from contextlib import ExitStack

import numpy as np

import concourse.bass as bass
from concourse import mybir

F32 = mybir.dt.float32
F32R = mybir.dt.float32r
BF16 = mybir.dt.bfloat16
ALU = mybir.AluOpType
ACT = mybir.ActivationFunctionType
AX = mybir.AxisListType

P = 128
D = 1024
S = 256
KC = D // P
TT = S // P
FF = 2816
FC = FF // P
HEADS, HD = 8, 64
ATT = HEADS * HD
PAIRS = ATT // P
IH, ID, IROT = 4, 64, 32
TOPK = 64
POOLS = (2, 4, 8, 16)
THETA = 10000.0
EPS = 1e-6
SGU_HEADS = 8
CONV = 3

BW = 1024
HALF = BW // 2
RING = 4
IDX_W = IH * ID + ID + IH
IDX_K = BW // IDX_W
IDX_B = -(-KC // IDX_K)
TOK_K = BW // 512
TOK_B = KC // TOK_K

FFN_B = 3 * FC
LOOPED = (FC - 4) // 4 * 4
MIX1_B = 4 * TOK_B + IDX_B + KC
CONV_B, GATE_B = 3 * KC, 4 * KC
MIX2_B = 2 * TOK_B + CONV_B + KC + GATE_B + KC
START = np.cumsum([0, FFN_B, MIX1_B, FFN_B, FFN_B, MIX2_B, FFN_B]).tolist()
BLOCKS = START[-1]

COLS = {"ffn1": 0, "mix": 8, "ffn2": 16, "ffn1_2": 24, "mix_2": 32, "ffn2_2": 40, "final": 48, "sgu": 56,
        "conv": 64, "pool": 88}
NCOLS = 92
PHASE_GAIN = ["ffn1", "mix", "ffn2", "ffn1_2", "mix_2", "ffn2_2", "final"]
C_COS, C_SIN, C_ICOS, C_ISIN, C_ID, C_BAND = 0, 128, 256, 288, 320, 448
NCONST = 448 + 2 * 4 * 256

UNSEL, NEG, MASKED = -3.0e38, -2.0e38, -1.0e30


def build(nc, stream, x_in, cols_in, rows_in, const_in, sgu_w_in, pool_w_in, out):
    ctx = ExitStack()
    with ctx:
        def sb(name, shape, dt=F32):
            return ctx.enter_context(nc.sbuf_tensor(name, shape, dt))

        def sem(name):
            return ctx.enter_context(nc.semaphore(name))

        w_raw = sb("w_raw", [P, RING, BW])
        w_hi = sb("w_hi", [P, RING, BW], F32R)
        w_lo = sb("w_lo", [P, RING, BW], F32R)
        x = sb("x", [P, KC, S])
        x_hi = sb("x_hi", [P, KC, S], F32R)
        x_lo = sb("x_lo", [P, KC, S], F32R)
        x_sq = sb("x_sq", [P, KC, S])
        ms = sb("ms", [P, S])
        root = sb("root", [P, S])
        newton = sb("newton", [P, S])
        rstd = sb("rstd", [P, S])
        rstd_sq = sb("rstd_sq", [P, S])
        r_col = sb("r_col", [P, TT])
        r_col16 = sb("r_col16", [P, TT])
        cols = sb("cols", [P, NCOLS])
        rows = sb("rows", [P, 2 * HD + SGU_HEADS * P])
        const = sb("const", [P, NCONST])
        sgu_w = sb("sgu_w", [P, SGU_HEADS, P])
        pool_w = sb("pool_w", [P, 4, P])
        ones = sb("ones", [P, P])
        zeros = sb("zeros", [P, 512], BF16)
        spare = sb("spare", [P, 1])
        end_tile = sb("end_tile", [P, 4, TT])
        end_ms, end_root, end_nt, end_r = (end_tile[:, n, :] for n in range(4))
        tmp = sb("tmp", [P, 4, S])
        gate_s, up_s, silu, hid = (tmp[:, n, :] for n in range(4))
        hid_hi = sb("hid_hi", [P, 4, S], F32R)
        hid_lo = sb("hid_lo", [P, 4, S], F32R)
        mix_hi = sb("mix_hi", [P, KC, S], F32R)
        mix_lo = sb("mix_lo", [P, KC, S], F32R)
        q_tok = sb("q_tok", [P, 2 * TT, ATT])
        qk_a = sb("qk_a", [P, 2 * TT, ATT])
        qk_b = x_sq[:].rearrange("p (a b) s -> p a (b s)", b=2)
        v_tok = sb("v_tok", [P, TT, D])
        u_tok = v_tok[:, :, ATT:2 * ATT]
        qk_ss = sb("qk_ss", [P, 2 * TT * HEADS])
        qk_ms = sb("qk_ms", [P, 2 * TT * HEADS])
        qk_root = sb("qk_root", [P, 2 * TT * HEADS])
        qk_nt = sb("qk_nt", [P, 2 * TT * HEADS])
        qk_r = sb("qk_r", [P, 2 * TT * HEADS])
        rope_c = sb("rope_c", [P, 2, TT, HD])
        rope_s = sb("rope_s", [P, 2, TT, HD])
        idx_tok = sb("idx_tok", [P, TT, (IH + 2) * ID])
        idx_w = sb("idx_w", [P, TT, IH])
        idx_t = tmp[:].rearrange("p a s -> p (a s)")[:, 0:4 * TT * (IH + 2) * IROT // 2].rearrange(
            "p (a t h d) -> p a t h d", a=4, t=TT, h=IH + 2)
        qiT = sb("qiT", [P, 2, S])
        kiT = sb("kiT", [P, S])
        rel = x_sq[:].rearrange("p (t h) s -> p t h s", t=TT)
        score = sb("score", [P, TT, S])
        work = sb("work", [P, TT, S])
        top8 = sb("top8", [P, TT, 8])
        bias = sb("bias", [P, TT, S])
        qT = q_tok[:, 0:2, :].rearrange("p a (b s) -> p (a b) s", b=2)
        kT = q_tok[:, 2:4, :].rearrange("p a (b s) -> p (a b) s", b=2)
        logit = qk_a[:, 0:2, :].rearrange("p a (t s) -> p a t s", t=TT)
        prob = qk_a[:, 2:4, :].rearrange("p a (t s) -> p a t s", t=TT)
        neg1 = sb("neg1", [P, HEADS, TT])
        psums = sb("psums", [P, HEADS, TT])
        rsum = sb("rsum", [P, HEADS, TT])
        probT = idx_tok
        pool_in = tmp
        v_ss = sb("v_ss", [P, 5, TT])
        gc_s, gb_s, conv_a, conv_y = (tmp[:, n, :] for n in range(4))
        conv_in = sb("conv_in", [P, S + 2])
        yb_hi = sb("yb_hi", [P, KC, S], F32R)
        yb_lo = sb("yb_lo", [P, KC, S], F32R)
        ya_hi = sb("ya_hi", [P, KC, S], F32R)
        ya_lo = sb("ya_lo", [P, KC, S], F32R)
        sg = x_sq
        u_s = qk_a[:].rearrange("p a (b s) -> p (a b) s", b=2)
        gates, sig, branch = (q_tok[:, n, :] for n in range(3))
        merged = tmp[:, 0, :]

        bank = [ctx.enter_context(nc.psum_tensor(f"bank{i}", [P, 512], F32)) for i in range(8)]

        ident = const[:, C_ID:C_ID + P]

        def acc(m):
            return bank[m // 2][:, (m % 2) * S:(m % 2 + 1) * S]

        arrived = [sem(f"arrived{i}") for i in range(RING)]
        half_arrived = [sem(f"half_arrived{i}") for i in range(2)]
        half_hi_done = sem("half_hi_done")
        half_split = sem("half_split")
        w_hi_done = sem("w_hi_done")
        w_split = sem("w_split")
        w_used = sem("w_used")
        x_loaded = [sem(f"x_loaded{c}") for c in range(4)]
        cols_loaded = sem("cols_loaded")
        const_loaded = sem("const_loaded")
        rows_loaded = sem("rows_loaded")
        sgu_loaded = sem("sgu_loaded")
        pool_loaded = sem("pool_loaded")
        spare_set = sem("spare_set")
        filled = sem("filled")
        tables_made = sem("tables_made")
        acc_done = sem("acc_done")
        x_new = sem("x_new")
        x_hi_done = sem("x_hi_done")
        x_split = sem("x_split")
        x_sq_done = sem("x_sq_done")
        x_sq_added = sem("x_sq_added")
        sumsq_done = sem("sumsq_done")
        ms_done = sem("ms_done")
        root_done = sem("root_done")
        rstd_done = sem("rstd_done")
        rT_done = sem("rT_done")
        r_col_done = sem("r_col_done")
        gate_scaled = sem("gate_scaled")
        up_scaled = sem("up_scaled")
        silu_done = sem("silu_done")
        hid_done = sem("hid_done")
        hid_hi_done = sem("hid_hi_done")
        hid_split = sem("hid_split")
        q_copied = sem("q_copied")
        qk_sq = sem("qk_sq")
        qk_ms_done = sem("qk_ms_done")
        qk_root_done = sem("qk_root_done")
        qk_normed = sem("qk_normed")
        qk_cos = sem("qk_cos")
        qk_sin = sem("qk_sin")
        qk_roped = sem("qk_roped")
        idx_copied = sem("idx_copied")
        idx_roped = sem("idx_roped")
        idx_T = sem("idx_T")
        idx_T_copied = sem("idx_T_copied")
        v_copied = sem("v_copied")
        u_copied = sem("u_copied")
        idx_dots = sem("idx_dots")
        rel_done = sem("rel_done")
        score_sum = sem("score_sum")
        score_done = sem("score_done")
        top_found = sem("top_found")
        top_taken = sem("top_taken")
        score_masked = sem("score_masked")
        sel_done = sem("sel_done")
        bias_done = sem("bias_done")
        pool_mean = sem("pool_mean")
        pool_mean_copied = sem("pool_mean_copied")
        pool_out = sem("pool_out")
        mix_hi_done = sem("mix_hi_done")
        mix_split = sem("mix_split")
        qk_T = sem("qk_T")
        qk_T_copied = sem("qk_T_copied")
        logits_done = sem("logits_done")
        logits_read = sem("logits_read")
        exp_done = sem("exp_done")
        prob_done = sem("prob_done")
        probT_done = sem("probT_done")
        probT_copied = sem("probT_copied")
        pv_done = sem("pv_done")
        v_gelu = sem("v_gelu")
        v_sq = sem("v_sq")
        v_ms_done = sem("v_ms_done")
        v_root_done = sem("v_root_done")
        v_normed = sem("v_normed")
        spatial_done = sem("spatial_done")
        sg_done = sem("sg_done")
        conv_read = sem("conv_read")
        gc_scaled = sem("gc_scaled")
        conv_mid = sem("conv_mid")
        conv_done = sem("conv_done")
        yb_hi_done = sem("yb_hi_done")
        yb_split = sem("yb_split")
        u_scaled = sem("u_scaled")
        u_gelu = sem("u_gelu")
        ya_done = sem("ya_done")
        ya_hi_done = sem("ya_hi_done")
        ya_split = sem("ya_split")
        gates_scaled = sem("gates_scaled")
        sig_done = sem("sig_done")
        branch_done = sem("branch_done")
        merged_done = sem("merged_done")
        dve_step = sem("dve_step")
        x_gained = sem("x_gained")
        out_ready = sem("out_ready")
        diagonal_done = sem("diagonal_done")
        spread_done = sem("spread_done")
        stored = sem("stored")

        block = ctx.enter_context(nc.Block())

        @block.sync
        def _(sp):
            for n in range(2):
                sp.dma_start(w_raw[:, n, 0:HALF], stream[n, :, 0:HALF]).then_inc(half_arrived[n], 16)
            for n in range(2):
                sp.dma_start(w_raw[:, n, HALF:BW], stream[n, :, HALF:BW]).then_inc(arrived[n], 16)
            for c in range(2, 4):
                sp.dma_start(x[:, 2 * c:2 * c + 2, :], x_in[:, 2 * c:2 * c + 2, :]).then_inc(x_loaded[c], 16)
            for n in range(2, RING):
                sp.dma_start(w_raw[:, n, :], stream[n]).then_inc(arrived[n], 16)
            with sp.Fori(1, BLOCKS // RING) as i:
                for j in range(RING):
                    sp.wait_ge(w_split, RING * i + (j - RING + 1))
                    sp.dma_start(w_raw[:, j, :],
                                 stream[bass.ds(RING * i + j, 1), :, :].rearrange("a p c -> p (a c)")
                                 ).then_inc(arrived[j], 16)
            for n in range(BLOCKS // RING * RING, BLOCKS):
                sp.wait_ge(w_split, n - RING + 1)
                sp.dma_start(w_raw[:, n % RING, :], stream[n]).then_inc(arrived[n % RING], 16)
            for c in range(4):
                sp.wait_ge(out_ready, c + 1)
                sp.dma_start(out[:, 2 * c:2 * c + 2, :], x_sq[:, 2 * c:2 * c + 2, :]).then_inc(stored, 16)
            sp.wait_ge(stored, 64)

        @block.gpsimd
        def _(pool):
            nc.gpsimd.memset(zeros[:], 0.0).then_inc(filled, 1)
            nc.gpsimd.memset(ones[:], 1.0).then_inc(filled, 1)
            nc.gpsimd.memset(conv_in[:], 0.0).then_inc(filled, 1)

            def add_squares(p):
                def pair(c):
                    return x_sq[:, 2 * c:2 * c + 2, :].rearrange("p a s -> p (a s)")

                for c in range(1, 4):
                    pool.wait_ge(x_sq_done, 4 * p + c + 1)
                    if c > 1:
                        pool.wait_ge(x_sq_added, 4 * p + c - 1)
                    nc.gpsimd.tensor_tensor(pair(0), pair(0), pair(c), ALU.add).then_inc(x_sq_added, 1)
                pool.wait_ge(x_sq_added, 4 * p + 3)
                nc.gpsimd.tensor_tensor(x_sq[:, 0, :], x_sq[:, 0, :], x_sq[:, 1, :], ALU.add).then_inc(x_sq_added, 1)

            add_squares(0)
            pool.dma_start(const[:], const_in).then_inc(const_loaded, 16)
            pool.dma_start(rows[:], rows_in).then_inc(rows_loaded, 16)
            pool.dma_start(pool_w[:], pool_w_in).then_inc(pool_loaded, 16)
            pool.dma_start(sgu_w[:], sgu_w_in).then_inc(sgu_loaded, 16)
            pool.wait_ge(const_loaded, 16)
            pool.wait_ge(rows_loaded, 16)
            cos = const[:, C_COS:C_COS + P].rearrange("p (t d) -> p t d", t=TT)
            sin = const[:, C_SIN:C_SIN + P].rearrange("p (t d) -> p t d", t=TT)
            h = HD // 2
            for a in range(2):
                for t in range(TT):
                    gain = rows[:, a * HD:(a + 1) * HD]
                    nc.gpsimd.tensor_tensor(rope_c[:, a, t, :], gain, cos[:, t, :], ALU.mult)
                    nc.gpsimd.tensor_tensor(rope_s[:, a, t, 0:h], gain[:, h:HD], sin[:, t, 0:h], ALU.mult)
                    last = nc.gpsimd.tensor_tensor(rope_s[:, a, t, h:HD], gain[:, 0:h], sin[:, t, h:HD], ALU.mult)
                    last.then_inc(tables_made, 1)
            add_squares(1)
            pool.wait_ge(tables_made, 4)

            def heads_of(tile):
                return tile.rearrange("p (h d) -> p h d", d=HD)

            def cosine_terms(a):
                for t in range(TT):
                    nc.gpsimd.tensor_tensor(heads_of(qk_a[:, 2 * a + t, :]), heads_of(q_tok[:, 2 * a + t, :]),
                                            rope_c[:, a, t, :].unsqueeze(1).to_broadcast([P, HEADS, HD]),
                                            ALU.mult).then_inc(qk_cos, 1)

            def sine_terms(a):
                for t in range(TT):
                    src, dst = heads_of(q_tok[:, 2 * a + t, :]), heads_of(qk_b[:, 2 * a + t, :])
                    for lo, hi in ((0, h), (h, 0)):
                        nc.gpsimd.tensor_tensor(dst[:, :, lo:lo + h], src[:, :, hi:hi + h],
                                                rope_s[:, a, t, lo:lo + h].unsqueeze(1).to_broadcast([P, HEADS, h]),
                                                ALU.mult).then_inc(qk_sin, 1)

            def terms_together(a):
                pool.wait_ge(qk_sin, 4 * (a + 1))
                pool.wait_ge(qk_cos, 2 * (a + 1))
                for t in range(TT):
                    nc.gpsimd.tensor_tensor(qk_b[:, 2 * a + t, :], qk_b[:, 2 * a + t, :], qk_a[:, 2 * a + t, :],
                                            ALU.add).then_inc(qk_roped, 1)

            pool.wait_ge(qk_normed, 1)
            cosine_terms(0)
            for t in range(TT):
                n = (t + 1) * P
                pool.wait_ge(score_done, t + 1)
                nc.gpsimd.affine_select(out=work[:, t, 0:n], in_=score[:, t, 0:n], compare_op=ALU.is_ge, fill=NEG,
                                        base=t * P, pattern=[[-1, n]], channel_multiplier=1).then_inc(score_masked, 1)
            sine_terms(0)
            terms_together(0)
            pool.wait_ge(qk_normed, 2)
            cosine_terms(1)
            sine_terms(1)
            terms_together(1)
            for t in range(TT):
                n = (t + 1) * P
                pool.wait_ge(sel_done, t + 1)
                nc.gpsimd.affine_select(out=bias[:, t, 0:n], in_=score[:, t, 0:n], compare_op=ALU.is_ge, fill=MASKED,
                                        base=t * P, pattern=[[-1, n]], channel_multiplier=1).then_inc(bias_done, 1)
            for p in range(2, 5):
                add_squares(p)
            for m in range(KC):
                pool.wait_ge(u_gelu, m + 1)
                pool.wait_ge(sg_done, m + 1)
                nc.gpsimd.tensor_tensor(u_s[:, m, :], u_s[:, m, :], sg[:, m, :], ALU.mult).then_inc(ya_done, 1)
            add_squares(5)

        @block.scalar
        def _(act):
            def split(n, i=0, per=0):
                if n >= BLOCKS:
                    return
                slot = n % RING
                act.wait_ge(arrived[slot], 16 * (n // RING + 1) + 16 * (per // RING) * i)
                if n >= RING:
                    act.wait_ge(w_used, n - RING + 1 + per * i)
                nc.scalar.activation(w_hi[:, slot, :], w_raw[:, slot, :], ACT.Copy).then_inc(w_hi_done, 1)

            def phase_input(p):
                g = COLS[PHASE_GAIN[p]]

                def square(c):
                    nc.scalar.activation(x_sq[:, 2 * c:2 * c + 2, :], x[:, 2 * c:2 * c + 2, :],
                                         ACT.Square).then_inc(x_sq_done, 1)

                for c in range(4):
                    if p:
                        act.wait_ge(x_new, 4 * (p - 1) + c + 1)
                    else:
                        act.wait_ge(x_loaded[c], 16)
                    if p == 6:
                        square(c)
                        continue
                    for k in (2 * c, 2 * c + 1):
                        nc.scalar.activation(x_hi[:, k, :], x[:, k, :], ACT.Identity,
                                             scale=cols[:, g + k:g + k + 1]).then_inc(x_hi_done, 1)
                    if p == 0 and c == 1:
                        for n in range(2):
                            act.wait_ge(arrived[n], 16)
                            nc.scalar.activation(w_hi[:, n, HALF:BW], w_raw[:, n, HALF:BW], ACT.Copy).then_inc(w_hi_done, 1)
                    if 1 <= c < 3:
                        square(c - 1)
                if p < 6:
                    split(START[p] + 2)
                    square(2)
                    square(3)

            def rms_root(p):
                act.wait_ge(ms_done, p + 1)
                nc.scalar.activation(root[:], ms[:], ACT.Sqrt).then_inc(root_done, 1)

            def ffn(e, n0, p):
                for b in range(3, 7):
                    split(n0 + b)
                rms_root(p)

                def gate(f):
                    act.wait_ge(gate_scaled, FC * e + 1 + f)
                    nc.scalar.activation(silu, gate_s, ACT.Silu).then_inc(silu_done, 1)

                def hidden(f, slot):
                    act.wait_ge(hid_done, FC * e + 1 + f)
                    nc.scalar.activation(hid_hi[:, slot, :], hid, ACT.Copy).then_inc(hid_hi_done, 1)

                for f in range(3):
                    if f:
                        split(n0 + 6 + 2 * f)
                    gate(f)
                    split(n0 + 7 + 2 * f)
                    hidden(f, f)

                def chunk(f, j, i=0):
                    b = n0 + 10 + 3 * (f - 4)
                    split(b + 2, i, 12)
                    gate(4 * i + (f - 1))
                    hidden(4 * i + (f - 1), (j - 1) % 4)
                    split(b + 3, i, 12)
                    split(b + 4, i, 12)

                with act.Fori(0, LOOPED // 4) as i:
                    for j in range(4):
                        chunk(4 + j, j, i)
                for f in range(4 + LOOPED, FC):
                    chunk(f, f % 4)
                split(n0 + FFN_B)
                gate(FC - 1)
                hidden(FC - 1, (FC - 1) % 4)
                split(n0 + FFN_B + 1)

            def attention_mixer(n0, p):
                for b in range(3, 6):
                    split(n0 + b)
                rms_root(p)
                for b in range(6, 10):
                    split(n0 + b)
                act.wait_ge(r_col_done, 1)

                def tokens_out(dst, src, used, done):
                    act.wait_ge(w_used, n0 + used)
                    for t in range(TT):
                        nc.scalar.activation(dst[t], src[t], ACT.Identity, scale=r_col[:, t:t + 1]).then_inc(done, 1)

                tokens_out([q_tok[:, 0, :], q_tok[:, 1, :]], [bank[4][:], bank[5][:]], 4, q_copied)
                split(n0 + 10)
                split(n0 + 11)
                tokens_out([q_tok[:, 2, :], q_tok[:, 3, :]], [bank[6][:], bank[7][:]], 8, q_copied)
                split(n0 + 12)
                split(n0 + 13)
                split(n0 + 14)
                act.wait_ge(w_used, n0 + 11)
                q_w = IH * ID
                for t in range(TT):
                    src, r = bank[t], r_col[:, t:t + 1]
                    nc.scalar.activation(idx_tok[:, t, 0:q_w + ID], src[:, 0:q_w + ID], ACT.Identity, scale=r)
                    nc.scalar.activation(idx_tok[:, t, q_w + ID:q_w + 2 * ID], src[:, q_w:q_w + ID], ACT.Identity, scale=r)
                    nc.scalar.activation(idx_w[:, t, :], src[:, q_w + ID:IDX_W], ACT.Identity,
                                         scale=r_col16[:, t:t + 1]).then_inc(idx_copied, 1)
                for a in range(2):
                    act.wait_ge(q_copied, 2 * a + 2)
                    nc.scalar.activation(qk_a[:, 2 * a:2 * a + 2, :], q_tok[:, 2 * a:2 * a + 2, :],
                                         ACT.Square).then_inc(qk_sq, 1)
                split(n0 + 15)
                split(n0 + 16)
                act.wait_ge(idx_T, 1)
                nc.scalar.activation(qiT[:].rearrange("p c s -> p (c s)"), bank[6][:], ACT.Copy).then_inc(idx_T_copied, 1)
                nc.scalar.activation(kiT[:], bank[7][:, 0:S], ACT.Copy).then_inc(idx_T_copied, 1)
                split(n0 + 17)
                act.wait_ge(qk_ms_done, 1)
                nc.scalar.activation(qk_root[:], qk_ms[:], ACT.Sqrt).then_inc(qk_root_done, 1)
                split(n0 + 18)
                tokens_out([u_tok[:, 0, :], u_tok[:, 1, :]], [bank[2][:], bank[3][:]], 15, u_copied)
                act.wait_ge(idx_dots, 1)
                for t in range(TT):
                    n = (t + 1) * P
                    for odd in range(2):
                        nc.scalar.activation(rel[:, t, odd::2, 0:n],
                                             bank[6 * t + odd][:, 0:2 * n].rearrange("p (h s) -> p h s", h=2),
                                             ACT.Relu).then_inc(rel_done, 1)
                split(n0 + 19)
                for g in range(4):
                    act.wait_ge(pool_mean, g // 2 + 1)
                    nc.scalar.activation(pool_in[:, g, :], bank[2 + g // 2][:, (g % 2) * S:(g % 2 + 1) * S],
                                         ACT.Copy).then_inc(pool_mean_copied, 1)
                split(n0 + 20)
                for g in range(4):
                    act.wait_ge(pool_out, g // 2 + 1)
                    nc.scalar.activation(mix_hi[:, PAIRS + g, :], bank[2 + g // 2][:, (g % 2) * S:(g % 2 + 1) * S],
                                         ACT.Identity, scale=cols[:, COLS["pool"] + g:COLS["pool"] + g + 1]
                                         ).then_inc(mix_hi_done, 1)
                split(n0 + 21)
                split(n0 + 22)
                tokens_out([v_tok[:, 0, 0:ATT], v_tok[:, 1, 0:ATT]], [bank[4][:], bank[5][:]], 19, v_copied)
                split(n0 + 23)
                for b in range(4):
                    act.wait_ge(qk_T, b + 1)
                    nc.scalar.activation((qT, kT)[b // 2][:, 2 * (b % 2):2 * (b % 2) + 2, :],
                                         bank[(6, 7, 4, 5)[b]][:].rearrange("p (c s) -> p c s", c=2),
                                         ACT.Copy).then_inc(qk_T_copied, 1)
                for s in range(1, HEADS + 4):
                    if s >= 4:
                        hd = s - 4
                        lo = hd % 2 * HD
                        act.wait_ge(pv_done, hd + 1)
                        nc.scalar.activation(mix_hi[lo:lo + HD, hd // 2, :], bank[7][lo:lo + HD, 0:S],
                                             ACT.Copy).then_inc(mix_hi_done, 1)
                    if 3 <= s <= HEADS + 2:
                        hd = s - 3
                        act.wait_ge(probT_done, hd + 1)
                        if hd >= 2:
                            act.wait_ge(pv_done, hd - 1)
                        nc.scalar.activation(probT[:, hd % 2, :], bank[6][:, 0:3 * P],
                                             ACT.Copy).then_inc(probT_copied, 1)
                    if s <= HEADS:
                        hd = s - 1
                        act.wait_ge(logits_read, 2 * hd + 2)
                        if hd >= 2:
                            act.wait_ge(probT_done, hd - 1)
                        for t in range(TT):
                            n = (t + 1) * P
                            nc.scalar.activation(prob[:, hd % 2, t, 0:n], logit[:, hd % 2, t, 0:n], ACT.Exp,
                                                 bias=neg1[:, hd, t:t + 1], scale=-1.0,
                                                 accum_out=psums[:, hd, t:t + 1]).then_inc(exp_done, 1)
                    if s in MIX1_SPLITS:
                        split(n0 + 24 + MIX1_SPLITS.index(s))

            def gated_mixer(n0, p):
                for b in range(3, 6):
                    split(n0 + b)
                rms_root(p)
                for b in range(6, 10):
                    split(n0 + b)
                act.wait_ge(r_col_done, 2)
                for g in range(2):
                    act.wait_ge(w_used, n0 + 4 * g + 4)
                    for t in range(TT):
                        nc.scalar.activation(v_tok[:, t, g * 512:(g + 1) * 512], bank[4 + 2 * g + t][:],
                                             ACT.Gelu_apprx_tanh, scale=r_col[:, t:t + 1]).then_inc(v_gelu, 1)
                    if g == 0:
                        split(n0 + 10)
                act.wait_ge(v_gelu, 4)
                for t in range(TT):
                    nc.scalar.activation(qk_a[:, 2 * t:2 * t + 2, :].rearrange("p a c -> p (a c)"), v_tok[:, t, :],
                                         ACT.Square, accum_out=v_ss[:, 0, t:t + 1]).then_inc(v_sq, 1)
                with act.Fori(0, 2) as i:
                    for j in range(4):
                        b = n0 + 8 + 3 * j
                        split(b + 3, i, 12)
                        split(b + 4, i, 12)
                        split(b + 5, i, 12)
                        act.wait_ge(conv_done, 4 * i + (j + 1))
                        nc.scalar.activation(yb_hi[:, bass.ds(4 * i + j, 1), :], conv_y.unsqueeze(1),
                                             ACT.Copy).then_inc(yb_hi_done, 1)
                split(n0 + 35)
                act.wait_ge(v_ms_done, 1)
                nc.scalar.activation(v_ss[:, 2, :], v_ss[:, 1, :], ACT.Sqrt).then_inc(v_root_done, 1)
                for b in range(36, 40):
                    split(n0 + b)

                def u_act(m):
                    act.wait_ge(u_scaled, m + 1)
                    nc.scalar.activation(u_s[:, m, :], u_s[:, m, :], ACT.Gelu_apprx_tanh).then_inc(u_gelu, 1)

                def ya_part(m):
                    act.wait_ge(ya_done, m + 1)
                    nc.scalar.activation(ya_hi[:, m, :], u_s[:, m, :], ACT.Copy).then_inc(ya_hi_done, 1)

                for m in range(4):
                    u_act(m)
                ya_part(0)
                ya_part(1)
                split(n0 + 40)
                u_act(4)
                ya_part(2)
                ya_part(3)
                split(n0 + 41)
                u_act(5)
                ya_part(4)
                split(n0 + 42)
                u_act(6)
                ya_part(5)
                split(n0 + 43)
                u_act(7)
                ya_part(6)
                ya_part(7)
                with act.Fori(0, 4) as i:
                    for j in range(2):
                        b = n0 + 40 + 4 * j
                        split(b + 4, i, 8)
                        split(b + 5, i, 8)
                        act.wait_ge(gates_scaled, 2 * i + (j + 1))
                        nc.scalar.activation(sig, gates, ACT.Sigmoid).then_inc(sig_done, 1)
                        split(b + 6, i, 8)
                        act.wait_ge(merged_done, 2 * i + (j + 1))
                        nc.scalar.activation(mix_hi[:, bass.ds(2 * i + j, 1), :], merged.unsqueeze(1),
                                             ACT.Copy).then_inc(mix_hi_done, 1)
                        split(b + 7, i, 8)
                for b in range(76, 82):
                    split(n0 + b)

            act.dma_start(x[:, 0:2, :], x_in[:, 0:2, :]).then_inc(x_loaded[0], 16)
            act.dma_start(cols[:], cols_in).then_inc(cols_loaded, 16)
            act.dma_start(x[:, 2:4, :], x_in[:, 2:4, :]).then_inc(x_loaded[1], 16)
            act.wait_ge(filled, 1)
            nc.scalar.activation(spare[:], zeros[:, 0:1], ACT.Copy).then_inc(spare_set, 1)
            for n in range(2):
                act.wait_ge(half_arrived[n], 16)
                nc.scalar.activation(w_hi[:, n, 0:HALF], w_raw[:, n, 0:HALF], ACT.Copy).then_inc(half_hi_done, 1)
            act.wait_ge(cols_loaded, 16)
            phase_input(0)
            ffn(0, START[0], 0)
            phase_input(1)
            attention_mixer(START[1], 1)
            phase_input(2)
            ffn(1, START[2], 2)
            phase_input(3)
            ffn(2, START[3], 3)
            phase_input(4)
            gated_mixer(START[4], 4)
            phase_input(5)
            ffn(3, START[5], 5)
            phase_input(6)
            act.wait_ge(spare_set, 1)
            nc.scalar.activation(spare[:], zeros[:, 0:1], ACT.Sqrt).then_inc(spare_set, 1)
            act.wait_ge(x_sq_done, 28)

            def gained(k):
                g = COLS["final"] + k
                nc.scalar.activation(x[:, k, :], x[:, k, :], ACT.Identity, scale=cols[:, g:g + 1]).then_inc(x_gained, 1)

            for k in range(3):
                gained(k)
            act.wait_ge(ms_done, 7)
            nc.scalar.activation(end_root, end_ms, ACT.Sqrt).then_inc(root_done, 1)
            for k in range(3, KC):
                gained(k)

        @block.vector
        def _(dve):
            steps = [0]

            def step(ins):
                steps[0] += 1
                ins.then_inc(dve_step, 1)
                dve.wait_ge(dve_step, steps[0])

            def split(n, i=0, per=0):
                if n >= BLOCKS:
                    return
                slot = n % RING
                dve.wait_ge(w_hi_done, n + 1 + per * i)
                nc.vector.tensor_tensor(w_lo[:, slot, :], w_raw[:, slot, :], w_hi[:, slot, :].bitcast(F32),
                                        ALU.subtract).then_inc(w_split, 1)

            def input_lo(p, k):
                g = COLS[PHASE_GAIN[p]]
                dve.wait_ge(x_hi_done, 8 * p + k + 1)
                nc.vector.scalar_tensor_tensor(x_lo[:, k, :], x[:, k, :], cols[:, g + k:g + k + 1],
                                               x_hi[:, k, :].bitcast(F32), ALU.mult, ALU.subtract).then_inc(x_split, 1)

            def residual(p, factor):
                for c in range(4):
                    if c < 3:
                        dve.wait_ge(acc_done, 3 * p + c + 1)
                    else:
                        dve.wait_ge(w_used, START[p + 1])
                    two = x[:, 2 * c:2 * c + 2, :].rearrange("p a s -> p (a s)")
                    nc.vector.scalar_tensor_tensor(two, bank[c][:], factor, two, ALU.mult, ALU.add).then_inc(x_new, 1)
                    if c and p < 5:
                        input_lo(p + 1, 2 * c - 2)
                        input_lo(p + 1, 2 * c - 1)
                if p < 5:
                    input_lo(p + 1, KC - 2)
                    input_lo(p + 1, KC - 1)

            def inv_root(ms_ap, root_ap, nt, r):
                step(nc.vector.reciprocal(r, root_ap))
                step(nc.vector.scalar_tensor_tensor(nt, ms_ap, -0.5, r, ALU.mult, ALU.mult))
                step(nc.vector.tensor_tensor(nt, nt, r, ALU.mult))
                return nc.vector.scalar_tensor_tensor(r, nt, 1.5, r, ALU.add, ALU.mult)

            def rms(p):
                dve.wait_ge(sumsq_done, p + 1)
                nc.vector.tensor_scalar(ms[:], bank[STAT[p]][:, 0:S], 1.0 / D, EPS, ALU.mult, ALU.add).then_inc(ms_done, 1)
                dve.wait_ge(root_done, p + 1)
                inv_root(ms[:], root[:], newton[:], rstd[:]).then_inc(rstd_done, 1)
                dve.wait_ge(rstd_done, p + 1)

            def token_scales(n):
                dve.wait_ge(rT_done, n)
                for t in range(TT):
                    last = nc.vector.tensor_copy(r_col[:, t:t + 1], bank[2][:, t * P:t * P + 1])
                    step(last)
                nc.vector.tensor_scalar(r_col16[:], r_col[:], IH ** -0.5 * ID ** -0.5, None,
                                        ALU.mult).then_inc(r_col_done, 1)

            def ffn(e, n0, p):
                for b in range(2, 7):
                    split(n0 + b)
                rms(p)

                def scale(f, slot, used):
                    dve.wait_ge(w_used, used)
                    nc.vector.tensor_tensor(gate_s, bank[4 + slot][:, 0:S], rstd[:], ALU.mult).then_inc(gate_scaled, 1)
                    nc.vector.tensor_tensor(up_s, bank[4 + slot][:, S:2 * S], rstd[:], ALU.mult).then_inc(up_scaled, 1)

                def product(f):
                    dve.wait_ge(up_scaled, FC * e + 1 + f)
                    dve.wait_ge(silu_done, FC * e + 1 + f)
                    nc.vector.tensor_tensor(hid, silu, up_s, ALU.mult).then_inc(hid_done, 1)

                def hidden_lo(f, slot):
                    dve.wait_ge(hid_hi_done, FC * e + 1 + f)
                    nc.vector.tensor_tensor(hid_lo[:, slot, :], hid, hid_hi[:, slot, :].bitcast(F32),
                                            ALU.subtract).then_inc(hid_split, 1)

                for f in range(3):
                    scale(f, f, n0 + 2 * f + 2)
                    if f:
                        split(n0 + 6 + 2 * f)
                    product(f)
                    split(n0 + 7 + 2 * f)
                    hidden_lo(f, f)

                def chunk(f, j, i=0):
                    b = n0 + 10 + 3 * (f - 4)
                    split(b + 2, i, 12)
                    scale(4 * i + (f - 1), (j - 1) % 4, 12 * i + (b - 1))
                    product(4 * i + (f - 1))
                    hidden_lo(4 * i + (f - 1), (j - 1) % 4)
                    split(b + 3, i, 12)
                    split(b + 4, i, 12)

                with dve.Fori(0, LOOPED // 4) as i:
                    for j in range(4):
                        chunk(4 + j, j, i)
                for f in range(4 + LOOPED, FC):
                    chunk(f, f % 4)
                scale(FC - 1, (FC - 1) % 4, n0 + FFN_B - 3)
                split(n0 + FFN_B)
                product(FC - 1)
                hidden_lo(FC - 1, (FC - 1) % 4)
                split(n0 + FFN_B + 1)
                residual(p, 0.5)

            def attention_mixer(n0, p):
                for b in range(2, 6):
                    split(n0 + b)
                rms(p)
                for b in range(6, 10):
                    split(n0 + b)
                token_scales(1)
                for b in range(10, 15):
                    split(n0 + b)
                dve.wait_ge(idx_copied, 2)
                heads = idx_tok[:].rearrange("p t (h d) -> p t h d", d=ID)
                h = IROT // 2
                x1, x2 = heads[:, :, :, 0:h], heads[:, :, :, h:IROT]
                shape = [P, TT, IH + 2, h]
                cos = const[:, C_ICOS:C_ICOS + TT * h].rearrange("p (t d) -> p t d", t=TT).unsqueeze(2).to_broadcast(shape)
                sin = const[:, C_ISIN:C_ISIN + TT * h].rearrange("p (t d) -> p t d", t=TT).unsqueeze(2).to_broadcast(shape)
                t1, t2, t3, t4 = (idx_t[:, n] for n in range(4))
                nc.vector.tensor_tensor(t1, x1, cos, ALU.mult)
                nc.vector.tensor_tensor(t2, x2, sin, ALU.mult)
                nc.vector.tensor_tensor(t3, x2, cos, ALU.mult)
                step(nc.vector.tensor_tensor(t4, x1, sin, ALU.mult))
                nc.vector.tensor_tensor(x1, t1, t2, ALU.subtract).then_inc(idx_roped, 1)
                nc.vector.tensor_tensor(x2, t3, t4, ALU.add).then_inc(idx_roped, 1)
                split(n0 + 15)
                split(n0 + 16)
                for a in range(2):
                    dve.wait_ge(qk_sq, a + 1)
                    step(nc.vector.tensor_reduce(qk_ss[:, 16 * a:16 * a + 16],
                                                 qk_a[:, 2 * a:2 * a + 2, :].rearrange("p t (h d) -> p (t h) d", d=HD),
                                                 AX.X, ALU.add))
                nc.vector.tensor_scalar(qk_ms[:], qk_ss[:], 1.0 / HD, EPS, ALU.mult, ALU.add).then_inc(qk_ms_done, 1)
                split(n0 + 17)
                dve.wait_ge(qk_root_done, 1)
                step(inv_root(qk_ms[:], qk_root[:], qk_nt[:], qk_r[:]))
                for a in range(2):
                    heads = q_tok[:, 2 * a:2 * a + 2, :].rearrange("p t (h d) -> p (t h) d", d=HD)
                    nc.vector.tensor_tensor(heads, heads, qk_r[:, 16 * a:16 * a + 16].unsqueeze(2).to_broadcast([P, 16, HD]),
                                            ALU.mult).then_inc(qk_normed, 1)
                for hd in range(IH):
                    for t in range(TT):
                        n = (t + 1) * P
                        dst, w = score[:, t, 0:n], idx_w[:, t, hd:hd + 1]
                        if hd == 0:
                            dve.wait_ge(rel_done, 2 * t + 2)
                            last = nc.vector.tensor_scalar(dst, rel[:, t, hd, 0:n], w, None, ALU.mult)
                        else:
                            dve.wait_ge(score_sum, TT * hd + t - 1)
                            last = nc.vector.scalar_tensor_tensor(dst, rel[:, t, hd, 0:n], w, dst, ALU.mult, ALU.add)
                        last.then_inc(score_done if hd == IH - 1 else score_sum, 1)
                split(n0 + 18)

                def top_round(r):
                    for t in range(TT):
                        if r:
                            dve.wait_ge(top_taken, TT * (r - 1) + t + 1)
                        else:
                            dve.wait_ge(score_masked, t + 1)
                        nc.vector.max(top8[:, t, :], work[:, t, 0:(t + 1) * P]).then_inc(top_found, 1)
                    for t in range(TT):
                        dve.wait_ge(top_found, TT * r + t + 1)
                        nc.vector.match_replace(work[:, t, 0:(t + 1) * P], top8[:, t, :], work[:, t, 0:(t + 1) * P],
                                                UNSEL).then_inc(top_taken, 1)

                for r in range(4):
                    top_round(r)
                split(n0 + 19)
                for g in range(4):
                    dve.wait_ge(mix_hi_done, 2 * (g // 2) + 2)
                    nc.vector.scalar_tensor_tensor(mix_lo[:, PAIRS + g, :],
                                                   bank[2 + g // 2][:, (g % 2) * S:(g % 2 + 1) * S],
                                                   cols[:, COLS["pool"] + g:COLS["pool"] + g + 1],
                                                   mix_hi[:, PAIRS + g, :].bitcast(F32), ALU.mult,
                                                   ALU.subtract).then_inc(mix_split, 1)
                top_round(4)
                split(n0 + 20)
                top_round(5)
                top_round(6)
                split(n0 + 21)
                top_round(7)
                for t in range(TT):
                    dve.wait_ge(top_taken, TOPK // 8 * TT - 1 + t)
                    nc.vector.tensor_scalar(score[:, t, 0:(t + 1) * P], work[:, t, 0:(t + 1) * P], UNSEL, MASKED,
                                            ALU.not_equal, ALU.mult).then_inc(sel_done, 1)
                for b in range(22, 24):
                    split(n0 + b)
                dve.wait_ge(bias_done, 2)
                for s in range(1, HEADS + 4):
                    if s <= HEADS:
                        hd = s - 1
                        dve.wait_ge(logits_done, hd + 1)
                        for t in range(TT):
                            n = (t + 1) * P
                            nc.vector.tensor_tensor_reduce(logit[:, hd % 2, t, 0:n], bank[4 + hd % 2][:, t * P:t * P + n],
                                                           bias[:, t, 0:n], -HD ** -0.5, -MASKED, ALU.add, ALU.min,
                                                           neg1[:, hd, t:t + 1]).then_inc(logits_read, 1)
                    if s >= 4:
                        hd = s - 4
                        lo = hd % 2 * HD
                        dve.wait_ge(mix_hi_done, 4 + hd + 1)
                        nc.vector.tensor_tensor(mix_lo[lo:lo + HD, hd // 2, :], bank[7][lo:lo + HD, 0:S],
                                                mix_hi[lo:lo + HD, hd // 2, :].bitcast(F32),
                                                ALU.subtract).then_inc(mix_split, 1)
                    if 2 <= s <= HEADS + 1:
                        hd = s - 2
                        dve.wait_ge(exp_done, 2 * hd + 2)
                        step(nc.vector.reciprocal(rsum[:, hd, :], psums[:, hd, :]))
                        for t in range(TT):
                            n = (t + 1) * P
                            nc.vector.tensor_scalar(prob[:, hd % 2, t, 0:n], prob[:, hd % 2, t, 0:n],
                                                    rsum[:, hd, t:t + 1], None, ALU.mult).then_inc(prob_done, 1)
                    if s - 1 in MIX1_SPLITS:
                        split(n0 + 24 + MIX1_SPLITS.index(s - 1))
                residual(p, 1.0)

            def gated_mixer(n0, p):
                for b in range(2, 6):
                    split(n0 + b)
                rms(p)
                for b in range(6, 8):
                    split(n0 + b)
                token_scales(2)
                for b in range(8, 10):
                    split(n0 + b)
                split(n0 + 10)
                step(nc.vector.tensor_tensor(rstd_sq[:], rstd[:], rstd[:], ALU.mult))
                with dve.Fori(0, 2) as i:
                    for j in range(4):
                        b = n0 + 8 + 3 * j
                        m = 4 * i + j
                        split(b + 3, i, 12)
                        split(b + 4, i, 12)
                        dve.wait_ge(w_used, 12 * i + (b + 3))
                        pair, single = bank[4 + 2 * (j % 2)], bank[5 + 2 * (j % 2)]
                        nc.vector.tensor_tensor(gc_s, pair[:, 0:S], rstd_sq[:], ALU.mult).then_inc(gc_scaled, 1)
                        nc.vector.tensor_tensor(gb_s, single[:, 0:S], rstd[:], ALU.mult)
                        dve.wait_ge(gc_scaled, m + 1)
                        nc.vector.tensor_tensor(conv_in[:, 1:S + 1], pair[:, S:2 * S], gc_s, ALU.mult).then_inc(conv_read, 1)

                        def tap(k):
                            return cols[:, bass.ds(m + (COLS["conv"] + k * KC), 1)]

                        dve.wait_ge(conv_read, m + 1)
                        nc.vector.tensor_scalar(conv_a, conv_in[:, 0:S], tap(0), None, ALU.mult).then_inc(conv_mid, 1)
                        for k in (1, 2):
                            dve.wait_ge(conv_mid, 3 * m + k)
                            nc.vector.scalar_tensor_tensor(conv_a, conv_in[:, k:S + k], tap(k), conv_a, ALU.mult,
                                                           ALU.add).then_inc(conv_mid, 1)
                        dve.wait_ge(conv_mid, 3 * m + 3)
                        nc.vector.tensor_tensor(conv_y, conv_a, gb_s, ALU.mult).then_inc(conv_done, 1)
                        split(b + 5, i, 12)
                        dve.wait_ge(yb_hi_done, m + 1)
                        nc.vector.tensor_tensor(yb_lo[:, bass.ds(m, 1), :], conv_y.unsqueeze(1),
                                                yb_hi[:, bass.ds(m, 1), :].bitcast(F32), ALU.subtract).then_inc(yb_split, 1)
                split(n0 + 35)
                dve.wait_ge(v_sq, 2)
                nc.vector.tensor_scalar(v_ss[:, 1, :], v_ss[:, 0, :], 1.0 / D, EPS, ALU.mult, ALU.add).then_inc(v_ms_done, 1)
                dve.wait_ge(v_root_done, 1)
                step(inv_root(v_ss[:, 1, :], v_ss[:, 2, :], v_ss[:, 3, :], v_ss[:, 4, :]))
                for t in range(TT):
                    nc.vector.tensor_scalar(v_tok[:, t, :], v_tok[:, t, :], v_ss[:, 4, t:t + 1], None,
                                            ALU.mult).then_inc(v_normed, 1)
                for b in range(36, 40):
                    split(n0 + b)

                def u_scale(m):
                    dve.wait_ge(w_used, n0 + 32 + m + 1)
                    nc.vector.tensor_tensor(u_s[:, m, :], bank[4 + m % 4][:, 0:S], rstd[:], ALU.mult).then_inc(u_scaled, 1)

                def ya_part(m):
                    dve.wait_ge(ya_hi_done, m + 1)
                    nc.vector.tensor_tensor(ya_lo[:, m, :], u_s[:, m, :], ya_hi[:, m, :].bitcast(F32),
                                            ALU.subtract).then_inc(ya_split, 1)

                for m in range(4):
                    u_scale(m)
                dve.wait_ge(spatial_done, 1)
                dve.wait_ge(rows_loaded, 16)
                for m in range(KC):
                    nc.vector.scalar_tensor_tensor(
                        sg[:, m, :].rearrange("p (c q) -> p c q", c=TT),
                        acc(m).rearrange("p (c q) -> p c q", c=TT), cols[:, COLS["sgu"] + m:COLS["sgu"] + m + 1],
                        rows[:, 2 * HD + m * P:2 * HD + (m + 1) * P].unsqueeze(1).to_broadcast([P, TT, P]),
                        ALU.mult, ALU.add).then_inc(sg_done, 1)
                u_scale(4)
                split(n0 + 40)
                ya_part(0)
                ya_part(1)
                u_scale(5)
                split(n0 + 41)
                ya_part(2)
                ya_part(3)
                u_scale(6)
                ya_part(4)
                split(n0 + 42)
                ya_part(5)
                u_scale(7)
                ya_part(6)
                split(n0 + 43)
                ya_part(7)
                with dve.Fori(0, 4) as i:
                    for j in range(2):
                        b = n0 + 40 + 4 * j
                        m = 2 * i + j
                        split(b + 4, i, 8)
                        split(b + 5, i, 8)
                        dve.wait_ge(w_used, 8 * i + (b + 2))
                        nc.vector.tensor_tensor(gates.rearrange("p (g s) -> p g s", g=2),
                                                bank[4 + 2 * j][:].rearrange("p (g s) -> p g s", g=2),
                                                rstd[:].unsqueeze(1).to_broadcast([P, 2, S]), ALU.mult).then_inc(gates_scaled, 1)
                        split(b + 6, i, 8)
                        dve.wait_ge(w_used, 8 * i + (b + 4))
                        dve.wait_ge(sig_done, m + 1)
                        nc.vector.tensor_tensor(branch, bank[5 + 2 * j][:], sig, ALU.mult).then_inc(branch_done, 1)
                        dve.wait_ge(branch_done, m + 1)
                        nc.vector.tensor_tensor(merged, branch[:, 0:S], branch[:, S:2 * S], ALU.add).then_inc(merged_done, 1)
                        dve.wait_ge(mix_hi_done, m + (4 + HEADS + 1))
                        nc.vector.tensor_tensor(mix_lo[:, bass.ds(m, 1), :], merged.unsqueeze(1),
                                                mix_hi[:, bass.ds(m, 1), :].bitcast(F32), ALU.subtract).then_inc(mix_split, 1)
                        split(b + 7, i, 8)
                for b in range(76, 82):
                    split(n0 + b)
                residual(p, 1.0)

            for n in range(2):
                dve.wait_ge(half_hi_done, n + 1)
                nc.vector.tensor_tensor(w_lo[:, n, 0:HALF], w_raw[:, n, 0:HALF], w_hi[:, n, 0:HALF].bitcast(F32),
                                        ALU.subtract).then_inc(half_split, 1)
            for k in range(4):
                input_lo(0, k)
            for n in range(2):
                dve.wait_ge(w_hi_done, n + 1)
                nc.vector.tensor_tensor(w_lo[:, n, HALF:BW], w_raw[:, n, HALF:BW], w_hi[:, n, HALF:BW].bitcast(F32),
                                        ALU.subtract).then_inc(w_split, 1)
            for k in range(4, KC):
                input_lo(0, k)
            ffn(0, START[0], 0)
            attention_mixer(START[1], 1)
            ffn(1, START[2], 2)
            ffn(2, START[3], 3)
            gated_mixer(START[4], 4)
            ffn(3, START[5], 5)
            dve.wait_ge(sumsq_done, 7)
            nc.vector.tensor_scalar(end_ms, bank[4][:, 0:TT], 1.0 / D, EPS, ALU.mult, ALU.add).then_inc(ms_done, 1)
            dve.wait_ge(root_done, 7)
            step(inv_root(end_ms, end_root, end_nt, end_r))
            for t in range(TT):
                nc.vector.tensor_scalar(newton[:, t * P:(t + 1) * P], ident, end_r[:, t:t + 1], None,
                                        ALU.mult).then_inc(diagonal_done, 1)
            dve.wait_ge(spread_done, 1)
            for c in range(4):
                dve.wait_ge(x_gained, 2 * c + 2)
                nc.vector.tensor_tensor(x_sq[:, 2 * c:2 * c + 2, :], x[:, 2 * c:2 * c + 2, :],
                                        bank[5][:, 0:S].unsqueeze(1).to_broadcast([P, 2, S]),
                                        ALU.mult).then_inc(out_ready, 1)

        @block.tensor
        def _(pe):
            def three(dst, a_hi, a_lo, b_hi, b_lo, first, last):
                nc.tensor.matmul(dst, a_hi, b_hi, start=first, stop=False, skip_group_check=True)
                nc.tensor.matmul(dst, a_hi, b_lo, start=False, stop=False, skip_group_check=True)
                return nc.tensor.matmul(dst, a_lo, b_hi, start=False, stop=last, skip_group_check=True)

            def feature_block(n, dst, b_hi, b_lo, i=0, per=0, p=None, ready=None):
                slot = n % RING
                pe.wait_ge(w_split, n + 1 + per * i)
                for k in range(KC):
                    if p is not None:
                        pe.wait_ge(x_split, 8 * p + k + 1)
                    if ready is not None:
                        pe.wait_ge(ready, k + 1)
                    w = slice(k * P, (k + 1) * P)
                    last = three(dst, w_hi[:, slot, w], w_lo[:, slot, w], b_hi[:, k, :], b_lo[:, k, :], k == 0, k == KC - 1)
                last.then_inc(w_used, 1)

            def token_block(n, b, per_block, width, dst, p=None):
                slot = n % RING
                pe.wait_ge(w_split, n + 1)
                for kk in range(min(per_block, KC - b * per_block)):
                    k = b * per_block + kk
                    if p is not None:
                        pe.wait_ge(x_split, 8 * p + k + 1)
                    for t in range(TT):
                        tok, w = slice(t * P, (t + 1) * P), slice(kk * width, (kk + 1) * width)
                        last = three(dst[t][:, 0:width], x_hi[:, k, tok], x_lo[:, k, tok], w_hi[:, slot, w],
                                     w_lo[:, slot, w], k == 0, k == KC - 1)
                last.then_inc(w_used, 1)

            def chunk_block(n, b_hi, b_lo, i=0, per=0, first=False, part=range(KC)):
                slot = n % RING
                pe.wait_ge(w_split, n + 1 + per * i)
                for m in part:
                    w = slice(m * P, (m + 1) * P)
                    last = three(acc(m), w_hi[:, slot, w], w_lo[:, slot, w], b_hi, b_lo, first and m % 2 == 0, False)
                    if m == KC - 1:
                        last.then_inc(w_used, 1)

            def last_chunk(n, b_hi, b_lo):
                slot = n % RING
                pe.wait_ge(w_split, n + 1)
                for m in range(KC):
                    w = slice(m * P, (m + 1) * P)
                    last = three(acc(m), w_hi[:, slot, w], w_lo[:, slot, w], b_hi, b_lo, False, True)
                    if m % 2 and m < KC - 1:
                        last.then_inc(acc_done, 1)
                last.then_inc(w_used, 1)

            def sum_squares(p):
                pe.wait_ge(x_sq_added, 4 * p + 4)
                nc.tensor.matmul(bank[STAT[p]][:, 0:S], ones[:], x_sq[:, 0, :], start=True, stop=True,
                                 skip_group_check=True).then_inc(sumsq_done, 1)

            def token_scales(p):
                pe.wait_ge(rstd_done, p + 1)
                for t in range(TT):
                    last = nc.tensor.transpose(bank[2][:, t * P:(t + 1) * P], rstd[:, t * P:(t + 1) * P], ident)
                last.then_inc(rT_done, 1)

            def ffn(e, n0, p):
                if p == 0:
                    pe.wait_ge(half_split, 2)
                for k in range(KC):
                    if k == (KC // 2 if p == 0 else 0):
                        pe.wait_ge(w_split, n0 + 2)
                    pe.wait_ge(x_split, 8 * p + k + 1)
                    w = slice(k * P, (k + 1) * P)
                    for c in range(2):
                        slot = (n0 + c) % RING
                        last = three(bank[4][:, c * S:(c + 1) * S], w_hi[:, slot, w], w_lo[:, slot, w], x_hi[:, k, :],
                                     x_lo[:, k, :], k == 0 and c == 0, k == KC - 1)
                        if k == KC - 1:
                            last.then_inc(w_used, 1)
                feature_block(n0 + 2, bank[5][:, 0:S], x_hi, x_lo)
                feature_block(n0 + 3, bank[5][:, S:2 * S], x_hi, x_lo)
                sum_squares(p)
                for b in range(4, 8):
                    feature_block(n0 + b, bank[4 + b // 2][:, b % 2 * S:(b % 2 + 1) * S], x_hi, x_lo)
                for f in range(2):
                    pe.wait_ge(hid_split, FC * e + f + 1)
                    chunk_block(n0 + 8 + f, hid_hi[:, f, :], hid_lo[:, f, :], first=(f == 0))

                def chunk(f, j, i=0):
                    b = n0 + 10 + 3 * (f - 4)
                    g = bank[4 + j]
                    feature_block(b, g[:, 0:S], x_hi, x_lo, i, 12)
                    feature_block(b + 1, g[:, S:2 * S], x_hi, x_lo, i, 12)
                    pe.wait_ge(hid_split, 4 * i + (FC * e + f - 1))
                    chunk_block(b + 2, hid_hi[:, (j - 2) % 4, :], hid_lo[:, (j - 2) % 4, :], i, 12)

                with pe.Fori(0, LOOPED // 4) as i:
                    for j in range(4):
                        chunk(4 + j, j, i)
                for f in range(4 + LOOPED, FC):
                    chunk(f, f % 4)
                pe.wait_ge(hid_split, FC * (e + 1) - 1)
                f = (FC - 2) % 4
                chunk_block(n0 + 64, hid_hi[:, f, :], hid_lo[:, f, :])
                pe.wait_ge(hid_split, FC * (e + 1))
                last_chunk(n0 + 65, hid_hi[:, f + 1, :], hid_lo[:, f + 1, :])

            def attention_mixer(n0, p):
                for b in range(4):
                    token_block(n0 + b, b, TOK_K, 512, (bank[4], bank[5]), p)
                sum_squares(p)
                for b in range(4):
                    if b == 2:
                        token_scales(p)
                    token_block(n0 + 4 + b, b, TOK_K, 512, (bank[6], bank[7]))
                for b in range(IDX_B):
                    token_block(n0 + 8 + b, b, IDX_K, IDX_W, (bank[0], bank[1]))
                pe.wait_ge(r_col_done, 1)
                for b in range(2):
                    token_block(n0 + 11 + b, b, TOK_K, 512, (bank[2], bank[3]))
                pe.wait_ge(idx_roped, 2)
                pe.wait_ge(q_copied, 4)
                for c in range(3):
                    for t in range(TT):
                        dst = bank[6 + c // 2][:, (c % 2) * S + t * P:(c % 2) * S + (t + 1) * P]
                        last = nc.tensor.transpose(dst, idx_tok[:, t, c * P:(c + 1) * P], ident)
                last.then_inc(idx_T, 1)
                for b in range(2, 4):
                    token_block(n0 + 11 + b, b, TOK_K, 512, (bank[2], bank[3]))
                pe.wait_ge(idx_T_copied, 2)
                for t in range(TT):
                    for hd in range(IH):
                        rows_ = slice(hd % 2 * ID, hd % 2 * ID + ID)
                        n = (t + 1) * P
                        dst = bank[6 * t + hd % 2][:, hd // 2 * n:(hd // 2 + 1) * n]
                        last = nc.tensor.matmul(dst, qiT[rows_, hd // 2, t * P:(t + 1) * P], kiT[rows_, 0:n], start=True,
                                                stop=True, skip_group_check=True)
                last.then_inc(idx_dots, 1)
                token_block(n0 + 15, 0, TOK_K, 512, (bank[4], bank[5]))
                band = const[:, C_BAND:].rearrange("p (t g s) -> p t g s", t=TT, g=4)
                pe.wait_ge(u_copied, 2)
                for g in range(4):
                    for t in range(TT):
                        last = nc.tensor.matmul(bank[2 + g // 2][:, (g % 2) * S + t * P:(g % 2 + 1) * S],
                                                u_tok[:, t, g * P:(g + 1) * P], band[:, t, g, t * P:S], start=(t == 0),
                                                stop=(t == TT - 1), skip_group_check=True)
                    if g % 2:
                        last.then_inc(pool_mean, 1)
                token_block(n0 + 16, 1, TOK_K, 512, (bank[4], bank[5]))
                pe.wait_ge(pool_loaded, 16)
                for g in range(4):
                    pe.wait_ge(pool_mean_copied, 2 * (g // 2) + 2)
                    last = nc.tensor.matmul(bank[2 + g // 2][:, (g % 2) * S:(g % 2 + 1) * S], pool_w[:, g, :],
                                            pool_in[:, g, :], start=True, stop=True, skip_group_check=True)
                    if g % 2:
                        last.then_inc(pool_out, 1)
                for b in range(2, 4):
                    token_block(n0 + 15 + b, b, TOK_K, 512, (bank[4], bank[5]))
                pe.wait_ge(mix_split, 4)
                pe.wait_ge(rel_done, 4)

                def pooled(g, part=range(KC)):
                    chunk_block(n0 + 19 + g, mix_hi[:, PAIRS + g, :], mix_lo[:, PAIRS + g, :], first=(g == 0), part=part)

                pooled(0)
                for a in range(2):
                    pe.wait_ge(qk_roped, 2 * a + 2)
                    if a:
                        pe.wait_ge(v_copied, 2)
                    for c in range(PAIRS):
                        for t in range(TT):
                            dst = bank[(6, 7, 4, 5)[2 * a + c // 2]][:, (c % 2) * S + t * P:(c % 2) * S + (t + 1) * P]
                            last = nc.tensor.transpose(dst, qk_b[:, 2 * a + t, c * P:(c + 1) * P], ident)
                        if c % 2:
                            last.then_inc(qk_T, 1)
                pooled(1)
                pe.wait_ge(qk_T_copied, 4)
                for s in range(HEADS + 3):
                    if s < HEADS:
                        rows_ = slice(s % 2 * HD, s % 2 * HD + HD)
                        if s >= 2:
                            pe.wait_ge(logits_read, 2 * (s - 1))
                        for t in range(TT):
                            n = (t + 1) * P
                            last = nc.tensor.matmul(bank[4 + s % 2][:, t * P:t * P + n],
                                                    qT[rows_, s // 2, t * P:(t + 1) * P], kT[rows_, s // 2, 0:n],
                                                    start=True, stop=True, skip_group_check=True)
                        last.then_inc(logits_done, 1)
                    if s >= 3:
                        hd = s - 3
                        pe.wait_ge(probT_copied, hd + 1)
                        if hd:
                            pe.wait_ge(mix_split, 4 + hd)
                        pair = slice(hd // 2 * P, (hd // 2 + 1) * P)
                        nc.tensor.matmul(bank[7][:, 0:S], v_tok[:, 0, pair], probT[:, hd % 2, 0:S], start=True, stop=False,
                                         skip_group_check=True)
                        nc.tensor.matmul(bank[7][:, P:S], v_tok[:, 1, pair], probT[:, hd % 2, S:S + P], start=False,
                                         stop=True, skip_group_check=True).then_inc(pv_done, 1)
                    if 2 <= s <= HEADS + 1:
                        hd = s - 2
                        pe.wait_ge(prob_done, 2 * hd + 2)
                        if hd:
                            pe.wait_ge(probT_copied, hd)
                        for n, (t, kt) in enumerate(((0, 0), (1, 0), (1, 1))):
                            last = nc.tensor.transpose(bank[6][:, n * P:(n + 1) * P],
                                                       prob[:, hd % 2, t, kt * P:(kt + 1) * P], ident)
                        last.then_inc(probT_done, 1)
                    half = KC // 2
                    if s == 0:
                        pooled(2)
                    elif s in (1, 3):
                        pooled(3, range(half) if s == 1 else range(half, KC))
                    elif s >= 5:
                        c = (s - 5) // 2
                        pe.wait_ge(mix_split, 4 + 2 * c + 2)
                        chunk_block(n0 + 23 + c, mix_hi[:, c, :], mix_lo[:, c, :],
                                    part=range(half) if s % 2 else range(half, KC))
                pe.wait_ge(mix_split, 4 + HEADS)
                last_chunk(n0 + 26, mix_hi[:, 3, :], mix_lo[:, 3, :])

            def gated_mixer(n0, p):
                for b in range(4):
                    token_block(n0 + b, b, TOK_K, 512, (bank[4], bank[5]), p)
                sum_squares(p)
                for b in range(4):
                    if b == 2:
                        token_scales(p)
                    token_block(n0 + 4 + b, b, TOK_K, 512, (bank[6], bank[7]))
                pe.wait_ge(v_gelu, 2)
                with pe.Fori(0, 2) as i:
                    for j in range(4):
                        b = n0 + 8 + 3 * j
                        pair, single = bank[4 + 2 * (j % 2)], bank[5 + 2 * (j % 2)]
                        if j == 1:
                            pe.wait_ge(v_gelu, 4)
                        feature_block(b, pair[:, 0:S], x_hi, x_lo, i, 12)
                        feature_block(b + 1, pair[:, S:2 * S], x_hi, x_lo, i, 12)
                        feature_block(b + 2, single[:, 0:S], x_hi, x_lo, i, 12)
                for m in range(4):
                    if m == 2:
                        pe.wait_ge(conv_read, KC)
                    feature_block(n0 + 32 + m, bank[4 + m][:, 0:S], x_hi, x_lo)
                pe.wait_ge(v_normed, 2)
                pe.wait_ge(sgu_loaded, 16)
                for m in range(KC):
                    for t in range(TT):
                        last = nc.tensor.matmul(acc(m)[:, t * P:(t + 1) * P], v_tok[:, t, m * P:(m + 1) * P], sgu_w[:, m, :],
                                                start=True, stop=True, skip_group_check=True)
                last.then_inc(spatial_done, 1)
                for m in range(4, KC):
                    pe.wait_ge(u_scaled, m - 3)
                    feature_block(n0 + 32 + m, bank[m][:, 0:S], x_hi, x_lo)
                pe.wait_ge(u_scaled, 6)
                with pe.Fori(0, 4) as i:
                    for j in range(2):
                        b = n0 + 40 + 4 * j
                        g, y = bank[4 + 2 * j], bank[5 + 2 * j]
                        if j == 1:
                            pe.wait_ge(u_scaled, KC)
                        feature_block(b, g[:, 0:S], x_hi, x_lo, i, 8)
                        feature_block(b + 1, g[:, S:2 * S], x_hi, x_lo, i, 8)
                        pe.wait_ge(ya_split, KC)
                        feature_block(b + 2, y[:, 0:S], ya_hi, ya_lo, i, 8)
                        pe.wait_ge(yb_split, KC)
                        feature_block(b + 3, y[:, S:2 * S], yb_hi, yb_lo, i, 8)
                base = 4 + HEADS
                pe.wait_ge(sg_done, KC)
                for c in range(KC - 1):
                    pe.wait_ge(mix_split, base + c + 1)
                    chunk_block(n0 + 72 + c, mix_hi[:, c, :], mix_lo[:, c, :], first=(c == 0))
                pe.wait_ge(mix_split, base + KC)
                last_chunk(n0 + 79, mix_hi[:, KC - 1, :], mix_lo[:, KC - 1, :])

            pe.wait_ge(filled, 1)
            for _ in range(WARM):
                nc.tensor.matmul(bank[7][:], zeros[:, 0:P], zeros[:], start=True, stop=True, skip_group_check=True)
            pe.wait_ge(filled, 3)
            ffn(0, START[0], 0)
            attention_mixer(START[1], 1)
            ffn(1, START[2], 2)
            ffn(2, START[3], 3)
            gated_mixer(START[4], 4)
            ffn(3, START[5], 5)
            for k in range(KC):
                pe.wait_ge(x_sq_done, 24 + k // 2 + 1)
                for t in range(TT):
                    last = nc.tensor.matmul(bank[4][:, t:t + 1], x_sq[:, k, t * P:(t + 1) * P], ones[:, 0:1],
                                            start=(k == 0 and t == 0), stop=(k == KC - 1), skip_group_check=True)
            last.then_inc(sumsq_done, 1)
            for t in range(TT):
                pe.wait_ge(diagonal_done, t + 1)
                last = nc.tensor.matmul(bank[5][:, t * P:(t + 1) * P], ones[:], newton[:, t * P:(t + 1) * P],
                                        start=True, stop=True, skip_group_check=True)
            last.then_inc(spread_done, 1)



MIX1_SPLITS = (1, 2, 4, 7, 9)
STAT = [0, 3, 0, 0, 3, 0, 4]
WARM = 16


def _cols(a):
    return np.asarray(a, np.float32).reshape(-1, P).T


def _features(w):
    return w.reshape(KC, P, -1, P).transpose(2, 1, 0, 3).reshape(-1, P, BW)


def _tokens(w, per_block):
    width = w.shape[1]
    n = -(-KC // per_block)
    out = np.zeros((n, P, BW), np.float32)
    for k in range(KC):
        b, j = divmod(k, per_block)
        out[b, :, j * width:(j + 1) * width] = w[k * P:(k + 1) * P]
    return out


def _chunks(w):
    return w.reshape(-1, P, BW)


def _ffn(gate, up, down):
    g, u, d = _features(gate), _features(up), _chunks(down)
    out = [w[f] for f in range(4) for w in (g, u)] + [d[0], d[1]]
    for f in range(4, FC):
        out += [g[f], u[f], d[f - 2]]
    return np.stack(out + [d[FC - 2], d[FC - 1]])


def _constants():
    c = np.zeros((P, NCONST), np.float32)
    pos = np.arange(S, dtype=np.float32)

    def tables(half):
        inv = np.float32(THETA) ** (-np.arange(half, dtype=np.float32) / np.float32(half))
        ang = pos[:, None] * inv[None, :]
        return np.cos(ang), np.sin(ang)

    cos, sin = tables(HD // 2)
    c[:, C_COS:C_COS + P] = np.concatenate([cos, cos], 1).reshape(TT, P, HD).transpose(1, 0, 2).reshape(P, -1)
    c[:, C_SIN:C_SIN + P] = np.concatenate([-sin, sin], 1).reshape(TT, P, HD).transpose(1, 0, 2).reshape(P, -1)
    cos, sin = tables(IROT // 2)
    c[:, C_ICOS:C_ICOS + 32] = cos.reshape(TT, P, -1).transpose(1, 0, 2).reshape(P, -1)
    c[:, C_ISIN:C_ISIN + 32] = sin.reshape(TT, P, -1).transpose(1, 0, 2).reshape(P, -1)
    c[:, C_ID:C_ID + P] = np.eye(P)
    band = np.zeros((S, 4, S), np.float32)
    for g, w in enumerate(POOLS):
        for t in range(S):
            lo = max(0, t - w + 1)
            band[lo:t + 1, g, t] = np.float32(1.0) / np.float32(t + 1 - lo)
            band[t, g, t] -= 1.0
    c[:, C_BAND:] = band.reshape(TT, P, 4 * S).transpose(1, 0, 2).reshape(P, -1)
    return c


def kernel(**inputs):
    import concourse.bacc as bacc
    from concourse.bass_utils import run_bass_kernel_spmd

    a = {k: np.asarray(v) for k, v in inputs.items()}
    w1 = {k: v[0] for k, v in a.items() if k not in ("x", "final_norm_2")}
    wi, wz = w1["w_in"], w1["w_in_2"]
    n_idx = 3 * ATT + IDX_W
    wo = _chunks(w1["w_out"])
    z = _features(wz)
    pa, pb = _features(w1["w_proj_a_2"]), _features(w1["w_proj_b_2"])
    up1, up2 = w1["ffn1_w_in_2"], w1["ffn2_w_in_2"]
    stream = np.concatenate([
        _ffn(w1["ffn1_w_gate"], w1["ffn1_w_up"], w1["ffn1_w_down"]),
        _tokens(wi[:, 0:ATT], TOK_K), _tokens(wi[:, ATT:2 * ATT], TOK_K), _tokens(wi[:, 3 * ATT:n_idx], IDX_K),
        _tokens(wi[:, n_idx:], TOK_K), _tokens(wi[:, 2 * ATT:3 * ATT], TOK_K), wo[4:], wo[:4],
        _ffn(w1["ffn2_w_gate"], w1["ffn2_w_up"], w1["ffn2_w_down"]),
        _ffn(up1[:, :FF], up1[:, FF:], w1["ffn1_w_out_2"]),
        _tokens(wz[:, D:D + 512], TOK_K), _tokens(wz[:, D + 512:2 * D], TOK_K),
        np.stack([z[c + m] for m in range(KC) for c in (24, 32, 16)]), z[0:8],
        np.stack([b[m] for m in range(KC) for b in (z[40:48], z[48:56], pa, pb)]),
        _chunks(w1["w_out_2"]),
        _ffn(up2[:, :FF], up2[:, FF:], w1["ffn2_w_out_2"]),
    ])
    assert stream.shape == (BLOCKS, P, BW)
    arrays = {
        "stream": stream,
        "x_in": a["x"][0].T.reshape(KC, P, S).transpose(1, 0, 2),
        "cols_in": np.concatenate([_cols(v) for v in (
            w1["ffn1_norm"], w1["mix_norm"], w1["ffn2_norm"], w1["ffn1_norm_2"], w1["mix_norm_2"], w1["ffn2_norm_2"],
            a["final_norm_2"], w1["sgu_norm_2"], w1["conv_w_2"].reshape(-1), w1["pool_scale"])], 1),
        "rows_in": np.broadcast_to(np.concatenate([w1["q_norm"], w1["k_norm"], w1["sgu_b_2"].reshape(-1)]),
                                   (P, 2 * HD + SGU_HEADS * P)),
        "const_in": _constants(),
        "sgu_w_in": w1["sgu_w_2"].transpose(2, 0, 1),
        "pool_w_in": w1["pool_w"].transpose(1, 0, 2),
    }
    arrays = {k: np.ascontiguousarray(v) for k, v in arrays.items()}
    nc = bacc.Bacc("TRN2", target_bir_lowering=False, num_devices=1)
    args = [nc.dram_tensor(k, v.shape, F32, kind="ExternalInput").ap() for k, v in arrays.items()]
    args.append(nc.dram_tensor("out", (P, KC, S), F32, kind="ExternalOutput").ap())
    build(nc, *args)
    r = run_bass_kernel_spmd(nc, [arrays], core_ids=[0])
    y = r.results[0]["out"]
    return y.transpose(1, 0, 2).reshape(D, S).T.reshape(1, S, D)
```
